# Optimizing a Trainium2 kernel written in Bass

```python
import math
import jax, jax.numpy as jnp
from jax import lax
import numpy as np

D_MODEL = 1024
BATCH = 1
SEQ = 256
DEPTH = 2

HEAD_DIM = 64
NSA_HEADS = 6
NSA_KV_GROUPS = 2
NSA_REP = NSA_HEADS // NSA_KV_GROUPS
N_BRANCH = 3
CMP_LEN = 32
CMP_STRIDE = 16
CMP_HIDDEN = 2 * HEAD_DIM
SEL_BLOCK = 64
SEL_TOP_N = 16
WINDOW = 512
NSA_Q_BLOCK = 32
MLA_HEADS = 5
MLA_Q_RANK = 256
MLA_KV_RANK = 128
MLA_NOPE_DIM = 64
MLA_ROPE_DIM = 32
MLA_V_DIM = 64
ATTN_Q_BLOCK = 128
RET_HEADS = 5
RET_CHUNK = 128
ROPE_THETA = 500000.0
PARTIAL_ROPE_DIM = HEAD_DIM // 4
RET_THETA = 10000.0
D_FF = 4 * D_MODEL
NORM_EPS = 1e-6
NEG_INF = -1e30
FORCE_SCORE = 1e9

NSA_Q_W = NSA_HEADS * HEAD_DIM
NSA_KV_W = NSA_KV_GROUPS * HEAD_DIM
NSA_GATE_W = NSA_HEADS * N_BRANCH
MLA_OUT_W = MLA_HEADS * MLA_V_DIM
RET_W = RET_HEADS * HEAD_DIM
MIX_WIDTH = NSA_Q_W + MLA_OUT_W + RET_W
IN_SIZES = (NSA_Q_W, NSA_KV_W, NSA_KV_W, NSA_KV_W, NSA_KV_W, NSA_KV_W, NSA_KV_W, NSA_GATE_W,
            MLA_Q_RANK, MLA_KV_RANK, MLA_ROPE_DIM, RET_W, RET_W, RET_W, RET_W)
N_IN = sum(IN_SIZES)


F32 = jnp.float32

def in_offsets():
    return [int(o) for o in np.cumsum(IN_SIZES)[:-1]]

def rms_norm(x, gain):
    xf = x.astype(F32)
    y = xf * lax.rsqrt(jnp.mean(xf * xf, axis=-1, keepdims=True) + NORM_EPS) * gain.astype(F32)
    return y.astype(x.dtype)

def masked_softmax(s, mask):
    s = jnp.where(mask, s.astype(F32), NEG_INF)
    m = jnp.max(s, axis=-1, keepdims=True)
    p = jnp.exp(s - m) * mask
    return p / jnp.maximum(jnp.sum(p, axis=-1, keepdims=True), 1e-30)

def rope_tables(positions, dim, theta):
    inv = 1.0 / (theta ** (jnp.arange(0, dim, 2, dtype=F32) / dim))
    ang = positions.astype(F32)[..., None] * inv
    return jnp.cos(ang), jnp.sin(ang)

def apply_rope(x, cos, sin):
    half = x.shape[-1] // 2
    x1 = x[..., :half].astype(F32)
    x2 = x[..., half:].astype(F32)
    c = cos[:, :, None, :]
    s = sin[:, :, None, :]
    return jnp.concatenate([x1 * c - x2 * s, x2 * c + x1 * s], axis=-1).astype(x.dtype)

def partial_rope(x, cos, sin):
    return jnp.concatenate([apply_rope(x[..., :PARTIAL_ROPE_DIM], cos, sin), x[..., PARTIAL_ROPE_DIM:]], axis=-1)

def selection_overlap(n_cmp, n_sel):
    cs = np.arange(n_cmp) * CMP_STRIDE
    ce = cs + CMP_LEN
    ss = np.arange(n_sel) * SEL_BLOCK
    se = ss + SEL_BLOCK
    ov = np.clip(np.minimum(ce[:, None], se[None, :]) - np.maximum(cs[:, None], ss[None, :]), 0, None) / CMP_LEN
    return jnp.asarray(ov.astype(np.float32))

def compress_blocks(tok, tok_idx, pos_emb, w1, w2):
    b, _, g, dh = tok.shape
    blk = tok[:, tok_idx] + pos_emb[None, None, :, None, :]
    flat = blk.transpose(0, 1, 3, 2, 4).reshape(b, tok_idx.shape[0], g, CMP_LEN * dh)
    return jax.nn.gelu(flat @ w1) @ w2

def nsa_mixer(q, k_cmp, v_cmp, k_slc, v_slc, k_win, v_win, gates, pos_k, w1_k, w2_k, pos_v, w1_v, w2_v):
    b, s, _, dh = q.shape
    g, r = NSA_KV_GROUPS, NSA_REP
    n_cmp = (s - CMP_LEN) // CMP_STRIDE + 1
    n_sel = s // SEL_BLOCK
    top_n = min(SEL_TOP_N, n_sel)
    scale = dh ** -0.5
    qb_len = NSA_Q_BLOCK

    tok_idx = np.arange(n_cmp)[:, None] * CMP_STRIDE + np.arange(CMP_LEN)[None, :]
    kc = compress_blocks(k_cmp, tok_idx, pos_k, w1_k, w2_k)
    vc = compress_blocks(v_cmp, tok_idx, pos_v, w1_v, w2_v)
    cmp_end = jnp.arange(n_cmp) * CMP_STRIDE + CMP_LEN - 1
    overlap = selection_overlap(n_cmp, n_sel)

    ks_blk = k_slc.reshape(b, n_sel, SEL_BLOCK, g, dh).transpose(0, 3, 1, 2, 4)
    vs_blk = v_slc.reshape(b, n_sel, SEL_BLOCK, g, dh).transpose(0, 3, 1, 2, 4)
    kw_pad = jnp.pad(k_win, ((0, 0), (WINDOW, 0), (0, 0), (0, 0)))
    vw_pad = jnp.pad(v_win, ((0, 0), (WINDOW, 0), (0, 0), (0, 0)))

    n_qb = s // qb_len
    q_blocks = q.reshape(b, n_qb, qb_len, g, r, dh).transpose(1, 0, 2, 3, 4, 5)
    gate_blocks = jax.nn.sigmoid(gates.astype(F32)).reshape(b, n_qb, qb_len, g, r, N_BRANCH).transpose(1, 0, 2, 3, 4, 5)
    b_idx = jnp.arange(b)[:, None, None, None]
    g_idx = jnp.arange(g)[None, :, None, None]
    sel_ids = jnp.arange(n_sel)[None, :]

    def block(args):
        qb, gb, i = args
        q0 = i * qb_len
        t = q0 + jnp.arange(qb_len)
        s_c = jnp.einsum('bqgrd,bngd->bgrqn', qb, kc) * scale
        p_c = masked_softmax(s_c, cmp_end[None, :] <= t[:, None])
        o_c = jnp.einsum('bgrqn,bngd->bqgrd', p_c, vc)
        imp = jnp.einsum('bgrqn,nm->bgqm', p_c, overlap)
        cur = (t // SEL_BLOCK)[:, None]
        valid = sel_ids <= cur
        forced = (sel_ids == 0) | (sel_ids == cur) | (sel_ids == cur - 1)
        imp = jnp.where(valid & forced, FORCE_SCORE, imp)
        imp = jnp.where(valid, imp, NEG_INF)
        _, idx = lax.top_k(imp, top_n)
        k_sel = ks_blk[b_idx, g_idx, idx]
        v_sel = vs_blk[b_idx, g_idx, idx]
        key_pos = idx[..., None] * SEL_BLOCK + jnp.arange(SEL_BLOCK)
        mask_s = (key_pos <= t[None, None, :, None, None]).reshape(b, g, 1, qb_len, top_n * SEL_BLOCK)
        s_s = jnp.einsum('bqgrd,bgqjsd->bgrqjs', qb, k_sel).reshape(b, g, r, qb_len, top_n * SEL_BLOCK) * scale
        p_s = masked_softmax(s_s, mask_s).reshape(b, g, r, qb_len, top_n, SEL_BLOCK)
        o_s = jnp.einsum('bgrqjs,bgqjsd->bqgrd', p_s, v_sel)
        kw = lax.dynamic_slice_in_dim(kw_pad, q0, qb_len + WINDOW, axis=1)
        vw = lax.dynamic_slice_in_dim(vw_pad, q0, qb_len + WINDOW, axis=1)
        kp = (q0 - WINDOW + jnp.arange(qb_len + WINDOW))[None, :]
        mask_w = (kp <= t[:, None]) & (kp > t[:, None] - WINDOW) & (kp >= 0)
        s_w = jnp.einsum('bqgrd,bkgd->bgrqk', qb, kw) * scale
        p_w = masked_softmax(s_w, mask_w)
        o_w = jnp.einsum('bgrqk,bkgd->bqgrd', p_w, vw)
        return gb[..., 0:1] * o_c + gb[..., 1:2] * o_s + gb[..., 2:3] * o_w

    out = lax.map(block, (q_blocks, gate_blocks, jnp.arange(n_qb)))
    return out.transpose(1, 0, 2, 3, 4, 5).reshape(b, s, NSA_HEADS * dh)

def causal_block_attention(q, k, v, scale):
    b, s, h, dq = q.shape
    n_qb = s // ATTN_Q_BLOCK
    q_blocks = q.reshape(b, n_qb, ATTN_Q_BLOCK, h, dq).transpose(1, 0, 2, 3, 4)
    kp = jnp.arange(s)[None, :]

    def block(args):
        qi, i = args
        t = (i * ATTN_Q_BLOCK + jnp.arange(ATTN_Q_BLOCK))[:, None]
        sc = jnp.einsum('bqhd,bkhd->bhqk', qi, k) * scale
        p = masked_softmax(sc, kp <= t)
        return jnp.einsum('bhqk,bkhd->bqhd', p, v)

    out = lax.map(block, (q_blocks, jnp.arange(n_qb)))
    return out.transpose(1, 0, 2, 3, 4).reshape(b, s, h, v.shape[-1])

def mla_mixer(c_q, c_kv, k_pe, q_norm, w_uq, kv_norm, w_ukv, cos, sin):
    b, s, _ = c_q.shape
    q = (rms_norm(c_q, q_norm) @ w_uq).reshape(b, s, MLA_HEADS, MLA_NOPE_DIM + MLA_ROPE_DIM)
    q_nope, q_pe = q[..., :MLA_NOPE_DIM], apply_rope(q[..., MLA_NOPE_DIM:], cos, sin)
    kv = (rms_norm(c_kv, kv_norm) @ w_ukv).reshape(b, s, MLA_HEADS, MLA_NOPE_DIM + MLA_V_DIM)
    k_nope, v = kv[..., :MLA_NOPE_DIM], kv[..., MLA_NOPE_DIM:]
    k_pe = apply_rope(k_pe[:, :, None, :], cos, sin)
    q_full = jnp.concatenate([q_nope, q_pe], axis=-1)
    k_full = jnp.concatenate([k_nope, jnp.broadcast_to(k_pe, (b, s, MLA_HEADS, MLA_ROPE_DIM)).astype(k_nope.dtype)], axis=-1)
    o = causal_block_attention(q_full, k_full, v, (MLA_NOPE_DIM + MLA_ROPE_DIM) ** -0.5)
    return o.reshape(b, s, MLA_OUT_W)

def chunkwise_retention(q, k, v):
    b, s, h, d = q.shape
    n = s // RET_CHUNK
    log_g = jnp.log(1.0 - 2.0 ** (-5.0 - jnp.arange(h, dtype=F32)))
    i = jnp.arange(RET_CHUNK, dtype=F32)
    diff = i[:, None] - i[None, :]
    intra = jnp.where(diff >= 0, jnp.exp(jnp.maximum(diff, 0.0)[None] * log_g[:, None, None]), 0.0)
    read_decay = jnp.exp((i + 1.0)[None, :] * log_g[:, None])[None, :, :, None]
    write_decay = jnp.exp((RET_CHUNK - 1.0 - i)[None, :] * log_g[:, None])[None, :, :, None]
    chunk_decay = jnp.exp(RET_CHUNK * log_g)[None, :, None, None]

    def to_chunks(a):
        return a.reshape(b, n, RET_CHUNK, h, d).transpose(1, 0, 3, 2, 4)

    def step(state, xs):
        qc, kc, vc = xs
        sc = jnp.einsum('bhid,bhjd->bhij', qc, kc) * intra
        o = jnp.einsum('bhij,bhjd->bhid', sc, vc) + jnp.einsum('bhid,bhde->bhie', qc, state) * read_decay
        state = state * chunk_decay + jnp.einsum('bhjd,bhje->bhde', kc * write_decay, vc)
        return state, o

    state0 = jnp.zeros((b, h, d, d), F32)
    _, outs = lax.scan(step, state0, (to_chunks(q), to_chunks(k), to_chunks(v)))
    return outs.transpose(1, 0, 3, 2, 4).reshape(b, s, h, d)

def retention_mixer(q, k, v, gate, gn_gain, cos, sin):
    b, s, _ = q.shape
    h, d = RET_HEADS, HEAD_DIM
    q = apply_rope(q.reshape(b, s, h, d), cos, sin).astype(F32)
    k = apply_rope(k.reshape(b, s, h, d), cos, sin).astype(F32) * (d ** -0.5)
    v = v.reshape(b, s, h, d).astype(F32)
    o = chunkwise_retention(q, k, v)
    mu = jnp.mean(o, axis=-1, keepdims=True)
    var = jnp.mean(jnp.square(o - mu), axis=-1, keepdims=True)
    o = (o - mu) * lax.rsqrt(var + NORM_EPS) * gn_gain.astype(F32)
    return jax.nn.silu(gate.astype(F32)) * o.reshape(b, s, h * d)

def first_inputs(seed: int = 0) -> dict:
    key = jax.random.key(seed)
    ks = jax.random.split(key, 24)

    def nrm(k, shape, scale):
        return scale * jax.random.normal(k, shape, F32)

    def gain(k, shape):
        return 1.0 + 0.02 * jax.random.normal(k, shape, F32)

    offs = jax.random.randint(ks[1], (BATCH, 1), 0, 4096)
    positions = (jnp.arange(SEQ, dtype=jnp.int32)[None, :] + offs).astype(jnp.int32)
    return {
        'x': nrm(ks[0], (BATCH, SEQ, D_MODEL), 1.0),
        'positions': positions,
        'ln1_gain': gain(ks[2], (DEPTH, D_MODEL)),
        'w_in': nrm(ks[3], (DEPTH, D_MODEL, N_IN), D_MODEL ** -0.5),
        'cmp_pos_k': nrm(ks[4], (DEPTH, CMP_LEN, HEAD_DIM), 0.1),
        'cmp_w1_k': nrm(ks[5], (DEPTH, CMP_LEN * HEAD_DIM, CMP_HIDDEN), (CMP_LEN * HEAD_DIM) ** -0.5),
        'cmp_w2_k': nrm(ks[6], (DEPTH, CMP_HIDDEN, HEAD_DIM), CMP_HIDDEN ** -0.5),
        'cmp_pos_v': nrm(ks[7], (DEPTH, CMP_LEN, HEAD_DIM), 0.1),
        'cmp_w1_v': nrm(ks[8], (DEPTH, CMP_LEN * HEAD_DIM, CMP_HIDDEN), (CMP_LEN * HEAD_DIM) ** -0.5),
        'cmp_w2_v': nrm(ks[9], (DEPTH, CMP_HIDDEN, HEAD_DIM), CMP_HIDDEN ** -0.5),
        'mla_q_norm': gain(ks[10], (DEPTH, MLA_Q_RANK)),
        'mla_w_uq': nrm(ks[11], (DEPTH, MLA_Q_RANK, MLA_HEADS * (MLA_NOPE_DIM + MLA_ROPE_DIM)), MLA_Q_RANK ** -0.5),
        'mla_kv_norm': gain(ks[12], (DEPTH, MLA_KV_RANK)),
        'mla_w_ukv': nrm(ks[13], (DEPTH, MLA_KV_RANK, MLA_HEADS * (MLA_NOPE_DIM + MLA_V_DIM)), MLA_KV_RANK ** -0.5),
        'ret_gn_gain': gain(ks[14], (DEPTH, RET_HEADS, HEAD_DIM)),
        'w_out': nrm(ks[15], (DEPTH, MIX_WIDTH, D_MODEL), MIX_WIDTH ** -0.5),
        'ln2_gain': gain(ks[16], (DEPTH, D_MODEL)),
        'w_up': nrm(ks[17], (DEPTH, D_MODEL, D_FF), D_MODEL ** -0.5),
        'w_down': nrm(ks[18], (DEPTH, D_FF, D_MODEL), D_FF ** -0.5),
        'final_gain': gain(ks[19], (D_MODEL,)),
    }

def first_block(x, positions, ln1_gain, w_in, cmp_pos_k, cmp_w1_k, cmp_w2_k, cmp_pos_v, cmp_w1_v, cmp_w2_v,
              mla_q_norm, mla_w_uq, mla_kv_norm, mla_w_ukv, ret_gn_gain, w_out, ln2_gain, w_up, w_down,
              final_gain):
    b, s, _ = x.shape
    cos_p, sin_p = rope_tables(positions, PARTIAL_ROPE_DIM, ROPE_THETA)
    cos_m, sin_m = rope_tables(positions, MLA_ROPE_DIM, ROPE_THETA)
    cos_r, sin_r = rope_tables(positions, HEAD_DIM, RET_THETA)
    offsets = in_offsets()
    for l in range(DEPTH):
        h = rms_norm(x, ln1_gain[l])
        proj = h @ w_in[l]
        (nsa_q, k_cmp, v_cmp, k_slc, v_slc, k_win, v_win, nsa_gate,
         mla_cq, mla_ckv, mla_kpe, ret_q, ret_k, ret_v, ret_gate) = jnp.split(proj, offsets, axis=-1)

        def kv_heads(a):
            return a.reshape(b, s, NSA_KV_GROUPS, HEAD_DIM)

        o_nsa = nsa_mixer(
            partial_rope(nsa_q.reshape(b, s, NSA_HEADS, HEAD_DIM), cos_p, sin_p),
            partial_rope(kv_heads(k_cmp), cos_p, sin_p), kv_heads(v_cmp),
            partial_rope(kv_heads(k_slc), cos_p, sin_p), kv_heads(v_slc),
            partial_rope(kv_heads(k_win), cos_p, sin_p), kv_heads(v_win),
            nsa_gate.reshape(b, s, NSA_HEADS, N_BRANCH),
            cmp_pos_k[l], cmp_w1_k[l], cmp_w2_k[l], cmp_pos_v[l], cmp_w1_v[l], cmp_w2_v[l])
        o_mla = mla_mixer(mla_cq, mla_ckv, mla_kpe, mla_q_norm[l], mla_w_uq[l], mla_kv_norm[l], mla_w_ukv[l],
                          cos_m, sin_m)
        o_ret = retention_mixer(ret_q, ret_k, ret_v, ret_gate, ret_gn_gain[l], cos_r, sin_r)
        mixed = jnp.concatenate([o_nsa.astype(x.dtype), o_mla.astype(x.dtype), o_ret.astype(x.dtype)], axis=-1)
        x = x + mixed @ w_out[l]
        h = rms_norm(x, ln2_gain[l])
        x = x + jnp.square(jax.nn.relu(h @ w_up[l])) @ w_down[l]
    return rms_norm(x, final_gain)


CTX_LEN = 256
GRID_W = 64
INNER = D_MODEL
A_WIDTH = INNER // 2
B_WIDTH = INNER - A_WIDTH
B_HEADS = B_WIDTH // HEAD_DIM
B_KV_HEADS = B_HEADS // 4
KV_WIDTH = B_KV_HEADS * HEAD_DIM
CONV_WIDTH = 31
Q_BLOCK = 128
ROPE_THETA_2 = 10000.0
C_WIDTH = INNER // 2
C_GROUPS = 4
C_GROUP_DIM = C_WIDTH // C_GROUPS
D_WIDTH = INNER - C_WIDTH
D_HEADS = D_WIDTH // HEAD_DIM
NA_ROWS = 8
NA_COLS = 16
EPS = 1e-6
NEG_INF_2 = -1e30
N_AB = (DEPTH + 1) // 2
N_CD = DEPTH // 2

AB_Q_OFF = 2 * A_WIDTH
AB_K_OFF = AB_Q_OFF + B_WIDTH
AB_V_OFF = AB_K_OFF + KV_WIDTH
AB_Z_OFF = AB_V_OFF + KV_WIDTH
AB_IN = AB_Z_OFF + INNER
CD_Q_OFF = C_WIDTH
CD_K_OFF = CD_Q_OFF + D_WIDTH
CD_V_OFF = CD_K_OFF + D_WIDTH
CD_Z_OFF = CD_V_OFF + D_WIDTH
CD_IN = CD_Z_OFF + INNER


def rms_norm_2(x, g):
    x32 = x.astype(jnp.float32)
    y = x32 * lax.rsqrt(jnp.mean(x32 * x32, axis=-1, keepdims=True) + EPS)
    return (y * g.astype(jnp.float32)).astype(x.dtype)

def layer_norm(x, g, b):
    x32 = x.astype(jnp.float32)
    mu = jnp.mean(x32, axis=-1, keepdims=True)
    xc = x32 - mu
    y = xc * lax.rsqrt(jnp.mean(xc * xc, axis=-1, keepdims=True) + EPS)
    return (y * g.astype(jnp.float32) + b.astype(jnp.float32)).astype(x.dtype)

def adaln(cond, w, b):
    m = jax.nn.silu(cond) @ w + b
    return jnp.split(m, 3, axis=-1)

def axial_rope(x):
    S = x.shape[1]
    t = jnp.arange(S)
    row = (t // GRID_W).astype(jnp.float32)
    col = (t % GRID_W).astype(jnp.float32)
    nf = HEAD_DIM // 4
    inv = ROPE_THETA_2 ** (-jnp.arange(nf, dtype=jnp.float32) / nf)
    ang = jnp.concatenate([row[:, None] * inv, col[:, None] * inv], axis=-1)
    cos = jnp.cos(ang)[None, :, None, :]
    sin = jnp.sin(ang)[None, :, None, :]
    xp = x.astype(jnp.float32).reshape(x.shape[:-1] + (HEAD_DIM // 2, 2))
    a, b = xp[..., 0], xp[..., 1]
    out = jnp.stack([a * cos - b * sin, a * sin + b * cos], axis=-1)
    return out.reshape(x.shape).astype(x.dtype)

def dense_attn(q, k, v):
    Bq, Lq, Hq, dh = q.shape
    Hk = k.shape[2]
    qg = q.reshape(Bq, Lq, Hk, Hq // Hk, dh)
    s = jnp.einsum('bqkgd,bskd->bkgqs', qg, k).astype(jnp.float32) * (dh ** -0.5)
    p = jax.nn.softmax(s, axis=-1).astype(v.dtype)
    o = jnp.einsum('bkgqs,bskd->bqkgd', p, v)
    return o.reshape(Bq, Lq, Hq * dh)

def blocked_attn(q, k, v):
    Bq, S, Hq, dh = q.shape
    nb = S // Q_BLOCK
    qb = q.reshape(Bq, nb, Q_BLOCK, Hq, dh).transpose(1, 0, 2, 3, 4)
    ob = lax.map(lambda qi: dense_attn(qi, k, v), qb)
    return ob.transpose(1, 0, 2, 3).reshape(Bq, S, Hq * dh)

def dwconv(x, w, b):
    K = w.shape[0]
    y = lax.conv_general_dilated(x, w[:, None, :].astype(x.dtype), (1,), [(K // 2, K // 2)],
                                 dimension_numbers=('NWC', 'WIO', 'NWC'),
                                 feature_group_count=x.shape[-1])
    return y + b

def conformer_conv(a_val, a_gate, conv_w, conv_b, ln_g, ln_b):
    u = a_val * jax.nn.sigmoid(a_gate)
    u = dwconv(u, conv_w, conv_b)
    return jax.nn.silu(layer_norm(u, ln_g, ln_b))

def fourier_mix(f, w_c):
    Bf, L, _ = f.shape
    fg = f.reshape(Bf, L, C_GROUPS, C_GROUP_DIM).astype(jnp.float32)
    fr = jnp.fft.fft2(fg, axes=(1, 3), norm='ortho').real.astype(f.dtype)
    return jnp.einsum('blgc,gce->blge', fr, w_c).reshape(Bf, L, C_WIDTH)

def neighborhood_attn(q, k, v, kc, vc, rpb):
    Bq, S, H, dh = q.shape
    rows = S // GRID_W
    kr = min(NA_ROWS, rows)
    qg = q.reshape(Bq, rows, GRID_W, H, dh)
    kg = k.reshape(Bq, rows, GRID_W, H, dh)
    vg = v.reshape(Bq, rows, GRID_W, H, dh)
    r = jnp.arange(rows)
    rs = jnp.clip(r - kr // 2, 0, rows - kr)
    row_idx = rs[:, None] + jnp.arange(kr)[None, :]
    kb = kg[:, row_idx]
    vb = vg[:, row_idx]
    wq = jnp.arange(GRID_W)
    cs = jnp.clip(wq - NA_COLS // 2, 0, GRID_W - NA_COLS)
    col_ok = (wq[None, :] >= cs[:, None]) & (wq[None, :] < cs[:, None] + NA_COLS)
    dr_idx = row_idx - r[:, None] + (NA_ROWS - 1)
    dc_idx = jnp.clip(wq[None, :] - wq[:, None] + (NA_COLS - 1), 0, 2 * NA_COLS - 2)
    bias = rpb[:, dr_idx[:, None, :, None], dc_idx[None, :, None, :]]
    scale = dh ** -0.5
    s_win = jnp.einsum('brqhd,brkwhd->bhrqkw', qg, kb).astype(jnp.float32) * scale \
        + bias.astype(jnp.float32)[None]
    s_win = jnp.where(col_ok[:, None, :], s_win, NEG_INF_2).reshape(Bq, H, rows, GRID_W, kr * GRID_W)
    s_ctx = jnp.einsum('brqhd,bchd->bhrqc', qg, kc).astype(jnp.float32) * scale
    p = jax.nn.softmax(jnp.concatenate([s_win, s_ctx], axis=-1), axis=-1).astype(v.dtype)
    p_win = p[..., :kr * GRID_W].reshape(Bq, H, rows, GRID_W, kr, GRID_W)
    p_ctx = p[..., kr * GRID_W:]
    o = jnp.einsum('bhrqkw,brkwhd->brqhd', p_win, vb) + jnp.einsum('bhrqc,bchd->brqhd', p_ctx, vc)
    return o.reshape(Bq, S, H * dh)

def layer_ab(x, xc, c, c_ctx, w_ada, b_ada, norm_g, w_in, conv_w, conv_b, ln_g, ln_b,
             qn_g, kn_g, w_out, need_ctx):
    Bx, S, _ = x.shape
    L = xc.shape[1]
    shift, scale, gate = adaln(c[:, None, :], w_ada, b_ada)
    cshift, cscale, cgate = adaln(c_ctx, w_ada, b_ada)
    h = rms_norm_2(x, norm_g) * (1 + scale) + shift
    hc = rms_norm_2(xc, norm_g) * (1 + cscale) + cshift
    u = h @ w_in
    a_val, a_gate = u[..., :A_WIDTH], u[..., A_WIDTH:AB_Q_OFF]
    q = u[..., AB_Q_OFF:AB_K_OFF].reshape(Bx, S, B_HEADS, HEAD_DIM)
    k = u[..., AB_K_OFF:AB_V_OFF].reshape(Bx, S, B_KV_HEADS, HEAD_DIM)
    v = u[..., AB_V_OFF:AB_Z_OFF].reshape(Bx, S, B_KV_HEADS, HEAD_DIM)
    z = u[..., AB_Z_OFF:]
    uc = hc @ (w_in if need_ctx else w_in[:, AB_K_OFF:AB_Z_OFF])
    kv_off = AB_K_OFF if need_ctx else 0
    ck = uc[..., kv_off:kv_off + KV_WIDTH].reshape(Bx, L, B_KV_HEADS, HEAD_DIM)
    cv = uc[..., kv_off + KV_WIDTH:kv_off + 2 * KV_WIDTH].reshape(Bx, L, B_KV_HEADS, HEAD_DIM)
    ck = rms_norm_2(ck, kn_g)
    q = axial_rope(rms_norm_2(q, qn_g))
    k = axial_rope(rms_norm_2(k, kn_g))
    y_b = blocked_attn(q, jnp.concatenate([ck, k], axis=1), jnp.concatenate([cv, v], axis=1))
    y_a = conformer_conv(a_val, a_gate, conv_w, conv_b, ln_g, ln_b)
    y = jnp.concatenate([y_a, y_b], axis=-1) * jax.nn.silu(z)
    x = x + gate * (y @ w_out)
    if need_ctx:
        cq = rms_norm_2(uc[..., AB_Q_OFF:AB_K_OFF].reshape(Bx, L, B_HEADS, HEAD_DIM), qn_g)
        yc_b = dense_attn(cq, ck, cv)
        yc_a = conformer_conv(uc[..., :A_WIDTH], uc[..., A_WIDTH:AB_Q_OFF], conv_w, conv_b, ln_g, ln_b)
        yc = jnp.concatenate([yc_a, yc_b], axis=-1) * jax.nn.silu(uc[..., AB_Z_OFF:])
        xc = xc + cgate * (yc @ w_out)
    return x, xc

def layer_cd(x, xc, c, c_ctx, w_ada, b_ada, norm_g, w_in, w_fourier, rpb, w_out, need_ctx):
    Bx, S, _ = x.shape
    L = xc.shape[1]
    shift, scale, gate = adaln(c[:, None, :], w_ada, b_ada)
    cshift, cscale, cgate = adaln(c_ctx, w_ada, b_ada)
    h = rms_norm_2(x, norm_g) * (1 + scale) + shift
    hc = rms_norm_2(xc, norm_g) * (1 + cscale) + cshift
    u = h @ w_in
    f = u[..., :C_WIDTH]
    q = u[..., CD_Q_OFF:CD_K_OFF].reshape(Bx, S, D_HEADS, HEAD_DIM)
    k = u[..., CD_K_OFF:CD_V_OFF].reshape(Bx, S, D_HEADS, HEAD_DIM)
    v = u[..., CD_V_OFF:CD_Z_OFF].reshape(Bx, S, D_HEADS, HEAD_DIM)
    z = u[..., CD_Z_OFF:]
    uc = hc @ (w_in if need_ctx else w_in[:, CD_K_OFF:CD_Z_OFF])
    kv_off = CD_K_OFF if need_ctx else 0
    ck = uc[..., kv_off:kv_off + D_WIDTH].reshape(Bx, L, D_HEADS, HEAD_DIM)
    cv = uc[..., kv_off + D_WIDTH:kv_off + 2 * D_WIDTH].reshape(Bx, L, D_HEADS, HEAD_DIM)
    y_c = fourier_mix(f, w_fourier)
    y_d = neighborhood_attn(q, k, v, ck, cv, rpb)
    y = jnp.concatenate([y_c, y_d], axis=-1) * jax.nn.silu(z)
    x = x + gate * (y @ w_out)
    if need_ctx:
        cq = uc[..., CD_Q_OFF:CD_K_OFF].reshape(Bx, L, D_HEADS, HEAD_DIM)
        yc_d = dense_attn(cq, ck, cv)
        yc_c = fourier_mix(uc[..., :C_WIDTH], w_fourier)
        yc = jnp.concatenate([yc_c, yc_d], axis=-1) * jax.nn.silu(uc[..., CD_Z_OFF:])
        xc = xc + cgate * (yc @ w_out)
    return x, xc

def second_inputs(seed: int = 0) -> dict:
    key = jax.random.key(seed)
    ks = iter(jax.random.split(key, 32))
    nrm = lambda shape, s: jax.random.normal(next(ks), shape, jnp.float32) * s
    gain = lambda shape: 1.0 + nrm(shape, 0.05)
    return {
        "x": nrm((BATCH, SEQ, D_MODEL), 1.0),
        "c": nrm((BATCH, D_MODEL), 1.0),
        "ctx": nrm((BATCH, CTX_LEN, D_MODEL), 1.0),
        "c_ctx": nrm((D_MODEL,), 1.0),
        "ab_w_ada": nrm((N_AB, D_MODEL, 3 * D_MODEL), 0.5 * D_MODEL ** -0.5),
        "ab_b_ada": nrm((N_AB, 3 * D_MODEL), 0.01),
        "ab_norm_g": gain((N_AB, D_MODEL)),
        "ab_w_in": nrm((N_AB, D_MODEL, AB_IN), D_MODEL ** -0.5),
        "ab_conv_w": nrm((N_AB, CONV_WIDTH, A_WIDTH), CONV_WIDTH ** -0.5),
        "ab_conv_b": nrm((N_AB, A_WIDTH), 0.01),
        "ab_ln_g": gain((N_AB, A_WIDTH)),
        "ab_ln_b": nrm((N_AB, A_WIDTH), 0.01),
        "ab_q_norm_g": gain((N_AB, HEAD_DIM)),
        "ab_k_norm_g": gain((N_AB, HEAD_DIM)),
        "ab_w_out": nrm((N_AB, INNER, D_MODEL), INNER ** -0.5),
        "cd_w_ada": nrm((N_CD, D_MODEL, 3 * D_MODEL), 0.5 * D_MODEL ** -0.5),
        "cd_b_ada": nrm((N_CD, 3 * D_MODEL), 0.01),
        "cd_norm_g": gain((N_CD, D_MODEL)),
        "cd_w_in": nrm((N_CD, D_MODEL, CD_IN), D_MODEL ** -0.5),
        "cd_w_fourier": nrm((N_CD, C_GROUPS, C_GROUP_DIM, C_GROUP_DIM), C_GROUP_DIM ** -0.5),
        "cd_rpb": nrm((N_CD, D_HEADS, 2 * NA_ROWS - 1, 2 * NA_COLS - 1), 0.1),
        "cd_w_out": nrm((N_CD, INNER, D_MODEL), INNER ** -0.5),
        "final_norm_g": gain((D_MODEL,)),
    }

def second_block(x, c, ctx, c_ctx, ab_w_ada, ab_b_ada, ab_norm_g, ab_w_in, ab_conv_w, ab_conv_b,
              ab_ln_g, ab_ln_b, ab_q_norm_g, ab_k_norm_g, ab_w_out, cd_w_ada, cd_b_ada, cd_norm_g,
              cd_w_in, cd_w_fourier, cd_rpb, cd_w_out, final_norm_g):
    xc = ctx
    for layer in range(DEPTH):
        need_ctx = layer < DEPTH - 1
        i = layer // 2
        if layer % 2 == 0:
            x, xc = layer_ab(x, xc, c, c_ctx, ab_w_ada[i], ab_b_ada[i], ab_norm_g[i], ab_w_in[i],
                             ab_conv_w[i], ab_conv_b[i], ab_ln_g[i], ab_ln_b[i],
                             ab_q_norm_g[i], ab_k_norm_g[i], ab_w_out[i], need_ctx)
        else:
            x, xc = layer_cd(x, xc, c, c_ctx, cd_w_ada[i], cd_b_ada[i], cd_norm_g[i], cd_w_in[i],
                             cd_w_fourier[i], cd_rpb[i], cd_w_out[i], need_ctx)
    return rms_norm_2(x, final_norm_g)


def setup_inputs(seed=0):
    out = dict(first_inputs(seed))
    for name, value in second_inputs(seed + 1).items():
        if name != "x":
            out[name + "_2"] = value
    return out


def reference(
    x, positions, ln1_gain, w_in, cmp_pos_k, cmp_w1_k, cmp_w2_k, cmp_pos_v, cmp_w1_v, cmp_w2_v,
    mla_q_norm, mla_w_uq, mla_kv_norm, mla_w_ukv, ret_gn_gain, w_out, ln2_gain, w_up, w_down,
    final_gain, c_2, ctx_2, c_ctx_2, ab_w_ada_2, ab_b_ada_2, ab_norm_g_2, ab_w_in_2,
    ab_conv_w_2, ab_conv_b_2, ab_ln_g_2, ab_ln_b_2, ab_q_norm_g_2, ab_k_norm_g_2, ab_w_out_2,
    cd_w_ada_2, cd_b_ada_2, cd_norm_g_2, cd_w_in_2, cd_w_fourier_2, cd_rpb_2, cd_w_out_2,
    final_norm_g_2,
):
    x = first_block(
        x, positions, ln1_gain, w_in, cmp_pos_k, cmp_w1_k, cmp_w2_k, cmp_pos_v, cmp_w1_v,
        cmp_w2_v, mla_q_norm, mla_w_uq, mla_kv_norm, mla_w_ukv, ret_gn_gain, w_out, ln2_gain,
        w_up, w_down, final_gain,
    )
    return second_block(
        x, c_2, ctx_2, c_ctx_2, ab_w_ada_2, ab_b_ada_2, ab_norm_g_2, ab_w_in_2, ab_conv_w_2,
        ab_conv_b_2, ab_ln_g_2, ab_ln_b_2, ab_q_norm_g_2, ab_k_norm_g_2, ab_w_out_2, cd_w_ada_2,
        cd_b_ada_2, cd_norm_g_2, cd_w_in_2, cd_w_fourier_2, cd_rpb_2, cd_w_out_2,
        final_norm_g_2,
    )


_drawn_inputs = setup_inputs


def setup_inputs(seed=0):
    import zlib

    import numpy as np

    out = dict(_drawn_inputs(seed))
    spreads = {}
    factors = {'ln1_gain': 2.784,
     'cmp_pos_k': 8.0,
     'mla_q_norm': 8.0,
     'mla_kv_norm': 8.0,
     'ret_gn_gain': 6.633,
     'final_gain': 2.807,
     'ctx_2': 3.464,
     'ab_b_ada_2': 8.0,
     'ab_norm_g_2': 8.0,
     'ab_conv_b_2': 8.0,
     'ab_ln_g_2': 8.0,
     'ab_ln_b_2': 8.0,
     'ab_q_norm_g_2': 8.0,
     'ab_k_norm_g_2': 8.0,
     'cd_b_ada_2': 8.0,
     'cd_norm_g_2': 7.008,
     'cd_rpb_2': 8.0}
    for name, (base, spread) in spreads.items():
        noise = np.random.default_rng([zlib.crc32(name.encode()), seed]).standard_normal(out[name].shape)
        drawn = base * np.exp(spread * noise) if base else spread * noise
        out[name] = __import__('jax').numpy.asarray(drawn.astype(out[name].dtype))
    for name, factor in factors.items():
        out[name] = (out[name] * factor).astype(out[name].dtype)
    return out
```

```python
from contextlib import ExitStack, contextmanager

import numpy as np

import concourse.bass as bass
from concourse import mybir

F32 = mybir.dt.float32
I32 = mybir.dt.int32
ALU = mybir.AluOpType
ACT = mybir.ActivationFunctionType
AX = mybir.AxisListType

P = 128
D = 1024
KC = D // P
SEQ = 256
TT = SEQ // P
DEPTH = 2
DFF = 4 * D
HD = 64
EPS = 1e-6
NEG = -1e30
SLAB = 4096
SLOTS = 4
BANK = 512

NSA_H, NSA_G, NSA_R = 6, 2, 3
MLA_H, MLA_NOPE, MLA_PE, MLA_QK = 5, 64, 32, 96
RET_H = 5
Q0, KCMP0, KSLC0, KWIN0 = 0, 384, 512, 640
VCMP0, VSLC0, VWIN0 = 768, 896, 1024
GATE0, CQ0, CKV0, KPE0 = 1152, 1170, 1426, 1554
RQ0, RK0, RV0, RG0 = 1586, 1906, 2226, 2546
N_IN = 2866
W_IN_SLABS = -(-N_IN // BANK)
NSA_PAIRS = ((0, 3), (1, 4), (2, 5))
N_CMP = (SEQ - 32) // 16 + 1
CMP_LP = 16
ROPE_P, ROPE_M, ROPE_R = (0, 8), (8, 24), (24, 56)
ROPE_N = 56

AB_VAL0, AB_GATE0, AB_Q0, AB_K0, AB_V0, AB_Z0, AB_N = 0, 512, 1024, 1536, 1664, 1792, 2816
B_HEADS, B_KV = 8, 2
CONV_W, CONV_PAD = 31, 15
CD_F0, CD_Q0, CD_K0, CD_V0, CD_Z0, CD_N = 0, 512, 1024, 1536, 2048, 3072
D_HEADS, C_GROUPS = 8, 4
GRID_W, ROWS, N_DR, N_DC = 64, 4, 7, 31

LAYER_SLABS = [("w_in", W_IN_SLABS), ("cmp_w1", 1), ("small", 1), ("w_out", 2), ("w_up", 8), ("w_down", 8)]
SECOND_SLABS = [("ab_ada", 6), ("ab_in", 6), ("ab_out", 2), ("cd_ada", 6), ("cd_in", 6), ("cd_out", 2)]
SMALL_W = 2 * 480 + 640 + 2 * HD
UQ0, UKV0, W2K0, W2V0 = 0, 960, 1600, 1664


class InOrder:

    def __init__(self, engine, done):
        self.engine, self.done, self.n = engine, done, 0

    def __call__(self, instruction):
        self.n += 1
        instruction.then_inc(self.done, 1)
        self.engine.wait_ge(self.done, self.n)


def slab_plan():
    plan, first = [], {}
    for layer in range(DEPTH):
        for name, n in LAYER_SLABS:
            first[name, layer] = len(plan)
            plan += [(name, layer * n + i, SMALL_W if name == "small" else SLAB) for i in range(n)]
    for name, n in SECOND_SLABS:
        first[name] = len(plan)
        plan += [(name, i, SLAB) for i in range(n)]
    return plan, first


def build_program(nc, dram, out):
    plan, first = slab_plan()
    with ExitStack() as ctx:
        def sbuf(name, shape, dt=F32):
            return ctx.enter_context(nc.sbuf_tensor(name, shape, dt))

        ring = sbuf("ring", [P, SLOTS, SLAB])
        x = sbuf("x", [P, 4, D])
        hT = sbuf("hT", [P, KC, 2 * SEQ])
        mixed = sbuf("mixed", [P, 4, D])
        proj = sbuf("proj", [P, 4, 3072])
        ident = sbuf("ident", [P, P])
        sums = sbuf("sums", [P, 96])
        rstd = sbuf("rstd", [P, 96])
        minus_half = sbuf("minus_half", [P, 96])
        banks = ctx.enter_context(nc.psum_tensor("banks", [P, 8, BANK], F32))

        slab_landed = [ctx.enter_context(nc.semaphore(f"slab_landed{i}")) for i in range(SLOTS)]
        slab_used = ctx.enter_context(nc.semaphore("slab_used"))
        loaded = ctx.enter_context(nc.semaphore("loaded"))
        stored = ctx.enter_context(nc.semaphore("stored"))
        n_loaded, n_stages = [0], [0]

        def load_slab(sp, i):
            if i >= len(plan):
                return
            if i >= SLOTS:
                sp.wait_ge(slab_used, i - SLOTS + 1)
            name, at, width = plan[i]
            sp.dma_start(ring[:, i % SLOTS, 0:width], dram[name][at, :, 0:width]).then_inc(slab_landed[i % SLOTS], 16)

        def load_behind(sp, slabs):
            for i in slabs:
                load_slab(sp, i + SLOTS)

        def slab_here(pe, i):
            pe.wait_ge(slab_landed[i % SLOTS], 16 * (i // SLOTS + 1))

        def load_const(sp, dst, src):
            sp.dma_start(dst, src).then_inc(loaded, 16)
            n_loaded[0] += 16

        @contextmanager
        def stage(*names):
            n_stages[0] += 1
            sems = [nc.alloc_semaphore(f"{n}_{n_stages[0]}") for n in names]
            yield sems
            nc.clear_and_free_semaphores(sems)
            nc.all_engine_barrier()

        def accumulate(dst, pairs):
            n = len(pairs)
            for i, (lhsT, rhs) in enumerate(pairs):
                mm = nc.tensor.matmul(dst, lhsT, rhs, start=(i == 0), stop=(i == n - 1))
            return mm


        def normalize_transpose(tiles, scales, shifts=None):
            T = len(tiles)
            per = len(scales)
            span = T * P // per
            with stage("squares_summed", "pool_step", "rstd_ready", "scaled", "turned") as (
                    squares_summed, pool_step, rstd_ready, scaled, turned), nc.Block() as block:
                @block.vector
                def _(dve):
                    for n, t in enumerate(tiles):
                        nc.vector.tensor_tensor_reduce(mixed[:, t, :], x[:, t, :], x[:, t, :], 1.0, 0.0, ALU.mult,
                                                       ALU.add, sums[:, n:n + 1]).then_inc(squares_summed, 1)
                    for c in range(KC):
                        dve.wait_ge(turned, c + 1)
                        for v in range(per):
                            src = banks[:, c, v * span:(v + 1) * span]
                            dst = hT[:, c, v * span:(v + 1) * span]
                            if shifts is None:
                                nc.vector.tensor_scalar(dst, src, scales[v][:, c:c + 1], None, ALU.mult)
                            else:
                                nc.vector.tensor_scalar(dst, src, scales[v][:, c:c + 1], shifts[v][:, c:c + 1],
                                                        ALU.mult, ALU.add)

                @block.gpsimd
                def _(pool):
                    step = InOrder(pool, pool_step)
                    pool.wait_ge(squares_summed, T)
                    step(nc.gpsimd.tensor_scalar(rstd[:, 0:T], sums[:, 0:T], 1.0 / D, EPS, ALU.mult, ALU.add))
                    nc.gpsimd.tensor_tensor(rstd[:, 0:T], rstd[:, 0:T], minus_half[:, 0:T],
                                            ALU.pow).then_inc(rstd_ready, 1)

                @block.scalar
                def _(act):
                    act.wait_ge(rstd_ready, 1)
                    for n, t in enumerate(tiles):
                        nc.scalar.activation(mixed[:, t, :], x[:, t, :], ACT.Copy,
                                             scale=rstd[:, n:n + 1]).then_inc(scaled, 1)

                @block.tensor
                def _(pe):
                    pe.wait_ge(scaled, T)
                    for c in range(KC):
                        for n, t in enumerate(tiles):
                            mm = nc.tensor.transpose(banks[:, c, n * P:(n + 1) * P],
                                                     mixed[:, t, c * P:(c + 1) * P], ident[:])
                        mm.then_inc(turned, 1)

        def project(slab0, widths, tiles_of, dst):
            units = [(s, t) for s in range(len(widths)) for t in tiles_of[s]]
            with stage("product_ready", "evacuated") as (product_ready, evacuated), nc.Block() as block:
                @block.sync
                def _(sp):
                    load_behind(sp, range(slab0, slab0 + len(widths)))

                @block.tensor
                def _(pe):
                    for u, (s, t) in enumerate(units):
                        w = ring[:, (slab0 + s) % SLOTS, :].rearrange("p (k n) -> p k n", k=KC)
                        if t == tiles_of[s][0]:
                            slab_here(pe, slab0 + s)
                        if u >= 8:
                            pe.wait_ge(evacuated, u - 7)
                        mm = accumulate(banks[:, u % 8, 0:widths[s]],
                                        [(hT[:, k, t * P:(t + 1) * P], w[:, k, 0:widths[s]]) for k in range(KC)])
                        mm.then_inc(product_ready, 1)
                        if t == tiles_of[s][-1]:
                            pe.wait_ge(product_ready, u + 1)
                            pe.sem_inc(slab_used, 1)

                @block.scalar
                def _(act):
                    for u, (s, t) in enumerate(units):
                        act.wait_ge(product_ready, u + 1)
                        nc.scalar.copy(dst[:, t, s * BANK:s * BANK + widths[s]],
                                       banks[:, u % 8, 0:widths[s]]).then_inc(evacuated, 1)

        def transpose_groups(groups):
            with stage("turned", "copied0", "copied1") as (turned, copied0, copied1), nc.Block() as block:
                @block.tensor
                def _(pe):
                    for g, (blocks, _) in enumerate(groups):
                        if g >= 8:
                            pe.wait_ge((copied0, copied1)[g % 2], (g - 8) // 2 + 1)
                        for j, src in enumerate(blocks):
                            w = src.shape[-1]
                            mm = nc.tensor.transpose(banks[0:w, g % 8, j * P:(j + 1) * P], src, ident[:])
                        mm.then_inc(turned, 1)

                @block.vector
                def _(dve):
                    for g, (_, copies) in enumerate(groups):
                        if g % 2 == 0:
                            dve.wait_ge(turned, g + 1)
                            for copy in copies:
                                last = copy(nc.vector, banks[:, g % 8, :])
                            last.then_inc(copied0, 1)

                @block.scalar
                def _(act):
                    for g, (_, copies) in enumerate(groups):
                        if g % 2 == 1:
                            act.wait_ge(turned, g + 1)
                            for copy in copies:
                                last = copy(nc.scalar, banks[:, g % 8, :])
                            last.then_inc(copied1, 1)

        def copy_out(engine, dst, src, scale=None, bias=None):
            if engine is nc.scalar:
                if scale is None:
                    return nc.scalar.copy(dst, src)
                return nc.scalar.activation(dst, src, ACT.Copy, scale=scale)
            if scale is None:
                return nc.vector.tensor_copy(dst, src)
            return nc.vector.tensor_scalar(dst, src, scale, None, ALU.mult)

        def out_project(slab0, lhsT, tiles, gates=None):
            units = [(s, t) for s in range(2) for t in tiles]
            with stage("product_ready", "added", "gated") as (product_ready, added, gated), nc.Block() as block:
                @block.sync
                def _(sp):
                    load_behind(sp, range(slab0, slab0 + 2))

                @block.tensor
                def _(pe):
                    for u, (s, t) in enumerate(units):
                        w = ring[:, (slab0 + s) % SLOTS, :].rearrange("p (k n) -> p k n", k=KC)
                        if t == tiles[0]:
                            slab_here(pe, slab0 + s)
                        mm = accumulate(banks[:, u, :],
                                        [(lhsT[:, k, t * P:(t + 1) * P], w[:, k, :]) for k in range(KC)])
                        mm.then_inc(product_ready, 1)
                        if t == tiles[-1]:
                            pe.wait_ge(product_ready, u + 1)
                            pe.sem_inc(slab_used, 1)

                @block.vector
                def _(dve):
                    for u, (s, t) in enumerate(units):
                        here = x[:, t, s * BANK:(s + 1) * BANK]
                        dve.wait_ge(product_ready, u + 1)
                        src = banks[:, u, :]
                        if gates is not None:
                            gated_y = mixed[:, t, s * BANK:(s + 1) * BANK]
                            nc.vector.tensor_tensor(gated_y, src, gates[t // 2][:, s * BANK:(s + 1) * BANK],
                                                    ALU.mult).then_inc(gated, 1)
                            dve.wait_ge(gated, u + 1)
                            src = gated_y
                        nc.vector.tensor_tensor(here, src, here, ALU.add)

        def attend(units, buffers):
            probs, probsT, nmax, total, inverse = buffers
            n_units = len(units)
            with stage("scores_ready", "max_ready", "probs_ready", "probs_turned",
                       "turned_copied", "values_ready", "weighed", "dve_step") as (
                    scores_ready, max_ready, probs_ready, probs_turned,
                    turned_copied, values_ready, weighed, dve_step), nc.Block() as block:
                @block.tensor
                def _(pe):
                    def scores(i):
                        if i >= 2:
                            pe.wait_ge(probs_ready, i - 1)
                        for qT, kT, c0, n, _ in units[i]["rows"]:
                            mm = nc.tensor.matmul(banks[:, i % 2, c0:c0 + n], qT, kT, start=True, stop=True)
                        mm.then_inc(scores_ready, 1)

                    def turn(i):
                        pe.wait_ge(probs_ready, i + 1)
                        if i >= 2:
                            pe.wait_ge(turned_copied, i - 1)
                        for c in range(units[i]["width"] // P):
                            mm = nc.tensor.transpose(banks[:, 2 + i % 2, c * P:(c + 1) * P],
                                                     probs[:, i % 2, c * P:(c + 1) * P], ident[:])
                        mm.then_inc(probs_turned, 1)

                    def values(i):
                        pe.wait_ge(turned_copied, i + 1)
                        if i >= 2:
                            pe.wait_ge(weighed, i - 1)
                        for r, (_, _, c0, n, vs) in enumerate(units[i]["rows"]):
                            mm = accumulate(banks[:, 4 + i % 2, r * HD:(r + 1) * HD],
                                            [(probsT[:, i % 2, c0 + c * P:c0 + (c + 1) * P], v)
                                             for c, v in enumerate(vs)])
                        mm.then_inc(values_ready, 1)

                    for i in range(n_units + 2):
                        if i < n_units:
                            scores(i)
                        if 1 <= i <= n_units:
                            turn(i - 1)
                        if i >= 2:
                            values(i - 2)

                @block.vector
                def _(dve):
                    step = InOrder(dve, dve_step)

                    def maxima(i):
                        unit = units[i]
                        dve.wait_ge(scores_ready, i + 1)
                        src = banks[:, i % 2, :]
                        if unit["mask"] is not None:
                            m = src[:, 0:unit["mask"].free_size()]
                            step(nc.vector.scalar_tensor_tensor(out=m, in0=m, scalar=unit["scale"],
                                                                in1=unit["mask"], op0=ALU.mult, op1=ALU.add))
                        for r, (_, _, c0, n, _) in enumerate(unit["rows"]):
                            last = nc.vector.tensor_reduce(nmax[:, i % 2, r:r + 1], src[:, c0:c0 + n], AX.X, ALU.max,
                                                           negate=True)
                        last.then_inc(max_ready, 1)

                    def copy_turned(i):
                        dve.wait_ge(probs_turned, i + 1)
                        if i >= 2:
                            dve.wait_ge(values_ready, i - 1)
                        w = units[i]["width"]
                        nc.vector.tensor_copy(probsT[:, i % 2, 0:w], banks[:, 2 + i % 2, 0:w]).then_inc(turned_copied, 1)

                    def weigh(i):
                        unit = units[i]
                        R = len(unit["rows"])
                        step(nc.vector.reciprocal(inverse[:, i % 2, 0:R], total[:, i % 2, 0:R]))
                        dve.wait_ge(values_ready, i + 1)
                        for r in range(R):
                            last = unit["weigh"](step, r, banks[:, 4 + i % 2, r * HD:(r + 1) * HD],
                                                 inverse[:, i % 2, r:r + 1])
                        last.then_inc(weighed, 1)

                    for i in range(n_units + 2):
                        if i < n_units:
                            maxima(i)
                        if 1 <= i <= n_units:
                            copy_turned(i - 1)
                        if i >= 2:
                            weigh(i - 2)

                @block.scalar
                def _(act):
                    for i, unit in enumerate(units):
                        act.wait_ge(max_ready, i + 1)
                        if i >= 2:
                            act.wait_ge(probs_turned, i - 1)
                            act.wait_ge(weighed, i - 1)
                        src = banks[:, i % 2, :]
                        for r, (_, _, c0, n, _) in enumerate(unit["rows"]):
                            last = nc.scalar.activation(probs[:, i % 2, c0:c0 + n], src[:, c0:c0 + n], ACT.Exp,
                                                        bias=nmax[:, i % 2, r:r + 1],
                                                        accum_out=total[:, i % 2, r:r + 1])
                        last.then_inc(probs_ready, 1)

        def rope(dve, step, v, cos, sin, half, temps):
            T, H = v.shape[1], v.shape[2]
            shape = [P, T, H, half]
            c = cos.unsqueeze(2).broadcast_to(shape)
            s = sin.unsqueeze(2).broadcast_to(shape)
            x1, x2 = v[:, :, :, 0:half], v[:, :, :, half:2 * half]
            a, b, e, f = [t[:, 0:T * H * half].rearrange("p (t h d) -> p t h d", t=T, h=H) for t in temps]
            nc.vector.tensor_tensor(a, x1, c, ALU.mult)
            nc.vector.tensor_tensor(b, x2, s, ALU.mult)
            nc.vector.tensor_tensor(e, x2, c, ALU.mult)
            step(nc.vector.tensor_tensor(f, x1, s, ALU.mult))
            nc.vector.tensor_tensor(x1, a, b, ALU.subtract)
            step(nc.vector.tensor_tensor(x2, e, f, ALU.add))

        def first_block():
            with ExitStack() as local:
                def sb(name, shape, dt=F32):
                    return local.enter_context(nc.sbuf_tensor(name, shape, dt))

                fT = sb("fT", [P, 11, SEQ])
                causal = sb("causal", [P, 3 * P])
                cmp_add = sb("cmp_add", [P, TT * 16])
                cmp_keep = sb("cmp_keep", [P, TT * 16])
                feats = sb("feats", [P, DEPTH, 51])
                gn_gain = sb("gn_gain", [P, RET_H * HD])
                cosT, sinT = sb("cosT", [P, TT, ROPE_N]), sb("sinT", [P, TT, ROPE_N])
                mla_v = sb("mla_v", [P, TT, MLA_H * HD])
                masked, probs, probsT = (sb(n, [P, 2, 3 * P]) for n in ("masked", "probs", "probsT"))
                nmax, total, inverse = (sb(n, [P, 2, 2]) for n in ("nmax", "total", "inverse"))
                buffers = (probs, probsT, nmax, total, inverse)
                k2 = sb("k2", [P, 2, NSA_G, P])
                flat = sb("flat", [P, 2, CMP_LP, NSA_G, N_CMP])
                gelu = sb("gelu", [P, 4, 4 * N_CMP])
                kcT, vc = sb("kcT", [P, N_CMP]), sb("vc", [N_CMP, NSA_G, HD])
                branch = sb("branch", [P, 2, TT * 18])
                cq_sq = sb("cq_sq", [P, TT * 384])

                mqT = hT[0:MLA_QK, 0:3, :].rearrange("p a b -> p (a b)")[:, 0:MLA_H * SEQ].rearrange(
                    "p (h s) -> p h s", h=MLA_H)
                mkT = hT[0:MLA_QK, 3:6, :].rearrange("p a b -> p (a b)")[:, 0:MLA_H * SEQ].rearrange(
                    "p (h s) -> p h s", h=MLA_H)
                decay = proj[:, 3, 0:RET_H * 3 * P].rearrange("p (h c) -> p h c", h=RET_H)
                mla_q = proj[:, 2, 0:TT * 480].rearrange("p (t n) -> p t n", t=TT)
                mla_k = proj[:, 2, TT * 480:2 * TT * 480].rearrange("p (t n) -> p t n", t=TT)
                flat_m = mixed[:, 2:4, :].rearrange("p a b -> p (a b)")
                temps = [flat_m[:, i * 640:(i + 1) * 640] for i in range(3)]
                temps.append(masked[:, :, :].rearrange("p a b -> p (a b)")[:, 0:640])
                scratch = mixed[:, 2:4, :].rearrange("p a b -> p (a b)")

                with stage("dve_step", "angles_ready", "sines_ready") as (dve_step, angles_ready, sines_ready), \
                        nc.Block() as block:
                    pos_i = local.enter_context(nc.sbuf_tensor("pos_i", [P, TT], I32))
                    pos = sb("pos", [P, TT])
                    freqs = sb("freqs", [P, ROPE_N])
                    ang = scratch[:, 0:TT * ROPE_N].rearrange("p (t n) -> p t n", t=TT)
                    turns = scratch[:, 256:256 + TT * ROPE_N].rearrange("p (t n) -> p t n", t=TT)
                    quarter = scratch[:, 512:512 + TT * ROPE_N].rearrange("p (t n) -> p t n", t=TT)

                    @block.sync
                    def _(sp):
                        load_const(sp, pos_i[:], dram["positions"])
                        load_const(sp, freqs[:], dram["freqs"])
                        load_const(sp, x[:, 0:TT, :], dram["x"])
                        load_const(sp, ident[:], dram["ident"])
                        load_const(sp, feats[:], dram["feats"])
                        for i in range(SLOTS):
                            load_slab(sp, i)
                        load_const(sp, causal[:], dram["causal"])
                        load_const(sp, decay, dram["decay"])
                        load_const(sp, cmp_add[:], dram["cmp_add"])
                        load_const(sp, cmp_keep[:], dram["cmp_keep"])
                        load_const(sp, x[:, TT:2 * TT, :], dram["ctx"])
                        sp.wait_ge(loaded, n_loaded[0])

                    @block.gpsimd
                    def _(pool):
                        nc.gpsimd.memset(minus_half[:], -0.5)

                    @block.vector
                    def _(dve):
                        step = InOrder(dve, dve_step)
                        dve.wait_ge(loaded, n_loaded[0])
                        step(nc.vector.tensor_copy(pos[:], pos_i[:]))
                        for t in range(TT):
                            last = nc.vector.tensor_scalar(ang[:, t, :], freqs[:], pos[:, t:t + 1], None, ALU.mult)
                        step(last)
                        step(nc.vector.tensor_scalar(turns, ang, 1.0 / (2 * np.pi), 1.5 * 2.0 ** 23, ALU.mult, ALU.add))
                        step(nc.vector.tensor_scalar(turns, turns, -1.5 * 2.0 ** 23, None, ALU.add))
                        hi = 6.28125
                        for part in (hi, 2 * np.pi - hi):
                            step(nc.vector.scalar_tensor_tensor(out=ang, in0=turns, scalar=-part, in1=ang,
                                                                op0=ALU.mult, op1=ALU.add))
                        edge = 3.1415925
                        step(nc.vector.tensor_scalar(ang, ang, edge, -edge, ALU.min, ALU.max))
                        step(nc.vector.scalar_tensor_tensor(out=quarter, in0=ang, scalar=-1.0, in1=ang,
                                                            op0=ALU.mult, op1=ALU.min))
                        nc.vector.tensor_scalar(quarter, quarter, np.pi / 2, None, ALU.add).then_inc(angles_ready, 1)

                    @block.scalar
                    def _(act):
                        act.wait_ge(angles_ready, 1)
                        nc.scalar.activation(sinT[:], ang, ACT.Sin)
                        nc.scalar.activation(cosT[:], quarter, ACT.Sin)

                for layer in range(DEPTH):
                    f = feats[:, layer, :]
                    ln1, ln2, qn, kvn = f[:, 0:8], f[:, 8:16], f[:, 16:18], f[:, 18:19]
                    pos_of = (f[:, 19:35], f[:, 35:51])
                    normalize_transpose((0, 1), [ln1])
                    widths = [min(BANK, N_IN - i * BANK) for i in range(W_IN_SLABS)]
                    project(first["w_in", layer], widths, [(0, 1)] * W_IN_SLABS, proj)
                    prepare_heads(layer, temps, cosT, sinT, gn_gain, branch, cq_sq, scratch)
                    transpose_heads(fT, k2, qn, kvn)
                    small_products(layer, k2, flat, pos_of, gelu, kcT, vc, mla_q, mla_k, mla_v, cosT, sinT, temps)
                    groups = []
                    for src, dst in ((mla_q, mqT), (mla_k, mkT)):
                        for h0 in range(0, MLA_H, 2):
                            hs = range(h0, min(h0 + 2, MLA_H))
                            blocks = [src[:, t, h * MLA_QK:(h + 1) * MLA_QK] for h in hs for t in range(TT)]
                            n = len(blocks) * P

                            def copy(engine, bank, dst=dst, h0=h0, hs=hs, n=n):
                                return copy_out(engine, dst[:, h0:h0 + len(hs), :],
                                                bank[0:MLA_QK, 0:n].rearrange("p (h s) -> p h s", h=len(hs)))
                            groups.append((blocks, [copy]))
                    transpose_groups(groups)
                    compressed_attention(fT, kcT, vc, cmp_add, cmp_keep, branch, probs, probsT, masked)

                    units = []
                    for b, (kT_block, v0) in enumerate(((3, VSLC0), (4, VWIN0))):
                        for pair in range(3):
                            for g in range(NSA_G):
                                units.append(causal_unit(
                                    fT[g * HD:(g + 1) * HD, pair, :], fT[g * HD:(g + 1) * HD, kT_block, :],
                                    [proj[:, t, v0 + g * HD:v0 + (g + 1) * HD] for t in range(TT)],
                                    HD ** -0.5, causal, nsa_weigh(NSA_PAIRS[pair][g], b + 1, branch)))
                    for h in range(MLA_H):
                        units.append(causal_unit(
                            mqT[:, h, :], mkT[:, h, :], [mla_v[:, t, h * HD:(h + 1) * HD] for t in range(TT)],
                            MLA_QK ** -0.5, causal, plain_weigh(NSA_H * HD + h * HD, (0, 1))))
                    attend(units, buffers)
                    retain(fT, decay, gn_gain, scratch, branch)
                    turn_mixed(TT)
                    out_project(first["w_out", layer], hT, (0, 1))
                    normalize_transpose((0, 1), [ln2])
                    feed_forward(first["w_up", layer], first["w_down", layer])

        def causal_unit(qT, kT, vs, scale, causal, weigh):
            return {"rows": [(qT[:, 0:P], kT[:, 0:P], 0, P, vs[0:1]),
                             (qT[:, P:2 * P], kT[:, 0:2 * P], P, 2 * P, vs)],
                    "width": 3 * P, "scale": scale, "mask": causal[:], "weigh": weigh}

        def nsa_weigh(head, b, branch):
            def weigh(step, t, product, inverse):
                gate = branch[:, 0, t * 18 + head * 3 + b:t * 18 + head * 3 + b + 1]
                here = mixed[:, t, head * HD:(head + 1) * HD]
                step(nc.vector.tensor_tensor(inverse, inverse, gate, ALU.mult))
                return nc.vector.scalar_tensor_tensor(out=here, in0=product, scalar=inverse, in1=here,
                                                      op0=ALU.mult, op1=ALU.add)
            return weigh

        def plain_weigh(column, tiles):
            def weigh(step, r, product, inverse):
                return nc.vector.tensor_scalar(mixed[:, tiles[r], column:column + HD], product, inverse, None, ALU.mult)
            return weigh

        def prepare_heads(layer, temps, cosT, sinT, gn_gain, branch, cq_sq, scratch):
            pr = proj[:, 0:TT, :]
            with stage("dve_step", "pool_step", "sums_ready", "rstd_ready", "tanh_ready", "gain_here") as (
                    dve_step, pool_step, sums_ready, rstd_ready, tanh_ready, gain_here), nc.Block() as block:
                @block.sync
                def _(sp):
                    sp.dma_start(gn_gain[:], dram["gn_gain"][layer:layer + 1, :].broadcast_to([P, RET_H * HD])
                                 ).then_inc(gain_here, 16)
                    sp.wait_ge(gain_here, 16)

                @block.vector
                def _(dve):
                    step = InOrder(dve, dve_step)
                    sq = cq_sq[:, :].rearrange("p (t n) -> p t n", t=TT)
                    for t in range(TT):
                        nc.vector.tensor_tensor_reduce(sq[:, t, 0:256], pr[:, t, CQ0:CQ0 + 256], pr[:, t, CQ0:CQ0 + 256],
                                                       1.0 / 256, 0.0, ALU.mult, ALU.add, sums[:, t:t + 1])
                        last = nc.vector.tensor_tensor_reduce(
                            sq[:, t, 256:384], pr[:, t, CKV0:CKV0 + P], pr[:, t, CKV0:CKV0 + P],
                            1.0 / P, 0.0, ALU.mult, ALU.add, sums[:, TT + t:TT + t + 1])
                    last.then_inc(sums_ready, 1)

                    def heads(c0, n, d):
                        return pr[:, :, c0:c0 + n * d].rearrange("p t (h d) -> p t h d", h=n)

                    for view, (a, b) in ((heads(Q0, 12, HD), ROPE_P), (heads(KPE0, 1, MLA_PE), ROPE_M),
                                         (heads(RQ0, 2 * RET_H, HD), ROPE_R)):
                        rope(dve, step, view, cosT[:, :, a:b], sinT[:, :, a:b], b - a, temps)
                    dve.wait_ge(rstd_ready, 1)
                    for t in range(TT):
                        for c0, n, k in ((CQ0, 256, t), (CKV0, P, TT + t)):
                            nc.vector.tensor_scalar(pr[:, t, c0:c0 + n], pr[:, t, c0:c0 + n], rstd[:, k:k + 1],
                                                    None, ALU.mult)
                    dve.wait_ge(tanh_ready, 1)
                    nc.vector.tensor_scalar(branch[:, 0, :], branch[:, 1, :], 0.5, 0.5, ALU.mult, ALU.add)
                    dve.wait_ge(tanh_ready, 2)
                    tanh = scratch_ret()
                    gate = pr[:, :, RG0:RG0 + RET_H * HD]
                    step(nc.vector.tensor_scalar(tanh, tanh, 0.5, 0.5, ALU.mult, ALU.add))
                    nc.vector.tensor_tensor(gate, gate, tanh, ALU.mult)

                @block.gpsimd
                def _(pool):
                    step = InOrder(pool, pool_step)
                    pool.wait_ge(sums_ready, 1)
                    step(nc.gpsimd.tensor_scalar(rstd[:, 0:4], sums[:, 0:4], EPS, None, ALU.add))
                    nc.gpsimd.tensor_tensor(rstd[:, 0:4], rstd[:, 0:4], minus_half[:, 0:4], ALU.pow).then_inc(rstd_ready, 1)

                @block.scalar
                def _(act):
                    nc.scalar.activation(branch[:, 1, :].rearrange("p (t n) -> p t n", t=TT),
                                         pr[:, :, GATE0:GATE0 + 18], ACT.Tanh, scale=0.5).then_inc(tanh_ready, 1)
                    nc.scalar.activation(scratch_ret(), pr[:, :, RG0:RG0 + RET_H * HD], ACT.Tanh,
                                         scale=0.5).then_inc(tanh_ready, 1)

        def scratch_ret():
            return mixed[:, 0:TT, 704:704 + RET_H * HD]

        def transpose_heads(fT, k2, qn, kvn):
            def cols(c0, w):
                return [proj[:, t, c0:c0 + w] for t in range(TT)]

            def to_fT(b):
                return lambda engine, bank: copy_out(engine, fT[:, b:b + 2, :], bank.rearrange("p (b s) -> p b s", b=2))

            order = [Q0, Q0 + P, Q0 + 2 * P, KSLC0, KWIN0, RQ0, RQ0 + P, RK0, RK0 + P]
            groups = [(cols(order[b], P) + cols(order[b + 1], P), [to_fT(b)]) for b in (0, 2, 4, 6)]
            groups.append((cols(order[8], P), [lambda engine, bank: copy_out(engine, fT[:, 8, :], bank[:, 0:SEQ])]))
            groups.append((cols(RQ0 + 2 * P, HD) + cols(RK0 + 2 * P, HD), [
                lambda engine, bank: copy_out(engine, fT[0:HD, 9:11, :],
                                              bank[0:HD, :].rearrange("p (b s) -> p b s", b=2))]))

            def pair_up(kv, g, parity):
                def copy(engine, bank):
                    src = bank[g * HD:(g + 1) * HD, kv * SEQ:(kv + 1) * SEQ].rearrange("p (m e) -> p m e", e=2)
                    return copy_out(engine, k2[parity * HD:(parity + 1) * HD, kv, g, :], src[:, :, parity])
                return copy

            groups.append((cols(KCMP0, P) + cols(VCMP0, P),
                           [pair_up(kv, g, e) for kv in range(2) for g in range(NSA_G) for e in range(2)]))

            def latent(dst, c0, scale):
                return lambda engine, bank: copy_out(engine, dst, bank[:, c0:c0 + SEQ], scale)

            groups.append((cols(CQ0, P) + cols(CQ0 + P, P),
                           [latent(hT[:, 6, 0:SEQ], 0, qn[:, 0:1]), latent(hT[:, 6, SEQ:2 * SEQ], SEQ, qn[:, 1:2])]))
            groups.append((cols(CKV0, P), [latent(hT[:, 7, 0:SEQ], 0, kvn)]))
            transpose_groups(groups)

        def small_products(layer, k2, flat, pos_of, gelu, kcT, vc, mla_q, mla_k, mla_v, cosT, sinT, temps):
            s_w1, s_small = first["cmp_w1", layer], first["small", layer]
            w1 = ring[:, s_w1 % SLOTS, :].rearrange("p (v l h) -> p v l h", v=2, l=CMP_LP)
            small = ring[:, s_small % SLOTS, :]
            NC2 = NSA_G * N_CMP
            with stage("dve_step", "flat_ready", "hidden_ready", "inner_ready", "tanh_ready", "gelu_ready", "mla_ready",
                       "cmp_ready", "act_copied", "pe_done") as (
                    dve_step, flat_ready, hidden_ready, inner_ready, tanh_ready, gelu_ready, mla_ready, cmp_ready,
                    act_copied, pe_done), nc.Block() as block:
                @block.sync
                def _(sp):
                    load_behind(sp, range(s_w1, s_small + 1))

                @block.tensor
                def _(pe):
                    slab_here(pe, s_w1)
                    pe.wait_ge(flat_ready, 1)
                    for kv in range(2):
                        mm = accumulate(banks[:, 0, kv * NC2:(kv + 1) * NC2],
                                        [(w1[:, kv, lp, :], flat[:, kv, lp, :, :].rearrange("p g n -> p (g n)"))
                                         for lp in range(CMP_LP)])
                    mm.then_inc(hidden_ready, 1)
                    pe.wait_ge(hidden_ready, 1)
                    pe.sem_inc(slab_used, 1)
                    slab_here(pe, s_small)
                    for t in range(TT):
                        accumulate(banks[:, 1 + t, 0:480],
                                   [(hT[:, 6, c * SEQ + t * P:c * SEQ + (t + 1) * P],
                                     small[:, UQ0 + c * 480:UQ0 + (c + 1) * 480]) for c in range(2)])
                        for part in range(2):
                            mm = nc.tensor.matmul(banks[:, 3 + 2 * part + t, 0:320], hT[:, 7, t * P:(t + 1) * P],
                                                  small[:, UKV0 + part * 320:UKV0 + (part + 1) * 320],
                                                  start=True, stop=True)
                    mm.then_inc(mla_ready, 1)
                    pe.wait_ge(gelu_ready, 1)
                    for g in range(NSA_G):
                        nc.tensor.matmul(banks[g * HD:(g + 1) * HD, 7, 0:N_CMP], small[:, W2K0:W2K0 + HD],
                                         gelu[:, 3, g * N_CMP:(g + 1) * N_CMP], start=True, stop=True)
                    for g in range(NSA_G):
                        mm = nc.tensor.matmul(banks[0:N_CMP, 0, 128 + g * HD:128 + (g + 1) * HD],
                                              gelu[:, 3, NC2 + g * N_CMP:NC2 + (g + 1) * N_CMP],
                                              small[:, W2V0:W2V0 + HD], start=True, stop=True)
                    mm.then_inc(cmp_ready, 1)
                    pe.wait_ge(cmp_ready, 1)
                    pe.sem_inc(slab_used, 1)

                @block.vector
                def _(dve):
                    step = InOrder(dve, dve_step)
                    for kv in range(2):
                        tok = k2[:, kv, :, :].rearrange("p g (m e) -> p e g m", e=8)
                        for half in range(2):
                            last = nc.vector.tensor_tensor(
                                flat[:, kv, half * 8:half * 8 + 8, :, :], tok[:, :, :, half:half + N_CMP],
                                pos_of[kv][:, half * 8:half * 8 + 8].unsqueeze(2).unsqueeze(3).broadcast_to(
                                    [P, 8, NSA_G, N_CMP]), ALU.add)
                    last.then_inc(flat_ready, 1)
                    dve.wait_ge(hidden_ready, 1)
                    step(nc.vector.tensor_copy(gelu[:, 0, :], banks[:, 0, 0:2 * NC2]))
                    step(nc.vector.tensor_tensor(gelu[:, 1, :], gelu[:, 0, :], gelu[:, 0, :], ALU.mult))
                    step(nc.vector.tensor_scalar(gelu[:, 1, :], gelu[:, 1, :], 0.044715, 1.0, ALU.mult, ALU.add))
                    nc.vector.tensor_tensor(gelu[:, 1, :], gelu[:, 1, :], gelu[:, 0, :], ALU.mult).then_inc(inner_ready, 1)
                    dve.wait_ge(tanh_ready, 1)
                    step(nc.vector.scalar_tensor_tensor(out=gelu[:, 3, :], in0=gelu[:, 2, :], scalar=1.0,
                                                        in1=gelu[:, 0, :], op0=ALU.add, op1=ALU.mult))
                    nc.vector.tensor_scalar(gelu[:, 3, :], gelu[:, 3, :], 0.5, None, ALU.mult).then_inc(gelu_ready, 1)
                    dve.wait_ge(act_copied, 1)
                    q4 = mla_q.rearrange("p t (h d) -> p t h d", h=MLA_H)
                    a, b = ROPE_M
                    rope(dve, step, q4[:, :, :, MLA_NOPE:MLA_QK], cosT[:, :, a:b], sinT[:, :, a:b], b - a, temps)
                    k4 = mla_k.rearrange("p t (h d) -> p t h d", h=MLA_H)
                    for t in range(TT):
                        nc.vector.tensor_copy(k4[:, t, :, MLA_NOPE:MLA_QK],
                                              proj[:, t, KPE0:KPE0 + MLA_PE].unsqueeze(1).broadcast_to(
                                                  [P, MLA_H, MLA_PE]))
                    dve.wait_ge(cmp_ready, 1)
                    nc.vector.tensor_copy(kcT[:], banks[:, 7, 0:N_CMP])
                    nc.vector.tensor_copy(vc[:, :, :].rearrange("p g d -> p (g d)"), banks[0:N_CMP, 0, 128:256])

                @block.scalar
                def _(act):
                    act.wait_ge(inner_ready, 1)
                    nc.scalar.activation(gelu[:, 2, :], gelu[:, 1, :], ACT.Tanh,
                                         scale=float(np.sqrt(2 / np.pi))).then_inc(tanh_ready, 1)
                    act.wait_ge(mla_ready, 1)
                    for t in range(TT):
                        last = nc.scalar.copy(mla_q[:, t, :], banks[:, 1 + t, 0:480])
                    last.then_inc(act_copied, 1)
                    for t in range(TT):
                        nc.scalar.copy(mla_k[:, t, :].rearrange("p (h d) -> p h d", h=MLA_H)[:, :, 0:MLA_NOPE],
                                       banks[:, 3 + t, 0:320].rearrange("p (h d) -> p h d", h=MLA_H))
                        nc.scalar.copy(mla_v[:, t, :], banks[:, 5 + t, 0:320])

        def compressed_attention(fT, kcT, vc, cmp_add, cmp_keep, branch, probs, probsT, masked):
            N = NSA_H * TT
            jobs = [(pair, g, t) for g in range(NSA_G) for pair in range(3) for t in range(TT)]
            NG = N // NSA_G
            s = masked[:, :, :].rearrange("p a b -> p (a b)")[:, 0:N * N_CMP].rearrange("p (j n) -> p j n", j=N)
            p = probs[:, :, :].rearrange("p a b -> p (a b)")[:, 0:N * N_CMP].rearrange("p (j n) -> p j n", j=N)
            pT = hT[0:N_CMP, 6:8, :].rearrange("p a b -> p (a b)")
            pT2 = probsT[0:N_CMP, :, :].rearrange("p a b -> p (a b)")
            s4 = s.rearrange("p (a t) n -> p a t n", t=TT)
            p4 = p.rearrange("p (a t) n -> p a t n", t=TT)

            def table(m):
                return m[:, :].rearrange("p (t n) -> p t n", t=TT)[:, :, 0:N_CMP].unsqueeze(1).broadcast_to(
                    [P, NSA_H, TT, N_CMP])

            def turned(j):
                return (pT[:, j * P:(j + 1) * P] if j < 8 else pT2[:, (j - 8) * P:(j - 7) * P])

            with stage("scores_ready", "dve_step", "shifted", "exp_ready", "probs_ready", "probs_turned", "copied",
                       "values_ready") as (
                    scores_ready, dve_step, shifted, exp_ready, probs_ready, probs_turned, copied,
                    values_ready), nc.Block() as block:
                @block.tensor
                def _(pe):
                    for j, (pair, g, t) in enumerate(jobs):
                        mm = nc.tensor.matmul(banks[:, 7 * g, (j - g * NG) * N_CMP:(j - g * NG + 1) * N_CMP],
                                              fT[g * HD:(g + 1) * HD, pair, t * P:(t + 1) * P],
                                              kcT[g * HD:(g + 1) * HD, :], start=True, stop=True)
                    mm.then_inc(scores_ready, 1)
                    pe.wait_ge(probs_ready, 1)
                    for j in range(N):
                        mm = nc.tensor.transpose(banks[0:N_CMP, 1 + j // 4, (j % 4) * P:(j % 4 + 1) * P],
                                                 p[:, j, :], ident[:])
                    mm.then_inc(probs_turned, 1)
                    pe.wait_ge(copied, 1)
                    for j, (pair, g, t) in enumerate(jobs):
                        mm = nc.tensor.matmul(banks[:, 4 + j // 8, (j % 8) * HD:(j % 8 + 1) * HD],
                                              turned(j), vc[:, g, :], start=True, stop=True)
                    mm.then_inc(values_ready, 1)

                @block.vector
                def _(dve):
                    step = InOrder(dve, dve_step)
                    dve.wait_ge(scores_ready, 1)
                    for g in range(NSA_G):
                        last = nc.vector.tensor_scalar(
                            s[:, g * NG:(g + 1) * NG, :],
                            banks[:, 7 * g, 0:NG * N_CMP].rearrange("p (j n) -> p j n", j=NG), HD ** -0.5, None, ALU.mult)
                    step(last)
                    step(nc.vector.tensor_tensor(s4, s4, table(cmp_add), ALU.add))
                    step(nc.vector.tensor_reduce(sums[:, 0:N], s, AX.X, ALU.max))
                    nc.vector.tensor_tensor(s, s, sums[:, 0:N].unsqueeze(2).broadcast_to([P, N, N_CMP]),
                                            ALU.subtract).then_inc(shifted, 1)
                    dve.wait_ge(exp_ready, 1)
                    step(nc.vector.tensor_tensor(p4, p4, table(cmp_keep), ALU.mult))
                    step(nc.vector.tensor_reduce(sums[:, 0:N], p, AX.X, ALU.add))
                    step(nc.vector.tensor_scalar(sums[:, 0:N], sums[:, 0:N], 1e-30, None, ALU.max))
                    step(nc.vector.reciprocal(sums[:, 16:16 + N], sums[:, 0:N]))
                    nc.vector.tensor_tensor(p, p, sums[:, 16:16 + N].unsqueeze(2).broadcast_to([P, N, N_CMP]),
                                            ALU.mult).then_inc(probs_ready, 1)
                    dve.wait_ge(probs_turned, 1)
                    for b in range(2):
                        nc.vector.tensor_copy(pT[:, b * BANK:(b + 1) * BANK], banks[0:N_CMP, 1 + b, :])
                    nc.vector.tensor_copy(pT2[:, 0:BANK], banks[0:N_CMP, 3, :]).then_inc(copied, 1)
                    dve.wait_ge(values_ready, 1)
                    for j, (pair, g, t) in enumerate(jobs):
                        head = NSA_PAIRS[pair][g]
                        nc.vector.tensor_scalar(mixed[:, t, head * HD:(head + 1) * HD],
                                                banks[:, 4 + j // 8, (j % 8) * HD:(j % 8 + 1) * HD],
                                                branch[:, 0, t * 18 + head * 3:t * 18 + head * 3 + 1], None, ALU.mult)

                @block.scalar
                def _(act):
                    act.wait_ge(shifted, 1)
                    nc.scalar.activation(p, s, ACT.Exp).then_inc(exp_ready, 1)

        def retain(fT, decay, gn_gain, scratch, branch):
            heads = [(fT[0:HD, 5, :], fT[0:HD, 7, :]), (fT[HD:P, 5, :], fT[HD:P, 7, :]),
                     (fT[0:HD, 6, :], fT[0:HD, 8, :]), (fT[HD:P, 6, :], fT[HD:P, 8, :]),
                     (fT[0:HD, 9, :], fT[0:HD, 10, :])]
            faded = scratch.rearrange("p (b c) -> p b c", b=4)
            N = TT * RET_H

            def faded_of(h):
                return faded[:, h, 0:3 * P] if h < 4 else hT[:, 6, 0:3 * P]

            with stage("scores_ready", "faded_ready", "values_ready", "dve_step", "sums_ready", "rstd_ready",
                       "pool_step") as (
                    scores_ready, faded_ready, values_ready, dve_step, sums_ready, rstd_ready, pool_step), \
                    nc.Block() as block:
                @block.tensor
                def _(pe):
                    for h, (qT, kT) in enumerate(heads):
                        nc.tensor.matmul(banks[:, h, 0:SEQ], kT[:, 0:P], qT[:, 0:SEQ], start=True, stop=True)
                        nc.tensor.matmul(banks[:, h, SEQ:SEQ + P], kT[:, P:SEQ], qT[:, P:SEQ],
                                         start=True, stop=True).then_inc(scores_ready, 1)
                    for h in range(RET_H):
                        pe.wait_ge(faded_ready, h + 1)
                        v = [proj[:, t, RV0 + h * HD:RV0 + (h + 1) * HD] for t in range(TT)]
                        f = faded_of(h)
                        nc.tensor.matmul(banks[:, 5, h * HD:(h + 1) * HD], f[:, 0:P], v[0], start=True, stop=True)
                        accumulate(banks[:, 6, h * HD:(h + 1) * HD],
                                   [(f[:, P:2 * P], v[0]), (f[:, 2 * P:3 * P], v[1])]).then_inc(values_ready, 1)

                @block.vector
                def _(dve):
                    step = InOrder(dve, dve_step)
                    for h in range(RET_H):
                        dve.wait_ge(scores_ready, h + 1)
                        nc.vector.tensor_tensor(faded_of(h), banks[:, h, 0:3 * P], decay[:, h, :],
                                                ALU.mult).then_inc(faded_ready, 1)
                    dve.wait_ge(values_ready, RET_H)
                    o3 = mixed[:, 0:TT, 704:1024]
                    for t in range(TT):
                        last = nc.vector.tensor_copy(o3[:, t, :], banks[:, 5 + t, 0:320])
                    step(last)
                    o = o3.rearrange("p t (h d) -> p t h d", h=RET_H)
                    sq = scratch[:, 0:TT * 320].rearrange("p (t h d) -> p t h d", t=TT, h=RET_H)

                    def per_head(a):
                        return a.rearrange("p (t h) -> p t h", t=TT).unsqueeze(3).broadcast_to([P, TT, RET_H, HD])

                    m3 = sums[:, 0:N].rearrange("p (t h) -> p t h", t=TT)
                    step(nc.vector.tensor_reduce(m3, o, AX.X, ALU.add))
                    step(nc.vector.tensor_scalar(sums[:, 0:N], sums[:, 0:N], 1.0 / HD, None, ALU.mult))
                    step(nc.vector.tensor_tensor(o, o, per_head(sums[:, 0:N]), ALU.subtract))
                    step(nc.vector.tensor_tensor(sq, o, o, ALU.mult))
                    nc.vector.tensor_reduce(sums[:, 16:16 + N].rearrange("p (t h) -> p t h", t=TT), sq, AX.X,
                                            ALU.add).then_inc(sums_ready, 1)
                    dve.wait_ge(rstd_ready, 1)
                    step(nc.vector.tensor_tensor(o, o, per_head(rstd[:, 0:N]), ALU.mult))
                    step(nc.vector.tensor_tensor(o3, o3, gn_gain[:].unsqueeze(1).broadcast_to([P, TT, 320]), ALU.mult))
                    nc.vector.tensor_tensor(o3, o3, proj[:, 0:TT, RG0:RG0 + 320], ALU.mult)

                @block.gpsimd
                def _(pool):
                    step = InOrder(pool, pool_step)
                    pool.wait_ge(sums_ready, 1)
                    step(nc.gpsimd.tensor_scalar(rstd[:, 0:N], sums[:, 16:16 + N], 1.0 / HD, EPS, ALU.mult, ALU.add))
                    nc.gpsimd.tensor_tensor(rstd[:, 0:N], rstd[:, 0:N], minus_half[:, 0:N], ALU.pow).then_inc(rstd_ready, 1)

        def turn_mixed(T):
            per = 4 // T
            groups = []
            for c in range(0, KC, per):
                blocks = [mixed[:, t, k * P:(k + 1) * P] for k in range(c, c + per) for t in range(T)]

                def copy(engine, bank, c=c):
                    return copy_out(engine, hT[:, c:c + per, 0:T * P], bank.rearrange("p (k s) -> p k s", k=per))
                groups.append((blocks, [copy]))
            transpose_groups(groups)

        def feed_forward(up0, down0):
            uT = proj[:, :, :].rearrange("p a b -> p (a b)")[:, 0:(DFF // P) * SEQ].rearrange(
                "p (f s) -> p f s", s=SEQ)
            FT = DFF // P
            with stage("hidden_ready", "rectified", "squared", "down_ready", "pe_step") as (
                    hidden_ready, rectified, squared, down_ready, pe_step), nc.Block() as block:
                relu = [hT[:, 4 + i, SEQ:2 * SEQ] for i in range(4)]

                @block.sync
                def _(sp):
                    load_behind(sp, range(up0, down0 + 8))

                @block.tensor
                def _(pe):
                    for f in range(FT):
                        s = up0 + f // 4
                        w = ring[:, s % SLOTS, :].rearrange("p (k n) -> p k n", k=KC)
                        if f % 4 == 0:
                            slab_here(pe, s)
                        if f >= 4:
                            pe.wait_ge(rectified, f - 3)
                        mm = accumulate(banks[:, f % 4, 0:SEQ],
                                        [(w[:, k, (f % 4) * P:(f % 4 + 1) * P], hT[:, k, 0:SEQ]) for k in range(KC)])
                        mm.then_inc(hidden_ready, 1)
                        if f % 4 == 3:
                            pe.wait_ge(hidden_ready, f + 1)
                            pe.sem_inc(slab_used, 1)
                    for f in range(FT):
                        s = down0 + f // 4
                        w = ring[:, s % SLOTS, :].rearrange("p (k n) -> p k n", k=4)
                        if f % 4 == 0:
                            slab_here(pe, s)
                        pe.wait_ge(squared, f + 1)
                        for t in range(TT):
                            for n in range(2):
                                mm = nc.tensor.matmul(banks[:, 4 + 2 * t + n, :], uT[:, f, t * P:(t + 1) * P],
                                                      w[:, f % 4, n * BANK:(n + 1) * BANK],
                                                      start=(f == 0), stop=(f == FT - 1))
                        if f % 4 == 3:
                            mm.then_inc(pe_step, 1)
                            pe.wait_ge(pe_step, f // 4 + 1)
                            pe.sem_inc(slab_used, 1)

                @block.scalar
                def _(act):
                    for f in range(FT):
                        act.wait_ge(hidden_ready, f + 1)
                        if f >= 4:
                            act.wait_ge(squared, f - 3)
                        nc.scalar.activation(relu[f % 4], banks[:, f % 4, 0:SEQ], ACT.Relu).then_inc(rectified, 1)

                @block.vector
                def _(dve):
                    for f in range(FT):
                        dve.wait_ge(rectified, f + 1)
                        nc.vector.tensor_tensor(uT[:, f, :], relu[f % 4], relu[f % 4], ALU.mult).then_inc(squared, 1)
                    dve.wait_ge(pe_step, FT // 4)
                    for t in range(TT):
                        for n in range(2):
                            here = x[:, t, n * BANK:(n + 1) * BANK]
                            nc.vector.tensor_tensor(here, banks[:, 4 + 2 * t + n, :], here, ALU.add)

        def final_norm(gain_dram, store):
            with stage("gain_here", "squares_summed", "pool_step", "rstd_ready", "normed") as (
                    gain_here, squares_summed, pool_step, rstd_ready, normed), nc.Block() as block:
                gain = proj[:, 0, 0:D]

                @block.sync
                def _(sp):
                    sp.dma_start(gain, gain_dram.broadcast_to([P, D])).then_inc(gain_here, 16)
                    if store:
                        for t in range(TT):
                            sp.wait_ge(normed, t + 1)
                            sp.dma_start(out[0, t * P:(t + 1) * P, :], x[:, t, :]).then_inc(stored, 16)
                        sp.wait_ge(stored, 16 * TT)

                @block.vector
                def _(dve):
                    for t in range(TT):
                        nc.vector.tensor_tensor_reduce(mixed[:, t, :], x[:, t, :], x[:, t, :], 1.0, 0.0, ALU.mult,
                                                       ALU.add, sums[:, t:t + 1]).then_inc(squares_summed, 1)
                    dve.wait_ge(rstd_ready, 1)
                    dve.wait_ge(gain_here, 16)
                    for t in range(TT):
                        nc.vector.scalar_tensor_tensor(out=x[:, t, :], in0=x[:, t, :], scalar=rstd[:, t:t + 1],
                                                       in1=gain, op0=ALU.mult, op1=ALU.mult).then_inc(normed, 1)

                @block.gpsimd
                def _(pool):
                    step = InOrder(pool, pool_step)
                    pool.wait_ge(squares_summed, TT)
                    step(nc.gpsimd.tensor_scalar(rstd[:, 0:TT], sums[:, 0:TT], 1.0 / D, EPS, ALU.mult, ALU.add))
                    nc.gpsimd.tensor_tensor(rstd[:, 0:TT], rstd[:, 0:TT], minus_half[:, 0:TT],
                                            ALU.pow).then_inc(rstd_ready, 1)

        def second_block():
            with ExitStack() as local:
                def sb(name, shape, dt=F32):
                    return local.enter_context(nc.sbuf_tensor(name, shape, dt))

                NF = 24 + 8 + 4 + 24 + 8
                feats2 = sb("feats2", [P, NF])
                cond = sb("cond", [P, KC, 2])
                cond_t = sb("cond_t", [P, KC, 2])
                ada = sb("ada", [P, 24, 2])
                scales = sb("scales", [P, 2, KC])
                gate_rows = sb("gate_rows", [P, 2, D])
                conv_w = sb("conv_w", [P, 4, CONV_W])
                rows = sb("rows", [P, 2 * BANK + 2 * HD])
                axial = sb("axial", [P, 2, TT, HD // 2])
                wf = sb("wf", [P, C_GROUPS, P])
                dft_c = sb("dft_c", [P, 2 * P])
                dft_t = sb("dft_t", [P, 2, TT, SEQ])
                onehot = sb("onehot", [N_DC, 2 * GRID_W - 1])
                rpb = sb("rpb", [N_DC, D_HEADS * N_DR])
                col_mask = sb("col_mask", [P, GRID_W])
                wide = sb("wide", [P, 4608])
                probs2 = sb("probs2", [P, 2, BANK])
                nmax2, total2, inverse2 = (sb(n, [P, 2, 2]) for n in ("nmax2", "total2", "inverse2"))
                b_ab, g_ab, conv_b, b_cd, g_cd = (feats2[:, a:b] for a, b in (
                    (0, 24), (24, 32), (32, 36), (36, 60), (60, 68)))

                def adapt(slab0, bias, gain, n_gates, load=None):
                    with stage("dve_step", "tanh_ready", "cond_ready", "product_ready", "ada_ready", "rows_ready") as (
                            dve_step, tanh_ready, cond_ready, product_ready, ada_ready, rows_ready), nc.Block() as block:
                        @block.sync
                        def _(sp):
                            if load is not None:
                                load(sp)
                                sp.wait_ge(loaded, n_loaded[0])
                            load_behind(sp, range(slab0, slab0 + 6))

                        @block.scalar
                        def _(act):
                            if load is not None:
                                act.wait_ge(loaded, n_loaded[0])
                                nc.scalar.activation(cond_t[:], cond[:], ACT.Tanh, scale=0.5).then_inc(tanh_ready, 1)

                        @block.tensor
                        def _(pe):
                            if load is not None:
                                pe.wait_ge(cond_ready, 1)
                            for s in range(6):
                                w = ring[:, (slab0 + s) % SLOTS, :].rearrange("p (k n) -> p k n", k=KC)
                                slab_here(pe, slab0 + s)
                                for j in range(4):
                                    f = 4 * s + j
                                    mm = accumulate(banks[:, 0, 2 * f:2 * f + 2],
                                                    [(w[:, k, j * P:(j + 1) * P], cond[:, k, :]) for k in range(KC)])
                                mm.then_inc(product_ready, 1)
                                pe.wait_ge(product_ready, s + 1)
                                pe.sem_inc(slab_used, 1)
                            pe.wait_ge(ada_ready, 1)
                            for v in range(n_gates):
                                for c in range(KC):
                                    mm = nc.tensor.matmul(banks[:, 1 + 2 * v + c // 4, (c % 4) * P:(c % 4 + 1) * P],
                                                          ada[:, 16 + c, v:v + 1].broadcast_to([P, P]), ident[:],
                                                          start=True, stop=True)
                            mm.then_inc(rows_ready, 1)

                        @block.vector
                        def _(dve):
                            step = InOrder(dve, dve_step)
                            if load is not None:
                                dve.wait_ge(tanh_ready, 1)
                                step(nc.vector.tensor_scalar(cond_t[:], cond_t[:], 0.5, 0.5, ALU.mult, ALU.add))
                                nc.vector.tensor_tensor(cond[:], cond[:], cond_t[:], ALU.mult).then_inc(cond_ready, 1)
                            dve.wait_ge(product_ready, 6)
                            nc.vector.tensor_tensor(ada[:], banks[:, 0, 0:48].rearrange("p (f v) -> p f v", v=2),
                                                    bias.unsqueeze(2).broadcast_to([P, 24, 2]),
                                                    ALU.add).then_inc(ada_ready, 1)
                            dve.wait_ge(ada_ready, 1)
                            for v in range(2):
                                nc.vector.scalar_tensor_tensor(out=scales[:, v, :], in0=ada[:, 8:16, v], scalar=1.0,
                                                               in1=gain, op0=ALU.add, op1=ALU.mult)
                            dve.wait_ge(rows_ready, 1)
                            for v in range(n_gates):
                                for half in range(2):
                                    nc.vector.tensor_copy(gate_rows[:, v, half * BANK:(half + 1) * BANK],
                                                          banks[:, 1 + 2 * v + half, :])

                def load_tables(sp):
                    for dst, name in ((cond, "cond"), (feats2, "feats2"), (conv_w, "conv_w"), (axial, "axial"),
                                      (wf, "w_fourier"), (dft_c, "dft_c"), (dft_t, "dft_t"), (onehot, "onehot"),
                                      (rpb, "rpb"), (col_mask, "col_mask")):
                        load_const(sp, dst[:], dram[name])
                    load_const(sp, rows[:], dram["rows"].broadcast_to([P, 2 * BANK + 2 * HD]))

                def adaln_scales():
                    return [scales[:, v, :] for v in range(2)], [ada[:, 0:8, v] for v in range(2)]

                adapt(first["ab_ada"], b_ab, g_ab, 2, load_tables)
                sc, sh = adaln_scales()
                normalize_transpose((0, 1, 2, 3), sc, sh)
                project_and_convolve(first["ab_in"], wide, conv_w, conv_b)
                finish_conv_and_heads(rows, axial)
                qT, kT = hT[:, 0:4, :], hT[:, 4, :]
                groups = []
                for i in range(5):
                    c0 = AB_Q0 + i * P
                    groups.append(([proj[:, t, c0:c0 + P] for t in range(4)],
                                   [lambda engine, bank, i=i: copy_out(engine, hT[:, i, :], bank)]))
                transpose_groups(groups)
                units = []
                for h in range(B_HEADS):
                    kv, i = h // 4, h % 4
                    lanes = slice(kv * HD, (kv + 1) * HD)
                    vs = [proj[:, t, AB_V0 + kv * HD:AB_V0 + (kv + 1) * HD] for t in range(4)]
                    for t in range(TT):
                        units.append({"rows": [(qT[lanes, i, t * P:(t + 1) * P], kT[lanes, :], 0, BANK, vs)],
                                      "width": BANK, "mask": None, "weigh": plain_weigh(BANK + h * HD, (t,))})
                    units.append({"rows": [(qT[lanes, i, t * P:(t + 1) * P], kT[lanes, SEQ:2 * SEQ], (t - 2) * SEQ,
                                            SEQ, vs[2:4]) for t in (2, 3)],
                                  "width": BANK, "mask": None, "weigh": plain_weigh(BANK + h * HD, (2, 3))})
                attend(units, (probs2, hT[:, 5:7, :], nmax2, total2, inverse2))
                gate_by_z(4, AB_Z0)
                turn_mixed(4)
                out_project(first["ab_out"], hT, (0, 1, 2, 3), [gate_rows[:, v, :] for v in range(2)])

                adapt(first["cd_ada"], b_cd, g_cd, 1)
                sc, sh = adaln_scales()
                normalize_transpose((0, 1, 2, 3), sc, sh)
                both, own = (0, 1, 2, 3), (0, 1)
                project(first["cd_in"], [BANK] * 6, [own, own, both, both, own, own], proj)
                kT = hT[:, 0:4, :]
                qT = hT[:, 4:6, :].rearrange("p a (b s) -> p (a b) s", b=2)
                fgT = hT[:, 6:8, :].rearrange("p a (b s) -> p (a b) s", b=2)
                groups = []
                for c0, dst, scale in ((CD_Q0, qT, HD ** -0.5), (CD_F0, fgT, None)):
                    for i in (0, 2):
                        groups.append(([proj[:, t, c0 + k * P:c0 + (k + 1) * P] for k in (i, i + 1) for t in own],
                                       [lambda engine, bank, dst=dst, i=i, scale=scale: copy_out(
                                           engine, dst[:, i:i + 2, :], bank.rearrange("p (k s) -> p k s", k=2), scale)]))
                for i in range(4):
                    groups.append(([proj[:, t, CD_K0 + i * P:CD_K0 + (i + 1) * P] for t in both],
                                   [lambda engine, bank, i=i: copy_out(engine, kT[:, i, :], bank)]))
                transpose_groups(groups)
                fourier(fgT, wf, dft_c, dft_t)
                bias = wide[:, 0:4096].rearrange("p (t h r c) -> p t h r c", t=TT, h=D_HEADS, r=ROWS)
                relative_bias(bias, onehot, rpb, col_mask)
                units = []
                for h in range(D_HEADS):
                    lanes = slice((h % 2) * HD, (h % 2 + 1) * HD)
                    vs = [proj[:, t, CD_V0 + h * HD:CD_V0 + (h + 1) * HD] for t in both]
                    for t in own:
                        units.append({"rows": [(qT[lanes, h // 2, t * P:(t + 1) * P], kT[lanes, h // 2, :], 0, BANK, vs)],
                                      "width": BANK, "scale": 1.0,
                                      "mask": bias[:, t, h, :, :].rearrange("p r c -> p (r c)"),
                                      "weigh": plain_weigh(BANK + h * HD, (t,))})
                attend(units, (probs2, hT[:, 6:8, :], nmax2, total2, inverse2))
                gate_by_z(2, CD_Z0)
                turn_mixed(2)
                out_project(first["cd_out"], hT, own, [gate_rows[:, 0, :]])

        def project_and_convolve(slab0, wide, conv_w, conv_b):
            span = SEQ + 2 * CONV_PAD
            uT = wide[:, 0:8 * span].rearrange("p (c s n) -> p c s n", c=4, s=2)
            cT = wide[:, 8 * span:8 * span + 2048].rearrange("p (c s n) -> p c s n", c=4, s=2)
            cT_flat = wide[:, 8 * span:8 * span + 2048].rearrange("p (c n) -> p c n", c=4)
            n_slabs = -(-AB_N // BANK)
            widths = [min(BANK, AB_N - s * BANK) for s in range(n_slabs)]
            units = [(s, t) for s in range(n_slabs) for t in range(4)]
            TURN_AT = 12
            with stage("product_ready", "evacuated", "tanh_ready", "glu_ready", "glu_turned", "uT_ready", "zeroed",
                       "tap_done") as (
                    product_ready, evacuated, tanh_ready, glu_ready, glu_turned, uT_ready, zeroed,
                    tap_done), nc.Block() as block:
                @block.sync
                def _(sp):
                    load_behind(sp, range(slab0, slab0 + n_slabs))

                @block.gpsimd
                def _(pool):
                    nc.gpsimd.memset(uT, 0.0).then_inc(zeroed, 1)

                @block.tensor
                def _(pe):
                    for u, (s, t) in enumerate(units):
                        if u == TURN_AT:
                            pe.wait_ge(glu_ready, 4)
                            for c in range(4):
                                for tile in range(4):
                                    mm = nc.tensor.transpose(banks[:, 4 + c, tile * P:(tile + 1) * P],
                                                             mixed[:, tile, BANK + c * P:BANK + (c + 1) * P], ident[:])
                                mm.then_inc(glu_turned, 1)
                        w = ring[:, (slab0 + s) % SLOTS, :].rearrange("p (k n) -> p k n", k=KC)
                        if t == 0:
                            slab_here(pe, slab0 + s)
                        if u >= 4:
                            pe.wait_ge(evacuated, u - 3)
                        mm = accumulate(banks[:, u % 4, 0:widths[s]],
                                        [(hT[:, k, t * P:(t + 1) * P], w[:, k, 0:widths[s]]) for k in range(KC)])
                        mm.then_inc(product_ready, 1)
                        if t == 3:
                            pe.wait_ge(product_ready, u + 1)
                            pe.sem_inc(slab_used, 1)
                    pe.wait_ge(tap_done, 4 * CONV_W)
                    for t in range(4):
                        for c in range(4):
                            nc.tensor.transpose(banks[:, 4 + t, c * P:(c + 1) * P],
                                                cT_flat[:, c, t * P:(t + 1) * P], ident[:])

                @block.scalar
                def _(act):
                    for u, (s, t) in enumerate(units):
                        if u == TURN_AT:
                            act.wait_ge(zeroed, 1)
                            for c in range(4):
                                act.wait_ge(glu_turned, c + 1)
                                nc.scalar.activation(uT[:, c, :, CONV_PAD:CONV_PAD + SEQ],
                                                     banks[:, 4 + c, :].rearrange("p (s n) -> p s n", s=2),
                                                     ACT.Copy, scale=0.5).then_inc(uT_ready, 1)
                        act.wait_ge(product_ready, u + 1)
                        nc.scalar.copy(proj[:, t, s * BANK:s * BANK + widths[s]],
                                       banks[:, u % 4, 0:widths[s]]).then_inc(evacuated, 1)
                        if s == 1:
                            act.wait_ge(evacuated, u + 1)
                            nc.scalar.activation(mixed[:, t, 0:BANK], proj[:, t, AB_GATE0:AB_GATE0 + BANK], ACT.Tanh,
                                                 scale=0.5).then_inc(tanh_ready, 1)

                @block.vector
                def _(dve):
                    for t in range(4):
                        dve.wait_ge(tanh_ready, t + 1)
                        dve.wait_ge(evacuated, 5 + t)
                        nc.vector.scalar_tensor_tensor(out=mixed[:, t, BANK:D], in0=mixed[:, t, 0:BANK], scalar=1.0,
                                                       in1=proj[:, t, 0:BANK], op0=ALU.add,
                                                       op1=ALU.mult).then_inc(glu_ready, 1)
                    for j in range(CONV_W):
                        for c in range(4):
                            tap = uT[:, c, :, j:j + SEQ]
                            if j == 0:
                                dve.wait_ge(uT_ready, c + 1)
                                ins = nc.vector.tensor_scalar(cT[:, c, :, :], tap, conv_w[:, c, 0:1], conv_b[:, c:c + 1],
                                                              ALU.mult, ALU.add)
                            else:
                                dve.wait_ge(tap_done, 4 * (j - 1) + c + 1)
                                ins = nc.vector.scalar_tensor_tensor(out=cT[:, c, :, :], in0=tap,
                                                                     scalar=conv_w[:, c, j:j + 1], in1=cT[:, c, :, :],
                                                                     op0=ALU.mult, op1=ALU.add)
                            ins.then_inc(tap_done, 1)

        def finish_conv_and_heads(rows, axial):
            ln_g, ln_b = rows[:, 0:BANK], rows[:, BANK:2 * BANK]
            qn, kn = rows[:, 2 * BANK:2 * BANK + HD], rows[:, 2 * BANK + HD:2 * BANK + 2 * HD]
            flat = hT[:, :, :].rearrange("p a b -> p (a b)")
            y = mixed[:, :, 0:BANK]
            H = B_HEADS + B_KV
            qk = proj[:, :, AB_Q0:AB_Q0 + H * HD].rearrange("p t (h d) -> p t h d", h=H)
            sq = flat[:, 0:4 * H * HD].rearrange("p (t h d) -> p t h d", t=4, h=H)
            temps = [flat[:, i * 640:(i + 1) * 640] for i in range(4)]
            stats, mv = sums[:, 48:72], sums[:, 72:80]
            sig = mixed[:, :, BANK:D]
            with stage("dve_step", "pool_step", "stats_ready", "sums_ready", "rstd_ready", "normed", "tanh_ready") as (
                    dve_step, pool_step, stats_ready, sums_ready, rstd_ready, normed, tanh_ready), \
                    nc.Block() as block:
                @block.vector
                def _(dve):
                    step = InOrder(dve, dve_step)
                    for t in range(4):
                        last = nc.vector.bn_stats(stats[:, 6 * t:6 * t + 6], banks[:, 4 + t, :])
                    step(last)
                    for t in range(4):
                        last = nc.vector.bn_aggr(mv[:, 2 * t:2 * t + 2], stats[:, 6 * t:6 * t + 6])
                    last.then_inc(stats_ready, 1)
                    step(nc.vector.tensor_tensor(sq, qk, qk, ALU.mult))
                    nc.vector.tensor_reduce(sums[:, 0:40].rearrange("p (t h) -> p t h", t=4), sq, AX.X,
                                            ALU.add).then_inc(sums_ready, 1)
                    dve.wait_ge(rstd_ready, 1)
                    for t in range(4):
                        last = nc.vector.tensor_scalar(y[:, t, :], banks[:, 4 + t, :], mv[:, 2 * t:2 * t + 1],
                                                       rstd[:, 48 + t:49 + t], ALU.subtract, ALU.mult)
                    step(last)
                    step(nc.vector.tensor_tensor(y, y, ln_g.unsqueeze(1).broadcast_to([P, 4, BANK]), ALU.mult))
                    nc.vector.tensor_tensor(y, y, ln_b.unsqueeze(1).broadcast_to([P, 4, BANK]),
                                            ALU.add).then_inc(normed, 1)
                    dve.wait_ge(rstd_ready, 2)
                    step(nc.vector.tensor_tensor(qk, qk, rstd[:, 0:40].rearrange("p (t h) -> p t h", t=4).unsqueeze(
                        3).broadcast_to([P, 4, H, HD]), ALU.mult))
                    nc.vector.tensor_tensor(qk[:, :, 0:B_HEADS, :], qk[:, :, 0:B_HEADS, :],
                                            qn.unsqueeze(1).unsqueeze(1).broadcast_to([P, 4, B_HEADS, HD]), ALU.mult)
                    step(nc.vector.tensor_tensor(qk[:, :, B_HEADS:H, :], qk[:, :, B_HEADS:H, :],
                                                 kn.unsqueeze(1).unsqueeze(1).broadcast_to([P, 4, B_KV, HD]), ALU.mult))
                    rope(dve, step, qk[:, 0:TT, :, :], axial[:, 0, :, :], axial[:, 1, :, :], HD // 2, temps)
                    nc.vector.tensor_scalar(qk[:, :, 0:B_HEADS, :], qk[:, :, 0:B_HEADS, :], HD ** -0.5, None, ALU.mult)
                    dve.wait_ge(tanh_ready, 1)
                    step(nc.vector.tensor_scalar(sig, sig, 0.5, 0.5, ALU.mult, ALU.add))
                    nc.vector.tensor_tensor(y, y, sig, ALU.mult)

                @block.scalar
                def _(act):
                    act.wait_ge(normed, 1)
                    nc.scalar.activation(sig, y, ACT.Tanh, scale=0.5).then_inc(tanh_ready, 1)

                @block.gpsimd
                def _(pool):
                    step = InOrder(pool, pool_step)
                    pool.wait_ge(stats_ready, 1)
                    step(nc.gpsimd.tensor_scalar(rstd[:, 48:52], mv.rearrange("p (t v) -> p t v", v=2)[:, :, 1],
                                                 EPS, None, ALU.add))
                    nc.gpsimd.tensor_tensor(rstd[:, 48:52], rstd[:, 48:52], minus_half[:, 0:4],
                                            ALU.pow).then_inc(rstd_ready, 1)
                    pool.wait_ge(sums_ready, 1)
                    step(nc.gpsimd.tensor_scalar(rstd[:, 0:40], sums[:, 0:40], 1.0 / HD, EPS, ALU.mult, ALU.add))
                    nc.gpsimd.tensor_tensor(rstd[:, 0:40], rstd[:, 0:40], minus_half[:, 0:40],
                                            ALU.pow).then_inc(rstd_ready, 1)

        def gate_by_z(T, z0):
            with stage("tanh_ready", "dve_step") as (tanh_ready, dve_step), nc.Block() as block:
                @block.scalar
                def _(act):
                    for t in range(T):
                        nc.scalar.activation(hT[:, 2 * t:2 * t + 2, :].rearrange("p a b -> p (a b)"),
                                             proj[:, t, z0:z0 + D], ACT.Tanh, scale=0.5).then_inc(tanh_ready, 1)

                @block.vector
                def _(dve):
                    step = InOrder(dve, dve_step)
                    for t in range(T):
                        z = proj[:, t, z0:z0 + D]
                        dve.wait_ge(tanh_ready, t + 1)
                        step(nc.vector.scalar_tensor_tensor(
                            out=z, in0=hT[:, 2 * t:2 * t + 2, :].rearrange("p a b -> p (a b)"), scalar=1.0, in1=z,
                            op0=ALU.add, op1=ALU.mult))
                        nc.vector.scalar_tensor_tensor(out=mixed[:, t, :], in0=z, scalar=0.5, in1=mixed[:, t, :],
                                                       op0=ALU.mult, op1=ALU.mult)

        def fourier(fgT, wf, dft_c, dft_t):
            def mixed_channels(g):
                return proj[:, 2 + g // 2, CD_V0 + BANK + (g % 2) * BANK:CD_V0 + BANK + (g % 2 + 1) * BANK].rearrange(
                    "p (t n) -> p t n", t=TT)

            frT = proj[:, 2, 0:C_GROUPS * SEQ].rearrange("p (g s) -> p g s", g=C_GROUPS)
            with stage("channels_ready", "channels_copied", "tokens_ready", "tokens_copied", "product_ready") as (
                    channels_ready, channels_copied, tokens_ready, tokens_copied, product_ready), nc.Block() as block:
                @block.tensor
                def _(pe):
                    for g in range(C_GROUPS):
                        for t in range(TT):
                            mm = nc.tensor.matmul(banks[:, g, t * SEQ:(t + 1) * SEQ], fgT[:, g, t * P:(t + 1) * P],
                                                  dft_c[:], start=True, stop=True)
                        mm.then_inc(channels_ready, 1)
                    for g in range(C_GROUPS):
                        pe.wait_ge(channels_copied, g + 1)
                        a = mixed_channels(g)
                        accumulate(banks[:, 4 + g // 2, (g % 2) * SEQ:(g % 2 + 1) * SEQ],
                                   [(a[:, t, v * P:(v + 1) * P], dft_t[:, v, t, :]) for t in range(TT)
                                    for v in range(2)]).then_inc(tokens_ready, 1)
                    for g in range(C_GROUPS):
                        pe.wait_ge(tokens_copied, g // 2 + 1)
                        for t in range(TT):
                            mm = nc.tensor.matmul(banks[:, 6 + t, g * P:(g + 1) * P], frT[:, g, t * P:(t + 1) * P],
                                                  wf[:, g, :], start=True, stop=True)
                    mm.then_inc(product_ready, 1)

                @block.vector
                def _(dve):
                    for g in range(C_GROUPS):
                        dve.wait_ge(channels_ready, g + 1)
                        nc.vector.tensor_copy(mixed_channels(g), banks[:, g, :].rearrange(
                            "p (t n) -> p t n", t=TT)).then_inc(channels_copied, 1)
                    dve.wait_ge(product_ready, 1)
                    for t in range(TT):
                        nc.vector.tensor_copy(mixed[:, t, 0:BANK], banks[:, 6 + t, :])

                @block.scalar
                def _(act):
                    for b in range(C_GROUPS // 2):
                        act.wait_ge(tokens_ready, 2 * b + 2)
                        nc.scalar.copy(frT[:, 2 * b:2 * b + 2, :],
                                       banks[:, 4 + b, :].rearrange("p (g s) -> p g s", g=2)).then_inc(tokens_copied, 1)

        def relative_bias(bias, onehot, rpb, col_mask):
            with stage("spread",) as (spread,), nc.Block() as block:
                @block.tensor
                def _(pe):
                    for ck in range(GRID_W):
                        shift = GRID_W - 1 - ck
                        for half in range(2):
                            mm = nc.tensor.matmul(
                                banks[half * HD:(half + 1) * HD, ck // 8, (ck % 8) * 56:(ck % 8 + 1) * 56],
                                onehot[:, shift:shift + GRID_W], rpb[:], start=True, stop=True)
                    mm.then_inc(spread, 1)

                @block.vector
                def _(dve):
                    dve.wait_ge(spread, 1)
                    table = banks[:, :, 0:8 * 56].rearrange("p b (j h r) -> p r h b j", j=8, h=D_HEADS)
                    for t in range(TT):
                        for rho in range(2):
                            lanes = slice(rho * HD, (rho + 1) * HD)
                            mask = col_mask[lanes, :].rearrange("p (b j) -> p b j", j=8).unsqueeze(1).broadcast_to(
                                [HD, D_HEADS, 8, 8])
                            for rk in range(ROWS):
                                nc.vector.tensor_tensor(
                                    bias[lanes, t, :, rk, :].rearrange("p h (b j) -> p h b j", j=8),
                                    table[lanes, rk - (2 * t + rho) + 3, :, :, :], mask, ALU.add)

        first_block()
        final_norm(dram["final_gain"], False)
        second_block()
        final_norm(dram["final_norm_g"], True)


def _slabs(w):
    w = np.asarray(w)
    short = -w.shape[-1] % BANK
    w = np.concatenate([w, np.zeros(w.shape[:-1] + (short,), w.dtype)], axis=-1)
    lead = w.shape[:-2]
    w = w.reshape(-1, KC, P, w.shape[-1] // BANK, BANK).transpose(0, 3, 2, 1, 4)
    return np.ascontiguousarray(w.reshape(-1, P, KC * BANK))


def _features(v):
    v = np.asarray(v)
    v = v.reshape(v.shape[:-1] + (-1, P))
    return np.moveaxis(v, -1, 0)


def _w_in_order():
    starts = dict(q=0, kc=384, vc=512, ks=640, vs=768, kw=896, vw=1024)
    cols = [c for pair in NSA_PAIRS for h in pair for c in range(h * HD, (h + 1) * HD)]
    for name in ("kc", "ks", "kw", "vc", "vs", "vw"):
        cols += list(range(starts[name], starts[name] + NSA_G * HD))
    return np.array(cols + list(range(GATE0, N_IN)))


def _ukv_order():
    per = MLA_NOPE + HD
    return np.array([h * per + part * MLA_NOPE + d for part in range(2) for h in range(MLA_H) for d in range(HD)])


def _tables():
    i = np.arange(P)
    q = np.arange(SEQ)
    t = {}
    t["ident"] = np.eye(P)
    inv = [1.0 / theta ** (np.arange(0, dim, 2, dtype=np.float32) / np.float32(dim))
           for theta, dim in ((np.float32(500000.0), 16), (np.float32(500000.0), 32), (np.float32(10000.0), 64))]
    t["freqs"] = np.tile(np.concatenate(inv), (P, 1))
    tri = np.where(i[:, None] >= i[None, :], 0.0, NEG)
    t["causal"] = np.concatenate([tri, np.zeros((P, P)), tri], axis=1)
    gamma = 1.0 - 2.0 ** (-5.0 - np.arange(RET_H))
    gap = (q[None, :] - i[:, None]).astype(np.float64)
    fade = np.where(gap >= 0, gamma[:, None, None] ** np.maximum(gap, 0)[None], 0.0) * HD ** -0.5
    t["decay"] = np.concatenate([fade, fade[:, :, 0:P]], axis=2).transpose(1, 0, 2)
    keep = np.zeros((P, TT, 16))
    for tile in range(TT):
        keep[:, tile, 0:N_CMP] = (np.arange(N_CMP)[None, :] * 16 + 31) <= (tile * P + i)[:, None]
    t["cmp_keep"] = keep.reshape(P, TT * 16)
    t["cmp_add"] = np.where(keep > 0, 0.0, NEG).reshape(P, TT * 16)
    freq = np.float32(10000.0) ** (-np.arange(HD // 4, dtype=np.float32) / np.float32(HD // 4))
    ang = np.concatenate([(q // GRID_W)[:, None] * freq, (q % GRID_W)[:, None] * freq], axis=1)
    t["axial"] = np.stack([np.cos(ang), np.sin(ang)]).reshape(2, TT, P, HD // 2).transpose(2, 0, 1, 3)
    w = 2 * np.pi * np.outer(i, i) / P
    t["dft_c"] = np.concatenate([np.cos(w), np.sin(w)], axis=1)
    w = 2 * np.pi * (np.outer(q, q) % SEQ) / SEQ
    t["dft_t"] = (np.stack([np.cos(w), -np.sin(w)]) / np.sqrt(SEQ * P)).reshape(2, TT, P, SEQ).transpose(2, 0, 1, 3)
    t["onehot"] = (np.arange(2 * GRID_W - 1)[None, :] == (GRID_W - 1 + 15 - np.arange(N_DC))[:, None])
    col = np.arange(GRID_W)
    start = np.clip(col - 8, 0, GRID_W - 16)
    ok = (col[None, :] >= start[:, None]) & (col[None, :] < start[:, None] + 16)
    t["col_mask"] = np.tile(np.where(ok, 0.0, NEG), (2, 1))
    return {k: np.ascontiguousarray(v, dtype=np.float32) for k, v in t.items()}


def _ab_order():
    split = np.concatenate([np.arange(0, HD, 2), np.arange(1, HD, 2)])
    cols = list(range(AB_Q0))
    for i in range(B_HEADS // 2):
        for h in (i, i + B_HEADS // 2):
            cols += list(AB_Q0 + h * HD + split)
    for kv in range(B_KV):
        cols += list(AB_K0 + kv * HD + split)
    return np.array(cols + list(range(AB_V0, AB_N))), split


def _layout(a):
    cat = np.concatenate
    d = _tables()
    L = DEPTH
    tiles = lambda v: np.ascontiguousarray(np.asarray(v).reshape(-1, P, D).transpose(1, 0, 2))
    d["x"] = tiles(a["x"])
    d["ctx"] = tiles(a["ctx_2"])
    d["positions"] = np.ascontiguousarray(np.asarray(a["positions"]).reshape(TT, P).T)
    d["w_in"] = _slabs(np.asarray(a["w_in"])[:, :, _w_in_order()])
    w1 = [np.asarray(a[n]).reshape(L, CMP_LP, P, P).transpose(0, 2, 1, 3).reshape(L, P, CMP_LP * P)
          for n in ("cmp_w1_k", "cmp_w1_v")]
    d["cmp_w1"] = cat(w1, axis=2)
    d["small"] = cat([np.asarray(a["mla_w_uq"]).reshape(L, 2, P, 480).transpose(0, 2, 1, 3).reshape(L, P, 960),
                      np.asarray(a["mla_w_ukv"])[:, :, _ukv_order()], np.asarray(a["cmp_w2_k"]),
                      np.asarray(a["cmp_w2_v"])], axis=2)
    d["w_out"] = _slabs(a["w_out"])
    d["w_up"] = _slabs(a["w_up"])
    d["w_down"] = np.asarray(a["w_down"]).reshape(L, 8, 4, P, D).transpose(0, 1, 3, 2, 4).reshape(L * 8, P, SLAB)
    d["feats"] = cat([_features(a["ln1_gain"]), _features(a["ln2_gain"]), _features(a["mla_q_norm"]),
                      _features(a["mla_kv_norm"]), _features(np.asarray(a["cmp_pos_k"]).reshape(L, -1)),
                      _features(np.asarray(a["cmp_pos_v"]).reshape(L, -1))], axis=2)
    d["gn_gain"] = np.asarray(a["ret_gn_gain"]).reshape(L, RET_H * HD)
    d["final_gain"] = np.asarray(a["final_gain"]).reshape(1, D)
    d["final_norm_g"] = np.asarray(a["final_norm_g_2"]).reshape(1, D)
    order, split = _ab_order()
    d["ab_in"] = _slabs(np.asarray(a["ab_w_in_2"])[:, :, order])
    for to, of in (("ab_ada", "ab_w_ada_2"), ("ab_out", "ab_w_out_2"), ("cd_ada", "cd_w_ada_2"),
                   ("cd_in", "cd_w_in_2"), ("cd_out", "cd_w_out_2")):
        d[to] = _slabs(a[of])
    d["cond"] = np.stack([_features(np.asarray(a[n]).reshape(-1)) for n in ("c_2", "c_ctx_2")], axis=2)
    d["feats2"] = cat([_features(np.asarray(a[n]).reshape(-1)) for n in (
        "ab_b_ada_2", "ab_norm_g_2", "ab_conv_b_2", "cd_b_ada_2", "cd_norm_g_2")], axis=1)
    d["conv_w"] = np.asarray(a["ab_conv_w_2"]).reshape(CONV_W, 4, P).transpose(2, 1, 0)
    d["rows"] = cat([np.asarray(a["ab_ln_g_2"]), np.asarray(a["ab_ln_b_2"]),
                     np.asarray(a["ab_q_norm_g_2"])[:, split], np.asarray(a["ab_k_norm_g_2"])[:, split]], axis=1)
    d["w_fourier"] = np.asarray(a["cd_w_fourier_2"]).reshape(C_GROUPS, P, P).transpose(1, 0, 2)
    d["rpb"] = np.asarray(a["cd_rpb_2"])[0, :, 4:4 + N_DR, :].transpose(2, 0, 1).reshape(N_DC, D_HEADS * N_DR)
    return {k: np.ascontiguousarray(v) for k, v in d.items()}


def kernel(**inputs):
    import concourse.bacc as bacc
    from concourse.bass_utils import run_bass_kernel_spmd

    nc = bacc.Bacc("TRN2", target_bir_lowering=False, num_devices=1)
    arrays, dram = {}, {}
    for name, a in _layout(inputs).items():
        arrays[f"in_{name}"] = a
        dram[name] = nc.dram_tensor(f"in_{name}", a.shape, mybir.dt.from_np(a.dtype), kind="ExternalInput").ap()
    out = nc.dram_tensor("out_0", (1, SEQ, D), F32, kind="ExternalOutput").ap()
    build_program(nc, dram, out)
    r = run_bass_kernel_spmd(nc, [arrays], core_ids=[0])
    return r.results[0]["out_0"]
```

```python
from contextlib import ExitStack, contextmanager

import numpy as np

import concourse.bass as bass
from concourse import mybir

F32 = mybir.dt.float32
F32R = mybir.dt.float32r
I32 = mybir.dt.int32
ALU = mybir.AluOpType
ACT = mybir.ActivationFunctionType
AX = mybir.AxisListType

P = 128
D = 1024
KC = D // P
SEQ = 256
TT = SEQ // P
DEPTH = 2
DFF = 4 * D
HD = 64
EPS = 1e-6
NEG = -1e30
SLAB = 4096
HALF = SLAB // 2
SLOTS = 5
PART = SLAB // 4
PARTS = 3
BANK = 512

NSA_H, NSA_G, NSA_R = 6, 2, 3
MLA_H, MLA_NOPE, MLA_PE, MLA_QK = 5, 64, 32, 96
RET_H = 5
Q0, KCMP0, KSLC0, KWIN0 = 0, 384, 512, 640
VCMP0, VSLC0, VWIN0 = 768, 896, 1024
GATE0, CQ0, CKV0, KPE0 = 1152, 1170, 1426, 1554
RQ0, RK0, RV0, RG0 = 1586, 1906, 2226, 2546
N_IN = 2866
W_IN_SLABS = -(-N_IN // BANK)
NSA_PAIRS = ((0, 3), (1, 4), (2, 5))
N_CMP = (SEQ - 32) // 16 + 1
CMP_LP = 16
ROPE_P, ROPE_M, ROPE_R = (0, 8), (8, 24), (24, 56)
ROPE_N = 56

AB_VAL0, AB_GATE0, AB_Q0, AB_K0, AB_V0, AB_Z0, AB_N = 0, 512, 1024, 1536, 1664, 1792, 2816
B_HEADS, B_KV = 8, 2
CONV_W, CONV_PAD = 31, 15
TAPS_WITH_SLABS, POOL_TAPS_WITH_SLABS = 54, 16
CD_F0, CD_Q0, CD_K0, CD_V0, CD_Z0, CD_N = 0, 512, 1024, 1536, 2048, 3072
D_HEADS, C_GROUPS = 8, 4
GRID_W, ROWS, N_DR, N_DC = 64, 4, 7, 31

LAYER_SLABS = [("w_in", W_IN_SLABS), ("adapt0", 1), ("adapt1", 1), ("cmp_w1", 1), ("small", 1), ("adapt2", 2),
               ("adapt3", 2), ("adapt5", 2), ("w_out", 2), ("ffn", 16)]
ADA_NAMES = ("ab_ada", "cd_ada")
ADA_SLABS = 3 * D // BANK
ADA_HALVES = {"adapt0": (0, 2), "adapt1": (2, 3), "adapt2": (3, 6), "adapt3": (6, 10), "adapt5": (10, 12)}
WHOLE = ("cmp_w1", "small")
FFN_GROUPS = DFF // BANK
FFN_ORDER = [("w_up", 0)] + [u for g in range(1, FFN_GROUPS) for u in (("w_up", g), ("w_down", g - 1))]
FFN_ORDER.append(("w_down", FFN_GROUPS - 1))
SECOND_SLABS = [("ab_in", 6), ("ab_out", 2), ("cd_in", 6), ("cd_out", 2)]
SMALL_W = 2 * 480 + 640 + 2 * HD
UQ0, UKV0, W2K0, W2V0 = 0, 960, 1600, 1664


class InOrder:

    def __init__(self, engine, done):
        self.engine, self.done, self.n = engine, done, 0

    def __call__(self, instruction):
        self.n += 1
        instruction.then_inc(self.done, 1)
        self.engine.wait_ge(self.done, self.n)


def slab_plan():
    halves, first, first_part, n_parts = [], {}, {}, 0
    uses = [((name, layer), name, layer * n, n) for layer in range(DEPTH) for name, n in LAYER_SLABS]
    uses += [(name, name, 0, n) for name, n in SECOND_SLABS]
    for key, name, at, n in uses:
        first[key], first_part[key] = len(halves), n_parts
        if name in ADA_HALVES:
            halves += [(ADA_NAMES[key[1]], h // 2, h % 2 * HALF, HALF) for h in range(*ADA_HALVES[name])]
            continue
        n_parts += 0 if name in WHOLE else 4 * n
        for i in range(n):
            for c0 in (0, HALF):
                if name == "small" and c0:
                    continue
                if name == "ffn":
                    name_of, g = FFN_ORDER[i]
                    halves.append((name_of, at // 2 + g, c0, HALF))
                else:
                    halves.append((name, at + i, c0, SMALL_W if name == "small" else HALF))
    return halves, first, first_part


def build_program(nc, dram, out):
    plan, first, first_part = slab_plan()
    with ExitStack() as ctx:
        def sbuf(name, shape, dt=F32):
            return ctx.enter_context(nc.sbuf_tensor(name, shape, dt))

        ring = sbuf("ring", [P, SLOTS, HALF])
        w_hi, w_lo = sbuf("w_hi", [P, PARTS, PART], F32R), sbuf("w_lo", [P, PARTS, PART], F32R)
        x = sbuf("x", [P, 4, D])
        mixed = sbuf("mixed", [P, 4, D])
        ident = sbuf("ident", [P, P])
        sums = sbuf("sums", [P, 96])
        rstd = sbuf("rstd", [P, 64])
        minus_half = sbuf("minus_half", [P, 40])
        cond, cond_t = sbuf("cond", [P, KC, 2]), sbuf("cond_t", [P, KC, 2])
        ada_rows = sbuf("ada_rows", [P, 3 * D])
        gate_rows = ada_rows[:, 0:2 * D].rearrange("p (v n) -> p v n", v=2)
        ada = sbuf("ada", [P, 2, 24, 2])
        scales = sbuf("scales", [P, 2, 2, KC])
        feats2 = sbuf("feats2", [P, 24 + 8 + 4 + 24 + 8])
        col_mask = sbuf("col_mask", [P, GRID_W])
        onehot = sbuf("onehot", [N_DC, 2 * GRID_W - 1])
        rpb = sbuf("rpb", [N_DC, 2, D_HEADS * N_DR])
        banks = ctx.enter_context(nc.psum_tensor("banks", [P, 8, BANK], F32))

        half_landed = [ctx.enter_context(nc.semaphore(f"half_landed{i}")) for i in range(SLOTS)]
        half_used = ctx.enter_context(nc.semaphore("half_used"))
        hi_ready = ctx.enter_context(nc.semaphore("hi_ready"))
        part_ready = ctx.enter_context(nc.semaphore("part_ready"))
        part_used = ctx.enter_context(nc.semaphore("part_used"))
        loaded = ctx.enter_context(nc.semaphore("loaded"))
        stored = ctx.enter_context(nc.semaphore("stored"))
        n_loaded, n_stages = [0], [0]

        def load_half(sp, i):
            if i >= len(plan):
                return
            if i >= SLOTS:
                sp.wait_ge(half_used, i - SLOTS + 1)
            name, at, c0, width = plan[i]
            sp.dma_start(ring[:, i % SLOTS, 0:width], dram[name][at, :, c0:c0 + width]).then_inc(
                half_landed[i % SLOTS], 16)

        def load_behind(sp, key, n_slabs, halves=2):
            for i in range(first[key], first[key] + halves * n_slabs):
                load_half(sp, i + SLOTS)

        def half_here(engine, i):
            engine.wait_ge(half_landed[i % SLOTS], 16 * (i // SLOTS + 1))

        def part_source(key, q):
            return ring[:, (first[key] + q // 2) % SLOTS, (q % 2) * PART:(q % 2 + 1) * PART]

        def split_hi(act, key, q):
            n = first_part[key] + q
            if q % 2 == 0:
                half_here(act, first[key] + q // 2)
            if n >= PARTS:
                act.wait_ge(part_used, n - PARTS + 1)
            nc.scalar.copy(w_hi[:, n % PARTS, :], part_source(key, q)).then_inc(hi_ready, 1)

        def split_lo(dve, key, q):
            n = first_part[key] + q
            dve.wait_ge(hi_ready, n + 1)
            nc.vector.tensor_tensor(w_lo[:, n % PARTS, :], part_source(key, q), w_hi[:, n % PARTS, :].bitcast(F32),
                                    ALU.subtract).then_inc(part_ready, 1)
            if q % 2 == 1:
                dve.wait_ge(part_ready, n + 1)
                dve.sem_inc(half_used, 1)

        def part(key, q):
            n = (first_part[key] + q) % PARTS
            return [w[:, n, :].rearrange("p (k n) -> p k n", k=2) for w in (w_hi, w_lo)]

        def multiply(dst, left, right, first_one, last_one, shares_bank=False):
            pairs = ((left[0], right[0]), (left[0], right[1]), (left[1], right[0]))
            for i, (a, b) in enumerate(pairs):
                mm = nc.tensor.matmul(dst, a, b, start=first_one and i == 0, stop=last_one and i == 2,
                                      skip_group_check=shares_bank)
            return mm

        def adapt_products(pe, layer, h0, h1, bank, copied):
            place = next(p for p, (a, b) in ADA_HALVES.items() if a <= h0 and h1 <= b)
            for h in range(h0, h1):
                i = first[place, layer] + h - ADA_HALVES[place][0]
                w = ring[:, i % SLOTS, :].rearrange("p (k n) -> p k n", k=KC // 2)
                half_here(pe, i)
                for kk in range(KC // 2):
                    k = h % 2 * (KC // 2) + kk
                    if k == 0 and copied is not None:
                        pe.wait_ge(copied, 1)
                    mm = nc.tensor.matmul(banks[0:2, bank, :], cond[:, k, :], w[:, kk, :], start=(k == 0),
                                          stop=(k == KC - 1))
                    if kk == KC // 2 - 1:
                        mm.then_inc(half_used, 1)
                    yield

        def copy_adapted(act, layer, s, bank):
            place, (a, _) = next((p, ab) for p, ab in ADA_HALVES.items() if ab[0] <= 2 * s + 1 < ab[1])
            act.wait_ge(half_used, first[place, layer] + 2 * s + 1 - a + 1)
            return nc.scalar.copy(ada_rows[HD * layer:HD * layer + 2, s * BANK:(s + 1) * BANK], banks[0:2, bank, :])

        def advance(work, n=1000):
            for _ in range(n):
                next(work, None)

        def load_const(sp, dst, src):
            sp.dma_start(dst, src).then_inc(loaded, 16)
            n_loaded[0] += 16

        @contextmanager
        def stage(*names):
            n_stages[0] += 1
            sems = [nc.alloc_semaphore(f"{n}_{n_stages[0]}") for n in names]
            yield sems
            nc.clear_and_free_semaphores(sems)
            nc.all_engine_barrier()

        def accumulate(dst, pairs):
            n = len(pairs)
            for i, (lhsT, rhs) in enumerate(pairs):
                mm = nc.tensor.matmul(dst, lhsT, rhs, start=(i == 0), stop=(i == n - 1))
            return mm


        def normalize_transpose(hidden, tiles, scales, shifts=None):
            T = len(tiles)
            per = len(scales)
            span = T * P // per
            hi, lo = hidden
            mine = [n for n in range(T) if n % 2 == 0]
            others = [n for n in range(T) if n % 2 == 1]
            with stage("squares_summed", "pool_step", "rstd_ready", "scaled", "scaled_too", "turned", "high_ready",
                       "whole_ready", "low_ready", "low_ready_too") as (
                    squares_summed, pool_step, rstd_ready, scaled, scaled_too, turned, high_ready, whole_ready,
                    low_ready, low_ready_too), \
                    nc.sbuf_tensor(f"spare_{n_stages[0]}", [P, 2, T * P if shifts else 1], F32) as spare, \
                    nc.Block() as block:
                def chunk(a, c):
                    return a[:, c, 0:T * P]

                @block.vector
                def _(dve):
                    for n in mine:
                        t = tiles[n]
                        nc.vector.tensor_tensor_reduce(mixed[:, t, :], x[:, t, :], x[:, t, :], 1.0, 0.0, ALU.mult,
                                                       ALU.add, sums[:, n:n + 1]).then_inc(squares_summed, 1)
                    dve.wait_ge(rstd_ready, 1)
                    for n in others:
                        t = tiles[n]
                        nc.vector.tensor_scalar(mixed[:, t, :], x[:, t, :], rstd[:, n:n + 1], None,
                                                ALU.mult).then_inc(scaled_too, 1)
                    if shifts is None:
                        for c in range(KC):
                            dve.wait_ge(high_ready, c + 1)
                            nc.vector.scalar_tensor_tensor(out=chunk(lo, c), in0=chunk(banks, c),
                                                           scalar=scales[0][:, c:c + 1], in1=chunk(hi, c).bitcast(F32),
                                                           op0=ALU.mult, op1=ALU.subtract)
                        return
                    for c in range(KC + 1):
                        if c < KC:
                            dve.wait_ge(high_ready, per * (c + 1))
                            if c >= 2:
                                dve.wait_ge((low_ready, low_ready_too)[c % 2], c // 2)
                            for v in range(per):
                                cols = slice(v * span, (v + 1) * span)
                                nc.vector.tensor_scalar(spare[:, c % 2, cols], banks[:, c, cols],
                                                        scales[v][:, c:c + 1], shifts[v][:, c:c + 1],
                                                        ALU.mult, ALU.add).then_inc(whole_ready, 1)
                        if c % 2 == 1:
                            dve.wait_ge(whole_ready, per * c)
                            nc.vector.tensor_tensor(chunk(lo, c - 1), spare[:, 0, :], chunk(hi, c - 1).bitcast(F32),
                                                    ALU.subtract).then_inc(low_ready, 1)

                @block.gpsimd
                def _(pool):
                    step = InOrder(pool, pool_step)
                    pool.wait_ge(squares_summed, T)
                    step(nc.gpsimd.tensor_scalar(rstd[:, 0:T], sums[:, 0:T], 1.0 / D, EPS, ALU.mult, ALU.add))
                    nc.gpsimd.tensor_tensor(rstd[:, 0:T], rstd[:, 0:T], minus_half[:, 0:T],
                                            ALU.pow).then_inc(rstd_ready, 1)
                    if shifts is not None:
                        for c in range(1, KC, 2):
                            pool.wait_ge(whole_ready, per * (c + 1))
                            nc.gpsimd.tensor_tensor(chunk(lo, c), spare[:, 1, :], chunk(hi, c).bitcast(F32),
                                                    ALU.subtract).then_inc(low_ready_too, 1)

                @block.scalar
                def _(act):
                    for n in others:
                        t = tiles[n]
                        nc.scalar.activation(mixed[:, t, :], x[:, t, :], ACT.Square,
                                             accum_out=sums[:, n:n + 1]).then_inc(squares_summed, 1)
                    act.wait_ge(rstd_ready, 1)
                    for n in mine:
                        t = tiles[n]
                        nc.scalar.activation(mixed[:, t, :], x[:, t, :], ACT.Copy,
                                             scale=rstd[:, n:n + 1]).then_inc(scaled, 1)
                    for c in range(KC):
                        act.wait_ge(turned, c + 1)
                        for v in range(per):
                            cols = slice(v * span, (v + 1) * span)
                            shift = {} if shifts is None else {"bias": shifts[v][:, c:c + 1]}
                            nc.scalar.activation(hi[:, c, cols], banks[:, c, cols],
                                                 ACT.Copy if shifts is None else ACT.Identity,
                                                 scale=scales[v][:, c:c + 1], **shift).then_inc(high_ready, 1)

                @block.tensor
                def _(pe):
                    for n, t in enumerate(tiles):
                        pe.wait_ge((scaled, scaled_too)[n % 2], n // 2 + 1)
                        for c in range(KC):
                            mm = nc.tensor.transpose(banks[:, c, n * P:(n + 1) * P],
                                                     mixed[:, t, c * P:(c + 1) * P], ident[:])
                            if n == T - 1:
                                mm.then_inc(turned, 1)

        def project(key, hidden, widths, tiles_of, dst):
            n_slabs = len(widths)
            with stage("evacuated") as (evacuated,), nc.Block() as block:
                @block.sync
                def _(sp):
                    load_behind(sp, key, n_slabs)

                @block.tensor
                def _(pe):
                    for s in range(n_slabs):
                        if s >= 2:
                            pe.wait_ge(evacuated, s - 1)
                        multiply_slab(pe, key, s, hidden, widths[s], tiles_of[s])

                @block.scalar
                def _(act):
                    def copy_products(s):
                        products_done(act, key, s)
                        for t in tiles_of[s]:
                            last = nc.scalar.copy(dst[:, t, s * BANK:s * BANK + widths[s]],
                                                  banks[:, 4 * (s % 2) + t, 0:widths[s]])
                        last.then_inc(evacuated, 1)

                    for q in range(4 * n_slabs):
                        split_hi(act, key, q)
                        if q >= 5 and q % 4 == 1:
                            copy_products(q // 4 - 1)
                    copy_products(n_slabs - 1)

                @block.vector
                def _(dve):
                    for q in range(4 * n_slabs):
                        split_lo(dve, key, q)

        def multiply_slab(pe, key, s, hidden, width, tiles):
            hi, lo = hidden
            for q in range(4):
                n = first_part[key] + 4 * s + q
                pe.wait_ge(part_ready, n + 1)
                wh, wl = part(key, 4 * s + q)
                for kk in range(2):
                    k = 2 * q + kk
                    for t in tiles:
                        cols = slice(t * P, (t + 1) * P)
                        mm = multiply(banks[:, 4 * (s % 2) + t, 0:width], (hi[:, k, cols], lo[:, k, cols]),
                                      (wh[:, kk, 0:width], wl[:, kk, 0:width]), k == 0, k == KC - 1)
                mm.then_inc(part_used, 1)

        def products_done(engine, key, s):
            engine.wait_ge(part_used, first_part[key] + 4 * (s + 1))

        def transpose_groups(groups, padded=None):
            with stage("turned", "copied0", "copied1", "cleared") as (turned, copied0, copied1, cleared), \
                    nc.Block() as block:
                @block.gpsimd
                def _(pool):
                    if padded is not None:
                        nc.gpsimd.memset(padded[:], 0.0).then_inc(cleared, 1)

                @block.tensor
                def _(pe):
                    for g, (blocks, _) in enumerate(groups):
                        if g >= 8:
                            pe.wait_ge((copied0, copied1)[g % 2], (g - 8) // 2 + 1)
                        for j, src in enumerate(blocks):
                            w = src.shape[-1]
                            mm = nc.tensor.transpose(banks[0:w, g % 8, j * P:(j + 1) * P], src, ident[:])
                        mm.then_inc(turned, 1)

                @block.vector
                def _(dve):
                    if padded is not None:
                        dve.wait_ge(cleared, 1)
                    for g, (_, copies) in enumerate(groups):
                        if g % 2 == 0:
                            dve.wait_ge(turned, g + 1)
                            for copy in copies:
                                last = copy(nc.vector, banks[:, g % 8, :])
                            last.then_inc(copied0, 1)

                @block.scalar
                def _(act):
                    if padded is not None:
                        act.wait_ge(cleared, 1)
                    for g, (_, copies) in enumerate(groups):
                        if g % 2 == 1:
                            act.wait_ge(turned, g + 1)
                            for copy in copies:
                                last = copy(nc.scalar, banks[:, g % 8, :])
                            last.then_inc(copied1, 1)

        def copy_out(engine, dst, src, scale=None, bias=None):
            if engine is nc.scalar:
                if scale is None:
                    return nc.scalar.copy(dst, src)
                return nc.scalar.activation(dst, src, ACT.Copy, scale=scale)
            if scale is None:
                return nc.vector.tensor_copy(dst, src)
            return nc.vector.tensor_scalar(dst, src, scale, None, ALU.mult)

        def out_project(key, turned_y, tiles, gates=None):
            with stage("gated") as (gated,), nc.Block() as block:
                @block.sync
                def _(sp):
                    load_behind(sp, key, 2)

                @block.tensor
                def _(pe):
                    for s in range(2):
                        multiply_slab(pe, key, s, turned_y, BANK, tiles)

                @block.scalar
                def _(act):
                    for q in range(8):
                        split_hi(act, key, q)

                @block.vector
                def _(dve):
                    for q in range(8):
                        split_lo(dve, key, q)
                    for s in range(2):
                        products_done(dve, key, s)
                        for i, t in enumerate(tiles):
                            here = x[:, t, s * BANK:(s + 1) * BANK]
                            src = banks[:, 4 * s + t, :]
                            if gates is not None:
                                gated_y = mixed[:, t, s * BANK:(s + 1) * BANK]
                                nc.vector.tensor_tensor(gated_y, src, gates[t // 2][:, s * BANK:(s + 1) * BANK],
                                                        ALU.mult).then_inc(gated, 1)
                                dve.wait_ge(gated, s * len(tiles) + i + 1)
                                src = gated_y
                            nc.vector.tensor_tensor(here, src, here, ALU.add)

        def attend(units, buffers, aside=None, pool_aside=None):
            probs, probsT, nmax, total, inverse = buffers
            n_units = len(units)
            S, T, O = 0, 3, 5
            TURN, VALUES, WEIGH = 2, 4, 5
            SUMS = 6
            with stage("scores_ready", "max_ready", "probs_ready", "probs_turned",
                       "turned_copied", "values_ready", "weighed", "dve_step", "aside_step", "pool_step") as (
                    scores_ready, max_ready, probs_ready, probs_turned,
                    turned_copied, values_ready, weighed, dve_step, aside_step,
                    pool_step), nc.Block() as block:
                @block.gpsimd
                def _(pool):
                    if pool_aside is not None:
                        pool_aside(InOrder(pool, pool_step))

                @block.tensor
                def _(pe):
                    def scores(i):
                        if i >= 3:
                            pe.wait_ge(probs_ready, i - 2)
                        for qT, kT, c0, n, _ in units[i]["rows"]:
                            mm = nc.tensor.matmul(banks[:, S + i % 3, c0:c0 + n], qT, kT, start=True, stop=True)
                        mm.then_inc(scores_ready, 1)

                    def turn(i):
                        pe.wait_ge(probs_ready, i + 1)
                        if i >= 2:
                            pe.wait_ge(turned_copied, i - 1)
                        for c in range(units[i]["width"] // P):
                            mm = nc.tensor.transpose(banks[:, T + i % 2, c * P:(c + 1) * P],
                                                     probs[:, i % 3, c * P:(c + 1) * P], ident[:])
                        mm.then_inc(probs_turned, 1)

                    def values(i):
                        pe.wait_ge(turned_copied, i + 1)
                        if i >= 3:
                            pe.wait_ge(weighed, i - 2)
                        for r, (_, _, c0, n, vs) in enumerate(units[i]["rows"]):
                            mm = accumulate(banks[:, O + i % 3, r * HD:(r + 1) * HD],
                                            [(probsT[:, i % 2, c0 + c * P:c0 + (c + 1) * P], v)
                                             for c, v in enumerate(vs)])
                        mm.then_inc(values_ready, 1)

                    for i in range(n_units + VALUES):
                        if i < n_units:
                            scores(i)
                        if TURN <= i < n_units + TURN:
                            turn(i - TURN)
                        if i >= VALUES:
                            values(i - VALUES)

                @block.vector
                def _(dve):
                    noted = [0]

                    def note(instruction):
                        noted[0] += 1
                        instruction.then_inc(dve_step, 1)
                        return noted[0]

                    def step_both(i, w):
                        unit = units[i] if i < n_units else None
                        done = units[w] if w >= 0 else None
                        src = banks[:, S + i % 3, :]
                        masked = None
                        if unit is not None:
                            dve.wait_ge(scores_ready, i + 1)
                            if unit["mask"] is not None:
                                m = src[:, 0:unit["mask"].free_size()]
                                masked = note(nc.vector.scalar_tensor_tensor(
                                    out=m, in0=m, scalar=unit["scale"], in1=unit["mask"], op0=ALU.mult, op1=ALU.add))
                        if done is not None:
                            R = len(done["rows"])
                            dve.wait_ge(probs_ready, w + 1)
                            inverted = note(nc.vector.reciprocal(inverse[:, w % 3, 0:R], total[:, w % SUMS, 0:R]))
                        if unit is not None:
                            if masked:
                                dve.wait_ge(dve_step, masked)
                            if done is not None and done.get("gates") is not None:
                                row_max(i, unit, src, 0)
                                dve.wait_ge(dve_step, inverted)
                                for r in range(R):
                                    here = inverse[:, w % 3, r:r + 1]
                                    inverted = note(nc.vector.tensor_tensor(here, here, done["gates"][r], ALU.mult))
                                last = row_max(i, unit, src, 1)
                            else:
                                for r in range(len(unit["rows"])):
                                    last = row_max(i, unit, src, r)
                            last.then_inc(max_ready, 1)
                        elif done is not None and done.get("gates") is not None:
                            dve.wait_ge(dve_step, inverted)
                            for r in range(R):
                                here = inverse[:, w % 3, r:r + 1]
                                inverted = note(nc.vector.tensor_tensor(here, here, done["gates"][r], ALU.mult))
                        if done is not None:
                            dve.wait_ge(dve_step, inverted)
                            dve.wait_ge(values_ready, w + 1)
                            for r in range(R):
                                last = done["weigh"](r, banks[:, O + w % 3, r * HD:(r + 1) * HD],
                                                     inverse[:, w % 3, r:r + 1])
                            last.then_inc(weighed, 1)

                    def row_max(i, unit, src, r):
                        _, _, c0, n, _ = unit["rows"][r]
                        return nc.vector.tensor_reduce(nmax[:, i % 3, r:r + 1], src[:, c0:c0 + n], AX.X, ALU.max,
                                                       negate=True)

                    more = iter(()) if aside is None else aside(aside_step)
                    for i in range(n_units + WEIGH):
                        step_both(i, i - WEIGH)
                        advance(more, 2)
                    advance(more)

                @block.scalar
                def _(act):
                    def exponential(i):
                        act.wait_ge(max_ready, i + 1)
                        if i >= 3:
                            act.wait_ge(probs_turned, i - 2)
                        if i >= SUMS:
                            act.wait_ge(weighed, i - SUMS + 1)
                        src = banks[:, S + i % 3, :]
                        for r, (_, _, c0, n, _) in enumerate(units[i]["rows"]):
                            last = nc.scalar.activation(probs[:, i % 3, c0:c0 + n], src[:, c0:c0 + n], ACT.Exp,
                                                        bias=nmax[:, i % 3, r:r + 1],
                                                        accum_out=total[:, i % SUMS, r:r + 1])
                        last.then_inc(probs_ready, 1)

                    def copy_turned(i):
                        act.wait_ge(probs_turned, i + 1)
                        if i >= 2:
                            act.wait_ge(values_ready, i - 1)
                        w = units[i]["width"]
                        nc.scalar.copy(probsT[:, i % 2, 0:w], banks[:, T + i % 2, 0:w]).then_inc(turned_copied, 1)

                    for i in range(n_units + TURN):
                        if i < n_units:
                            exponential(i)
                        if i >= TURN:
                            copy_turned(i - TURN)

        def rope(dve, step, v, cos, sin, half, temps):
            T, H = v.shape[1], v.shape[2]
            shape = [P, T, H, half]
            c = cos.unsqueeze(2).broadcast_to(shape)
            s = sin.unsqueeze(2).broadcast_to(shape)
            x1, x2 = v[:, :, :, 0:half], v[:, :, :, half:2 * half]
            a, b, e, f = [t[:, 0:T * H * half].rearrange("p (t h d) -> p t h d", t=T, h=H) for t in temps]
            nc.vector.tensor_tensor(a, x1, c, ALU.mult)
            nc.vector.tensor_tensor(b, x2, s, ALU.mult)
            nc.vector.tensor_tensor(e, x2, c, ALU.mult)
            step(nc.vector.tensor_tensor(f, x1, s, ALU.mult))
            nc.vector.tensor_tensor(x1, a, b, ALU.subtract)
            step(nc.vector.tensor_tensor(x2, e, f, ALU.add))

        def first_block():
            with ExitStack() as local:
                def sb(name, shape, dt=F32):
                    return local.enter_context(nc.sbuf_tensor(name, shape, dt))

                causal = sb("causal", [P, 3 * P])
                cmp_add = sb("cmp_add", [P, TT * 16])
                cmp_keep = sb("cmp_keep", [P, TT * 16])
                feats = sb("feats", [P, DEPTH, 51])
                gn_gain = sb("gn_gain", [P, RET_H * HD])
                cosT, sinT = sb("cosT", [P, TT, ROPE_N]), sb("sinT", [P, TT, ROPE_N])
                nmax, total, inverse = (sb(n, [P, 6, 2]) for n in ("nmax", "total", "inverse"))
                k2 = sb("k2", [P, 2, NSA_G, P])
                flat = sb("flat", [P, 2, CMP_LP, NSA_G, N_CMP])
                gelu = sb("gelu", [P, 4, 4 * N_CMP])
                kcT, vc = sb("kcT", [P, N_CMP]), sb("vc", [N_CMP, NSA_G, HD])
                branch = sb("branch", [P, 2, TT * 18])

                decay = sb("decay", [P, RET_H, 3 * P])
                scratch = mixed[:, 2:4, :].rearrange("p a b -> p (a b)")

                def mixers(layer, sb2, proj, qn, kvn, pos_of):
                    fT = sb2("fT", [P, 9, SEQ])
                    k_padded = sb2("k_padded", [P, 2, NSA_G, SEQ])
                    mqT, mkT = (sb2(n, [MLA_QK, MLA_H, SEQ]) for n in ("mqT", "mkT"))
                    mla_q, mla_k = (sb2(n, [P, TT, MLA_H * MLA_QK]) for n in ("mla_q", "mla_k"))
                    mla_v = sb2("mla_v", [P, TT, MLA_H * HD])
                    latents = sb2("latents", [P, 3, SEQ])
                    probs, probsT = sb2("probs", [P, 3, 3 * P]), sb2("probsT", [P, 2, 3 * P])
                    four = sb2("four", [P, 4, 640])
                    temps = [four[:, i, :] for i in range(4)]
                    prepare_heads(layer, proj, temps, cosT, sinT, gn_gain, branch,
                                  latents.rearrange("p a b -> p (a b)"))
                    transpose_heads(proj, fT, k_padded, k2, latents, qn, kvn)
                    small_products(layer, proj, latents, k2, flat, pos_of, gelu, kcT, vc, mla_q, mla_k, mla_v,
                                   cosT, sinT, temps)
                    groups = []
                    for src, dst in ((mla_q, mqT), (mla_k, mkT)):
                        for h0 in range(0, MLA_H, 2):
                            hs = range(h0, min(h0 + 2, MLA_H))
                            blocks = [src[:, t, h * MLA_QK:(h + 1) * MLA_QK] for h in hs for t in range(TT)]
                            n = len(blocks) * P

                            def copy(engine, bank, dst=dst, h0=h0, hs=hs, n=n):
                                return copy_out(engine, dst[:, h0:h0 + len(hs), :],
                                                bank[0:MLA_QK, 0:n].rearrange("p (h s) -> p h s", h=len(hs)))
                            groups.append((blocks, [copy]))
                    transpose_groups(groups)
                    compressed_attention(layer, fT, kcT, vc, cmp_add, cmp_keep, branch, four)

                    units = []
                    for b, v0 in enumerate((VSLC0, VWIN0)):
                        for pair in range(3):
                            for g in range(NSA_G):
                                units.append(causal_unit(
                                    fT[:, pair, :], k_padded[:, b, g, :],
                                    [proj[:, t, v0 + g * HD:v0 + (g + 1) * HD] for t in range(TT)],
                                    HD ** -0.5, causal, add_weigh(NSA_PAIRS[pair][g] * HD),
                                    [branch[:, 0, t * 18 + NSA_PAIRS[pair][g] * 3 + b + 1:
                                            t * 18 + NSA_PAIRS[pair][g] * 3 + b + 2] for t in range(TT)]))
                    for h in range(MLA_H):
                        units.append(causal_unit(
                            mqT[:, h, :], mkT[:, h, :], [mla_v[:, t, h * HD:(h + 1) * HD] for t in range(TT)],
                            MLA_QK ** -0.5, causal, plain_weigh(NSA_H * HD + h * HD, (0, 1))))
                    attend(units, (probs, probsT, nmax, total, inverse))
                    retain(layer, proj, fT, decay, gn_gain, four)

                with stage("first_loaded", "dve_step", "angles_ready") as (first_loaded, dve_step, angles_ready), \
                        nc.Block() as block:
                    def load_first(sp, dst, src):
                        sp.dma_start(dst, src).then_inc(first_loaded, 16)

                    pos_i = local.enter_context(nc.sbuf_tensor("pos_i", [P, TT], I32))
                    pos = sb("pos", [P, TT])
                    freqs = sb("freqs", [P, ROPE_N])
                    ang = scratch[:, 0:TT * ROPE_N].rearrange("p (t n) -> p t n", t=TT)
                    turns = scratch[:, 256:256 + TT * ROPE_N].rearrange("p (t n) -> p t n", t=TT)
                    quarter = scratch[:, 512:512 + TT * ROPE_N].rearrange("p (t n) -> p t n", t=TT)

                    @block.sync
                    def _(sp):
                        load_first(sp, pos_i[:], dram["positions"])
                        load_first(sp, freqs[:], dram["freqs"])
                        load_first(sp, x[:, 0:TT, :], dram["x"])
                        load_first(sp, ident[:], dram["ident"])
                        load_first(sp, feats[:], dram["feats"])
                        for i in range(SLOTS):
                            load_half(sp, i)
                        load_const(sp, causal[:], dram["causal"])
                        load_const(sp, decay[:], dram["decay"])
                        load_const(sp, cmp_add[:], dram["cmp_add"])
                        load_const(sp, cmp_keep[:], dram["cmp_keep"])
                        for dst, name in ((cond, "cond"), (feats2, "feats2"), (col_mask, "col_mask"),
                                          (onehot, "onehot"), (rpb, "rpb")):
                            load_const(sp, dst[:], dram[name])
                        load_const(sp, x[:, TT:2 * TT, :], dram["ctx"])

                    @block.gpsimd
                    def _(pool):
                        nc.gpsimd.memset(minus_half[:], -0.5)

                    @block.vector
                    def _(dve):
                        step = InOrder(dve, dve_step)
                        dve.wait_ge(first_loaded, 16 * 5)
                        step(nc.vector.tensor_copy(pos[:], pos_i[:]))
                        for t in range(TT):
                            last = nc.vector.tensor_scalar(ang[:, t, :], freqs[:], pos[:, t:t + 1], None, ALU.mult)
                        step(last)
                        step(nc.vector.tensor_scalar(turns, ang, 1.0 / (2 * np.pi), 1.5 * 2.0 ** 23, ALU.mult, ALU.add))
                        step(nc.vector.tensor_scalar(turns, turns, -1.5 * 2.0 ** 23, None, ALU.add))
                        hi = 6.28125
                        for part in (hi, 2 * np.pi - hi):
                            step(nc.vector.scalar_tensor_tensor(out=ang, in0=turns, scalar=-part, in1=ang,
                                                                op0=ALU.mult, op1=ALU.add))
                        edge = 3.1415925
                        step(nc.vector.tensor_scalar(ang, ang, edge, -edge, ALU.min, ALU.max))
                        step(nc.vector.scalar_tensor_tensor(out=quarter, in0=ang, scalar=-1.0, in1=ang,
                                                            op0=ALU.mult, op1=ALU.min))
                        nc.vector.tensor_scalar(quarter, quarter, np.pi / 2, None, ALU.add).then_inc(angles_ready, 1)

                    @block.scalar
                    def _(act):
                        act.wait_ge(angles_ready, 1)
                        nc.scalar.activation(sinT[:], ang, ACT.Sin)
                        nc.scalar.activation(cosT[:], quarter, ACT.Sin)

                for layer in range(DEPTH):
                    f = feats[:, layer, :]
                    ln1, ln2, qn, kvn = f[:, 0:8], f[:, 8:16], f[:, 16:18], f[:, 18:19]
                    pos_of = (f[:, 19:35], f[:, 35:51])
                    with scope(layer) as sb2:
                        proj = sb2("proj", [P, TT, N_IN])
                        with scope(layer) as sb3:
                            hidden = [sb3(n, [P, KC, SEQ], F32R) for n in ("h_hi", "h_lo")]
                            normalize_transpose(hidden, (0, 1), [ln1])
                            widths = [min(BANK, N_IN - i * BANK) for i in range(W_IN_SLABS)]
                            project(("w_in", layer), hidden, widths, [(0, 1)] * W_IN_SLABS, proj)
                        mixers(layer, sb2, proj, qn, kvn, pos_of)
                    with scope(layer) as sb2:
                        turned_y = [sb2(n, [P, KC, SEQ], F32R) for n in ("y_hi", "y_lo")]
                        turn_mixed(turned_y, TT)
                        out_project(("w_out", layer), turned_y, (0, 1))
                    with scope(layer) as sb2:
                        hidden = [sb2(n, [P, KC, SEQ], F32R) for n in ("f_hi", "f_lo")]
                        normalize_transpose(hidden, (0, 1), [ln2])
                        feed_forward(layer, sb2, hidden)

        @contextmanager
        def scope(layer):
            with ExitStack() as local:
                yield lambda name, shape, dt=F32: local.enter_context(nc.sbuf_tensor(f"{name}_{layer}", shape, dt))

        def causal_unit(qT, kT, vs, scale, causal, weigh, gates=None):
            return {"rows": [(qT[:, 0:P], kT[:, 0:P], 0, P, vs[0:1]),
                             (qT[:, P:2 * P], kT[:, 0:2 * P], P, 2 * P, vs)],
                    "width": 3 * P, "scale": scale, "mask": causal[:], "weigh": weigh, "gates": gates}

        def add_weigh(column):
            def weigh(t, product, inverse):
                here = mixed[:, t, column:column + HD]
                return nc.vector.scalar_tensor_tensor(out=here, in0=product, scalar=inverse, in1=here,
                                                      op0=ALU.mult, op1=ALU.add)
            return weigh

        def plain_weigh(column, tiles):
            def weigh(r, product, inverse):
                return nc.vector.tensor_scalar(mixed[:, tiles[r], column:column + HD], product, inverse, None, ALU.mult)
            return weigh

        def prepare_heads(layer, proj, temps, cosT, sinT, gn_gain, branch, cq_sq):
            pr = proj[:, 0:TT, :]
            with stage("dve_step", "pool_step", "sums_ready", "rstd_ready", "tanh_ready", "gain_here",
                       "cond_tanh", "cond_ready") as (
                    dve_step, pool_step, sums_ready, rstd_ready, tanh_ready, gain_here, cond_tanh,
                    cond_ready), nc.Block() as block:
                @block.tensor
                def _(pe):
                    if layer == 0:
                        pe.wait_ge(cond_ready, 1)
                    advance(adapt_products(pe, layer, 0, 2, 0, None))

                @block.sync
                def _(sp):
                    load_behind(sp, ("adapt0", layer), 1)
                    sp.wait_ge(loaded, n_loaded[0])
                    sp.dma_start(gn_gain[:], dram["gn_gain"][layer:layer + 1, :].broadcast_to([P, RET_H * HD])
                                 ).then_inc(gain_here, 16)
                    sp.wait_ge(gain_here, 16)

                @block.vector
                def _(dve):
                    step = InOrder(dve, dve_step)
                    sq = cq_sq[:, :].rearrange("p (t n) -> p t n", t=TT)
                    if layer == 0:
                        dve.wait_ge(cond_tanh, 1)
                        step(nc.vector.tensor_scalar(cond_t[:], cond_t[:], 0.5, 0.5, ALU.mult, ALU.add))
                        nc.vector.tensor_tensor(cond[:], cond[:], cond_t[:], ALU.mult).then_inc(cond_ready, 1)
                    for t in range(TT):
                        nc.vector.tensor_tensor_reduce(sq[:, t, 0:256], pr[:, t, CQ0:CQ0 + 256], pr[:, t, CQ0:CQ0 + 256],
                                                       1.0 / 256, 0.0, ALU.mult, ALU.add, sums[:, t:t + 1])
                        last = nc.vector.tensor_tensor_reduce(
                            sq[:, t, 256:384], pr[:, t, CKV0:CKV0 + P], pr[:, t, CKV0:CKV0 + P],
                            1.0 / P, 0.0, ALU.mult, ALU.add, sums[:, TT + t:TT + t + 1])
                    last.then_inc(sums_ready, 1)

                    def heads(c0, n, d):
                        return pr[:, :, c0:c0 + n * d].rearrange("p t (h d) -> p t h d", h=n)

                    for view, (a, b) in ((heads(Q0, 12, HD), ROPE_P), (heads(KPE0, 1, MLA_PE), ROPE_M),
                                         (heads(RQ0, 2 * RET_H, HD), ROPE_R)):
                        rope(dve, step, view, cosT[:, :, a:b], sinT[:, :, a:b], b - a, temps)
                    dve.wait_ge(rstd_ready, 1)
                    for t in range(TT):
                        for c0, n, k in ((CQ0, 256, t), (CKV0, P, TT + t)):
                            nc.vector.tensor_scalar(pr[:, t, c0:c0 + n], pr[:, t, c0:c0 + n], rstd[:, k:k + 1],
                                                    None, ALU.mult)
                    dve.wait_ge(tanh_ready, 1)
                    nc.vector.tensor_scalar(branch[:, 0, :], branch[:, 1, :], 0.5, 0.5, ALU.mult, ALU.add)
                    dve.wait_ge(tanh_ready, 2)
                    tanh = scratch_ret()
                    gate = pr[:, :, RG0:RG0 + RET_H * HD]
                    step(nc.vector.tensor_scalar(tanh, tanh, 0.5, 0.5, ALU.mult, ALU.add))
                    nc.vector.tensor_tensor(gate, gate, tanh, ALU.mult)

                @block.gpsimd
                def _(pool):
                    step = InOrder(pool, pool_step)
                    pool.wait_ge(sums_ready, 1)
                    step(nc.gpsimd.tensor_scalar(rstd[:, 0:4], sums[:, 0:4], EPS, None, ALU.add))
                    nc.gpsimd.tensor_tensor(rstd[:, 0:4], rstd[:, 0:4], minus_half[:, 0:4], ALU.pow).then_inc(rstd_ready, 1)

                @block.scalar
                def _(act):
                    if layer == 0:
                        act.wait_ge(loaded, n_loaded[0])
                        nc.scalar.activation(cond_t[:], cond[:], ACT.Tanh, scale=0.5).then_inc(cond_tanh, 1)
                    nc.scalar.activation(branch[:, 1, :].rearrange("p (t n) -> p t n", t=TT),
                                         pr[:, :, GATE0:GATE0 + 18], ACT.Tanh, scale=0.5).then_inc(tanh_ready, 1)
                    nc.scalar.activation(scratch_ret(), pr[:, :, RG0:RG0 + RET_H * HD], ACT.Tanh,
                                         scale=0.5).then_inc(tanh_ready, 1)
                    copy_adapted(act, layer, 0, 0)

        def scratch_ret():
            return mixed[:, 0:TT, 704:704 + RET_H * HD]

        def transpose_heads(proj, fT, k_padded, k2, latents, qn, kvn):
            def cols(c0, w):
                return [proj[:, t, c0:c0 + w] for t in range(TT)]

            def pad_keys(branch, parity):
                lanes = slice(parity * HD, (parity + 1) * HD)
                return lambda engine, bank: copy_out(engine, k_padded[lanes, branch, parity, :],
                                                     bank[lanes, branch * SEQ:(branch + 1) * SEQ])

            def to_fT(b):
                return lambda engine, bank: copy_out(engine, fT[:, b:b + 2, :], bank.rearrange("p (b s) -> p b s", b=2))

            order = [Q0, Q0 + P, Q0 + 2 * P, KSLC0, KWIN0, RQ0, RQ0 + P, RK0, RK0 + P]
            order[3:5] = []
            groups = [(cols(order[b], P) + cols(order[b + 1], P), [to_fT(b)]) for b in (0, 2, 4)]
            groups.append((cols(KSLC0, P) + cols(KWIN0, P), [pad_keys(b, g) for b in range(2) for g in range(2)]))
            groups.append((cols(order[6], P), [lambda engine, bank: copy_out(engine, fT[:, 6, :], bank[:, 0:SEQ])]))
            groups.append((cols(RQ0 + 2 * P, HD) + cols(RK0 + 2 * P, HD), [
                lambda engine, bank: copy_out(engine, fT[0:HD, 7:9, :],
                                              bank[0:HD, :].rearrange("p (b s) -> p b s", b=2))]))

            def pair_up(kv, g, parity):
                def copy(engine, bank):
                    src = bank[g * HD:(g + 1) * HD, kv * SEQ:(kv + 1) * SEQ].rearrange("p (m e) -> p m e", e=2)
                    return copy_out(engine, k2[parity * HD:(parity + 1) * HD, kv, g, :], src[:, :, parity])
                return copy

            groups.append((cols(KCMP0, P) + cols(VCMP0, P),
                           [pair_up(kv, g, e) for kv in range(2) for g in range(NSA_G) for e in range(2)]))

            def latent(dst, c0, scale):
                return lambda engine, bank: copy_out(engine, dst, bank[:, c0:c0 + SEQ], scale)

            groups.append((cols(CQ0, P) + cols(CQ0 + P, P),
                           [latent(latents[:, 0, :], 0, qn[:, 0:1]), latent(latents[:, 1, :], SEQ, qn[:, 1:2])]))
            groups.append((cols(CKV0, P), [latent(latents[:, 2, :], 0, kvn)]))
            transpose_groups(groups, k_padded)

        def small_products(layer, proj, latents, k2, flat, pos_of, gelu, kcT, vc, mla_q, mla_k, mla_v, cosT, sinT, temps):
            h_w1, h_small = first["cmp_w1", layer], first["small", layer]
            w1 = [ring[:, (h_w1 + v) % SLOTS, :].rearrange("p (l h) -> p l h", l=CMP_LP) for v in range(2)]
            small = ring[:, h_small % SLOTS, :]
            NC2 = NSA_G * N_CMP
            with stage("dve_step", "flat_ready", "hidden_ready", "inner_ready", "tanh_ready", "gelu_ready", "mla_ready",
                       "cmp_ready", "act_copied", "row_copied") as (
                    dve_step, flat_ready, hidden_ready, inner_ready, tanh_ready, gelu_ready, mla_ready, cmp_ready,
                    act_copied, row_copied), nc.Block() as block:
                @block.sync
                def _(sp):
                    for i in range(first["adapt1", layer], first["adapt3", layer]):
                        load_half(sp, i + SLOTS)

                @block.tensor
                def _(pe):
                    advance(adapt_products(pe, layer, 2, 3, 7, None))
                    pe.wait_ge(flat_ready, 1)
                    for kv in range(2):
                        half_here(pe, h_w1 + kv)
                        mm = accumulate(banks[:, 0, kv * NC2:(kv + 1) * NC2],
                                        [(w1[kv][:, lp, :], flat[:, kv, lp, :, :].rearrange("p g n -> p (g n)"))
                                         for lp in range(CMP_LP)])
                    mm.then_inc(hidden_ready, 1)
                    pe.wait_ge(hidden_ready, 1)
                    pe.sem_inc(half_used, 2)
                    half_here(pe, h_small)
                    for t in range(TT):
                        accumulate(banks[:, 1 + t, 0:480],
                                   [(latents[:, c, t * P:(t + 1) * P],
                                     small[:, UQ0 + c * 480:UQ0 + (c + 1) * 480]) for c in range(2)])
                        for part in range(2):
                            mm = nc.tensor.matmul(banks[:, 3 + 2 * part + t, 0:320], latents[:, 2, t * P:(t + 1) * P],
                                                  small[:, UKV0 + part * 320:UKV0 + (part + 1) * 320],
                                                  start=True, stop=True)
                    mm.then_inc(mla_ready, 1)
                    pe.wait_ge(gelu_ready, 1)
                    for g in range(NSA_G):
                        nc.tensor.matmul(banks[g * HD:(g + 1) * HD, 0, BANK // 2:BANK // 2 + N_CMP], small[:, W2K0:W2K0 + HD],
                                         gelu[:, 3, g * N_CMP:(g + 1) * N_CMP], start=True, stop=True)
                    for g in range(NSA_G):
                        mm = nc.tensor.matmul(banks[0:N_CMP, 0, 128 + g * HD:128 + (g + 1) * HD],
                                              gelu[:, 3, NC2 + g * N_CMP:NC2 + (g + 1) * N_CMP],
                                              small[:, W2V0:W2V0 + HD], start=True, stop=True)
                    mm.then_inc(cmp_ready, 1)
                    pe.wait_ge(cmp_ready, 1)
                    pe.sem_inc(half_used, 1)
                    advance(adapt_products(pe, layer, 3, 4, 7, None))
                    advance(adapt_products(pe, layer, 4, 6, 7, row_copied))

                @block.vector
                def _(dve):
                    step = InOrder(dve, dve_step)
                    for kv in range(2):
                        tok = k2[:, kv, :, :].rearrange("p g (m e) -> p e g m", e=8)
                        for half in range(2):
                            last = nc.vector.tensor_tensor(
                                flat[:, kv, half * 8:half * 8 + 8, :, :], tok[:, :, :, half:half + N_CMP],
                                pos_of[kv][:, half * 8:half * 8 + 8].unsqueeze(2).unsqueeze(3).broadcast_to(
                                    [P, 8, NSA_G, N_CMP]), ALU.add)
                    last.then_inc(flat_ready, 1)
                    dve.wait_ge(hidden_ready, 1)
                    step(nc.vector.tensor_copy(gelu[:, 0, :], banks[:, 0, 0:2 * NC2]))
                    step(nc.vector.tensor_tensor(gelu[:, 1, :], gelu[:, 0, :], gelu[:, 0, :], ALU.mult))
                    step(nc.vector.tensor_scalar(gelu[:, 1, :], gelu[:, 1, :], 0.044715, 1.0, ALU.mult, ALU.add))
                    nc.vector.tensor_tensor(gelu[:, 1, :], gelu[:, 1, :], gelu[:, 0, :], ALU.mult).then_inc(inner_ready, 1)
                    dve.wait_ge(tanh_ready, 1)
                    step(nc.vector.scalar_tensor_tensor(out=gelu[:, 3, :], in0=gelu[:, 2, :], scalar=1.0,
                                                        in1=gelu[:, 0, :], op0=ALU.add, op1=ALU.mult))
                    nc.vector.tensor_scalar(gelu[:, 3, :], gelu[:, 3, :], 0.5, None, ALU.mult).then_inc(gelu_ready, 1)
                    dve.wait_ge(act_copied, 1)
                    q4 = mla_q.rearrange("p t (h d) -> p t h d", h=MLA_H)
                    a, b = ROPE_M
                    rope(dve, step, q4[:, :, :, MLA_NOPE:MLA_QK], cosT[:, :, a:b], sinT[:, :, a:b], b - a, temps)
                    k4 = mla_k.rearrange("p t (h d) -> p t h d", h=MLA_H)
                    for t in range(TT):
                        nc.vector.tensor_copy(k4[:, t, :, MLA_NOPE:MLA_QK],
                                              proj[:, t, KPE0:KPE0 + MLA_PE].unsqueeze(1).broadcast_to(
                                                  [P, MLA_H, MLA_PE]))
                    dve.wait_ge(cmp_ready, 1)
                    nc.vector.tensor_copy(kcT[:], banks[:, 0, BANK // 2:BANK // 2 + N_CMP])
                    nc.vector.tensor_copy(vc[:, :, :].rearrange("p g d -> p (g d)"), banks[0:N_CMP, 0, 128:256])

                @block.scalar
                def _(act):
                    act.wait_ge(inner_ready, 1)
                    nc.scalar.activation(gelu[:, 2, :], gelu[:, 1, :], ACT.Tanh,
                                         scale=float(np.sqrt(2 / np.pi))).then_inc(tanh_ready, 1)
                    act.wait_ge(mla_ready, 1)
                    for t in range(TT):
                        last = nc.scalar.copy(mla_q[:, t, :], banks[:, 1 + t, 0:480])
                    last.then_inc(act_copied, 1)
                    for t in range(TT):
                        nc.scalar.copy(mla_k[:, t, :].rearrange("p (h d) -> p h d", h=MLA_H)[:, :, 0:MLA_NOPE],
                                       banks[:, 3 + t, 0:320].rearrange("p (h d) -> p h d", h=MLA_H))
                        nc.scalar.copy(mla_v[:, t, :], banks[:, 5 + t, 0:320])
                    copy_adapted(act, layer, 1, 7).then_inc(row_copied, 1)
                    copy_adapted(act, layer, 2, 7)

        def compressed_attention(layer, fT, kcT, vc, cmp_add, cmp_keep, branch, four):
            N = NSA_H * TT
            jobs = [(pair, g, t) for g in range(NSA_G) for pair in range(3) for t in range(TT)]
            NG = N // NSA_G
            s, p = (four[:, i, 0:N * N_CMP].rearrange("p (j n) -> p j n", j=N) for i in range(2))
            pT = mixed[0:N_CMP, 2:4, :].rearrange("p a b -> p (a b)")
            s4 = s.rearrange("p (a t) n -> p a t n", t=TT)
            p4 = p.rearrange("p (a t) n -> p a t n", t=TT)

            def table(m):
                return m[:, :].rearrange("p (t n) -> p t n", t=TT)[:, :, 0:N_CMP].unsqueeze(1).broadcast_to(
                    [P, NSA_H, TT, N_CMP])

            def turned(j):
                return pT[:, j * P:(j + 1) * P]

            with stage("scores_ready", "dve_step", "shifted", "exp_ready", "probs_ready", "probs_turned", "copied",
                       "values_ready", "row_copied") as (
                    scores_ready, dve_step, shifted, exp_ready, probs_ready, probs_turned, copied,
                    values_ready, row_copied), nc.Block() as block:
                @block.sync
                def _(sp):
                    load_behind(sp, ("adapt3", layer), 2)

                @block.tensor
                def _(pe):
                    for j, (pair, g, t) in enumerate(jobs):
                        mm = nc.tensor.matmul(banks[:, 7 * g, (j - g * NG) * N_CMP:(j - g * NG + 1) * N_CMP],
                                              fT[g * HD:(g + 1) * HD, pair, t * P:(t + 1) * P],
                                              kcT[g * HD:(g + 1) * HD, :], start=True, stop=True)
                    mm.then_inc(scores_ready, 1)
                    advance(adapt_products(pe, layer, 6, 8, 6, None))
                    second_slab = adapt_products(pe, layer, 8, 10, 6, row_copied)
                    pe.wait_ge(probs_ready, 1)
                    for j in range(N):
                        mm = nc.tensor.transpose(banks[0:N_CMP, 1 + j // 4, (j % 4) * P:(j % 4 + 1) * P],
                                                 p[:, j, :], ident[:])
                    mm.then_inc(probs_turned, 1)
                    advance(second_slab, 2)
                    pe.wait_ge(copied, 1)
                    for j, (pair, g, t) in enumerate(jobs):
                        mm = nc.tensor.matmul(banks[:, 4 + j // 8, (j % 8) * HD:(j % 8 + 1) * HD],
                                              turned(j), vc[:, g, :], start=True, stop=True)
                    mm.then_inc(values_ready, 1)
                    advance(second_slab)

                @block.vector
                def _(dve):
                    step = InOrder(dve, dve_step)
                    dve.wait_ge(scores_ready, 1)
                    for g in range(NSA_G):
                        last = nc.vector.tensor_scalar(
                            s[:, g * NG:(g + 1) * NG, :],
                            banks[:, 7 * g, 0:NG * N_CMP].rearrange("p (j n) -> p j n", j=NG), HD ** -0.5, None, ALU.mult)
                    step(last)
                    step(nc.vector.tensor_tensor(s4, s4, table(cmp_add), ALU.add))
                    step(nc.vector.tensor_reduce(sums[:, 0:N], s, AX.X, ALU.max))
                    nc.vector.tensor_tensor(s, s, sums[:, 0:N].unsqueeze(2).broadcast_to([P, N, N_CMP]),
                                            ALU.subtract).then_inc(shifted, 1)
                    dve.wait_ge(exp_ready, 1)
                    step(nc.vector.tensor_tensor(p4, p4, table(cmp_keep), ALU.mult))
                    step(nc.vector.tensor_reduce(sums[:, 0:N], p, AX.X, ALU.add))
                    step(nc.vector.tensor_scalar(sums[:, 0:N], sums[:, 0:N], 1e-30, None, ALU.max))
                    step(nc.vector.reciprocal(sums[:, 16:16 + N], sums[:, 0:N]))
                    nc.vector.tensor_tensor(p, p, sums[:, 16:16 + N].unsqueeze(2).broadcast_to([P, N, N_CMP]),
                                            ALU.mult).then_inc(probs_ready, 1)
                    dve.wait_ge(probs_turned, 1)
                    nc.vector.tensor_copy(pT[:, 0:3 * BANK].rearrange("p (b n) -> p b n", b=3),
                                          banks[0:N_CMP, 1:4, :]).then_inc(copied, 1)
                    dve.wait_ge(values_ready, 1)
                    for j, (pair, g, t) in enumerate(jobs):
                        head = NSA_PAIRS[pair][g]
                        nc.vector.tensor_scalar(mixed[:, t, head * HD:(head + 1) * HD],
                                                banks[:, 4 + j // 8, (j % 8) * HD:(j % 8 + 1) * HD],
                                                branch[:, 0, t * 18 + head * 3:t * 18 + head * 3 + 1], None, ALU.mult)

                @block.scalar
                def _(act):
                    act.wait_ge(shifted, 1)
                    nc.scalar.activation(p, s, ACT.Exp).then_inc(exp_ready, 1)
                    copy_adapted(act, layer, 3, 6).then_inc(row_copied, 1)
                    copy_adapted(act, layer, 4, 6)

        def retain(layer, proj, fT, decay, gn_gain, four):
            heads = [(fT[0:HD, 3, :], fT[0:HD, 5, :]), (fT[HD:P, 3, :], fT[HD:P, 5, :]),
                     (fT[0:HD, 4, :], fT[0:HD, 6, :]), (fT[HD:P, 4, :], fT[HD:P, 6, :]),
                     (fT[0:HD, 7, :], fT[0:HD, 8, :])]
            N = TT * RET_H

            def faded_of(h):
                return four[:, h, 0:3 * P] if h < 4 else mixed[:, 2, 0:3 * P]

            with stage("scores_ready", "faded_ready", "values_ready", "dve_step", "sums_ready", "rstd_ready",
                       "pool_step") as (
                    scores_ready, faded_ready, values_ready, dve_step, sums_ready, rstd_ready, pool_step), \
                    nc.Block() as block:
                @block.sync
                def _(sp):
                    load_behind(sp, ("adapt5", layer), 1)

                @block.scalar
                def _(act):
                    copy_adapted(act, layer, 5, 7)

                @block.tensor
                def _(pe):
                    for h, (qT, kT) in enumerate(heads):
                        nc.tensor.matmul(banks[:, h, 0:SEQ], kT[:, 0:P], qT[:, 0:SEQ], start=True, stop=True)
                        nc.tensor.matmul(banks[:, h, SEQ:SEQ + P], kT[:, P:SEQ], qT[:, P:SEQ],
                                         start=True, stop=True).then_inc(scores_ready, 1)
                    for h in range(RET_H):
                        pe.wait_ge(faded_ready, h + 1)
                        v = [proj[:, t, RV0 + h * HD:RV0 + (h + 1) * HD] for t in range(TT)]
                        f = faded_of(h)
                        nc.tensor.matmul(banks[:, 5, h * HD:(h + 1) * HD], f[:, 0:P], v[0], start=True, stop=True)
                        accumulate(banks[:, 6, h * HD:(h + 1) * HD],
                                   [(f[:, P:2 * P], v[0]), (f[:, 2 * P:3 * P], v[1])]).then_inc(values_ready, 1)
                    advance(adapt_products(pe, layer, 10, 12, 7, None))

                @block.vector
                def _(dve):
                    step = InOrder(dve, dve_step)
                    for h in range(RET_H):
                        dve.wait_ge(scores_ready, h + 1)
                        nc.vector.tensor_tensor(faded_of(h), banks[:, h, 0:3 * P], decay[:, h, :],
                                                ALU.mult).then_inc(faded_ready, 1)
                    dve.wait_ge(values_ready, RET_H)
                    o3 = mixed[:, 0:TT, 704:1024]
                    for t in range(TT):
                        last = nc.vector.tensor_copy(o3[:, t, :], banks[:, 5 + t, 0:320])
                    step(last)
                    o = o3.rearrange("p t (h d) -> p t h d", h=RET_H)
                    sq = mixed[:, 3, 0:TT * 320].rearrange("p (t h d) -> p t h d", t=TT, h=RET_H)

                    def per_head(a):
                        return a.rearrange("p (t h) -> p t h", t=TT).unsqueeze(3).broadcast_to([P, TT, RET_H, HD])

                    m3 = sums[:, 0:N].rearrange("p (t h) -> p t h", t=TT)
                    step(nc.vector.tensor_reduce(m3, o, AX.X, ALU.add))
                    step(nc.vector.tensor_scalar(sums[:, 0:N], sums[:, 0:N], 1.0 / HD, None, ALU.mult))
                    step(nc.vector.tensor_tensor(o, o, per_head(sums[:, 0:N]), ALU.subtract))
                    step(nc.vector.tensor_tensor(sq, o, o, ALU.mult))
                    nc.vector.tensor_reduce(sums[:, 16:16 + N].rearrange("p (t h) -> p t h", t=TT), sq, AX.X,
                                            ALU.add).then_inc(sums_ready, 1)
                    dve.wait_ge(rstd_ready, 1)
                    step(nc.vector.tensor_tensor(o, o, per_head(rstd[:, 0:N]), ALU.mult))
                    step(nc.vector.tensor_tensor(o3, o3, gn_gain[:].unsqueeze(1).broadcast_to([P, TT, 320]), ALU.mult))
                    nc.vector.tensor_tensor(o3, o3, proj[:, 0:TT, RG0:RG0 + 320], ALU.mult)

                @block.gpsimd
                def _(pool):
                    step = InOrder(pool, pool_step)
                    pool.wait_ge(sums_ready, 1)
                    step(nc.gpsimd.tensor_scalar(rstd[:, 0:N], sums[:, 16:16 + N], 1.0 / HD, EPS, ALU.mult, ALU.add))
                    nc.gpsimd.tensor_tensor(rstd[:, 0:N], rstd[:, 0:N], minus_half[:, 0:N], ALU.pow).then_inc(rstd_ready, 1)

        def turn_mixed(turned_y, T):
            hi, lo = turned_y
            per = 4 // T
            n_groups = KC // per
            with stage("turned", "high_ready") as (turned, high_ready), nc.Block() as block:
                @block.tensor
                def _(pe):
                    for g in range(n_groups):
                        for j in range(4):
                            k, t = g * per + j // T, j % T
                            mm = nc.tensor.transpose(banks[:, g, j * P:(j + 1) * P], mixed[:, t, k * P:(k + 1) * P],
                                                     ident[:])
                        mm.then_inc(turned, 1)

                @block.scalar
                def _(act):
                    for g in range(n_groups):
                        act.wait_ge(turned, g + 1)
                        nc.scalar.copy(hi[:, g * per:(g + 1) * per, 0:T * P],
                                       banks[:, g, :].rearrange("p (k s) -> p k s", k=per)).then_inc(high_ready, 1)

                @block.vector
                def _(dve):
                    for g in range(n_groups):
                        dve.wait_ge(high_ready, g + 1)
                        k = slice(g * per, (g + 1) * per)
                        nc.vector.tensor_tensor(lo[:, k, 0:T * P], banks[:, g, :].rearrange("p (k s) -> p k s", k=per),
                                                hi[:, k, 0:T * P].bitcast(F32), ALU.subtract)

        def feed_forward(layer, sb2, hidden):
            hi, lo = hidden
            key = ("ffn", layer)
            relu, square = sb2("relu", [P, 4, SEQ]), sb2("square", [P, 4, SEQ])
            u_hi, u_lo = (sb2(n, [P, 2, 4, SEQ], F32R) for n in ("u_hi", "u_lo"))

            def hidden_banks(g):
                return banks[:, 2 * (g % 2):2 * (g % 2) + 2, :].rearrange("p b (f s) -> p (b f) s", f=2)

            with stage("relu_ready", "square_ready", "high_ready", "u_ready") as (
                    relu_ready, square_ready, high_ready, u_ready), nc.Block() as block:
                @block.sync
                def _(sp):
                    load_behind(sp, key, 2 * FFN_GROUPS)

                @block.tensor
                def _(pe):
                    def up(i, g):
                        if g >= 2:
                            pe.wait_ge(relu_ready, g - 1)
                        for q in range(4):
                            pe.wait_ge(part_ready, first_part[key] + 4 * i + q + 1)
                            wh, wl = part(key, 4 * i + q)
                            for kk in range(2):
                                k = 2 * q + kk
                                for f in range(4):
                                    cols = slice(f * P, (f + 1) * P)
                                    mm = multiply(banks[:, 2 * (g % 2) + f // 2, (f % 2) * SEQ:(f % 2 + 1) * SEQ],
                                                  (wh[:, kk, cols], wl[:, kk, cols]), (hi[:, k, :], lo[:, k, :]),
                                                  k == 0 and f % 2 == 0, k == KC - 1, shares_bank=True)
                            mm.then_inc(part_used, 1)

                    def down(i, g):
                        pe.wait_ge(u_ready, g + 1)
                        for q in range(4):
                            pe.wait_ge(part_ready, first_part[key] + 4 * i + q + 1)
                            wh, wl = [w.rearrange("p k n -> p (k n)") for w in part(key, 4 * i + q)]
                            for t in range(TT):
                                tok = slice(t * P, (t + 1) * P)
                                for n in range(2):
                                    cols = slice(n * BANK, (n + 1) * BANK)
                                    mm = multiply(banks[:, 4 + 2 * t + n, :],
                                                  (u_hi[:, g % 2, q, tok], u_lo[:, g % 2, q, tok]),
                                                  (wh[:, cols], wl[:, cols]), g == 0 and q == 0,
                                                  g == FFN_GROUPS - 1 and q == 3)
                            mm.then_inc(part_used, 1)

                    for i, (name, g) in enumerate(FFN_ORDER):
                        (up if name == "w_up" else down)(i, g)

                @block.scalar
                def _(act):
                    def activate(i, g):
                        products_done(act, key, i)
                        if g >= 1:
                            act.wait_ge(square_ready, g)
                        nc.scalar.activation(relu[:], hidden_banks(g), ACT.Relu).then_inc(relu_ready, 1)
                        act.wait_ge(square_ready, g + 1)
                        nc.scalar.copy(u_hi[:, g % 2, :, :], square[:]).then_inc(high_ready, 1)

                    for i in range(2 * FFN_GROUPS):
                        for q in range(PARTS):
                            split_hi(act, key, 4 * i + q)
                        if i >= 1 and FFN_ORDER[i - 1][0] == "w_up":
                            activate(i - 1, FFN_ORDER[i - 1][1])
                        split_hi(act, key, 4 * i + PARTS)

                @block.vector
                def _(dve):
                    def activate(g):
                        dve.wait_ge(relu_ready, g + 1)
                        nc.vector.tensor_tensor(square[:], relu[:], relu[:], ALU.mult).then_inc(square_ready, 1)
                        dve.wait_ge(high_ready, g + 1)
                        nc.vector.tensor_tensor(u_lo[:, g % 2, :, :], square[:], u_hi[:, g % 2, :, :].bitcast(F32),
                                                ALU.subtract).then_inc(u_ready, 1)

                    for i in range(2 * FFN_GROUPS):
                        for q in range(PARTS):
                            split_lo(dve, key, 4 * i + q)
                        if i >= 1 and FFN_ORDER[i - 1][0] == "w_up":
                            activate(FFN_ORDER[i - 1][1])
                        split_lo(dve, key, 4 * i + PARTS)
                    products_done(dve, key, 2 * FFN_GROUPS - 1)
                    for t in range(TT):
                        for n in range(2):
                            here = x[:, t, n * BANK:(n + 1) * BANK]
                            nc.vector.tensor_tensor(here, banks[:, 4 + 2 * t + n, :], here, ALU.add)

        def final_norm(gain_dram, store):
            with stage("gain_here", "squares_summed", "pool_step", "rstd_ready", "normed", "turned",
                       "ada_ready") as (
                    gain_here, squares_summed, pool_step, rstd_ready, normed, turned, ada_ready), nc.Block() as block:
                gain = mixed[:, 2, :]

                @block.tensor
                def _(pe):
                    if not store:
                        turn_conditions(pe, turned)

                @block.sync
                def _(sp):
                    sp.dma_start(gain, gain_dram.broadcast_to([P, D])).then_inc(gain_here, 16)
                    if store:
                        for t in range(TT):
                            sp.wait_ge(normed, t + 1)
                            sp.dma_start(out[0, t * P:(t + 1) * P, :], x[:, t, :]).then_inc(stored, 16)
                        sp.wait_ge(stored, 16 * TT)

                @block.vector
                def _(dve):
                    for t in range(TT):
                        nc.vector.tensor_tensor_reduce(mixed[:, t, :], x[:, t, :], x[:, t, :], 1.0, 0.0, ALU.mult,
                                                       ALU.add, sums[:, t:t + 1]).then_inc(squares_summed, 1)
                    dve.wait_ge(rstd_ready, 1)
                    dve.wait_ge(gain_here, 16)
                    for t in range(TT):
                        nc.vector.scalar_tensor_tensor(out=x[:, t, :], in0=x[:, t, :], scalar=rstd[:, t:t + 1],
                                                       in1=gain, op0=ALU.mult, op1=ALU.mult).then_inc(normed, 1)
                    if not store:
                        add_biases(dve, turned, ada_ready)

                @block.gpsimd
                def _(pool):
                    step = InOrder(pool, pool_step)
                    pool.wait_ge(squares_summed, TT)
                    step(nc.gpsimd.tensor_scalar(rstd[:, 0:TT], sums[:, 0:TT], 1.0 / D, EPS, ALU.mult, ALU.add))
                    nc.gpsimd.tensor_tensor(rstd[:, 0:TT], rstd[:, 0:TT], minus_half[:, 0:TT],
                                            ALU.pow).then_inc(rstd_ready, 1)

        def second_block():
            with ExitStack() as local:
                def sb(name, shape, dt=F32):
                    return local.enter_context(nc.sbuf_tensor(name, shape, dt))

                nmax2, total2, inverse2 = (sb(n, [P, 6, 2]) for n in ("nmax2", "total2", "inverse2"))
                sums2 = (nmax2, total2, inverse2)
                conv_b = feats2[:, 32:36]
                sc = [[scales[:, kind, v, :] for v in range(2)] for kind in range(2)]
                sh = [[ada[:, kind, 0:8, v] for v in range(2)] for kind in range(2)]

                with scope("ab") as sb2:
                    proj = sb2("proj", [P, 4, AB_N])
                    conv_w = sb2("conv_w", [P, 4, CONV_W])
                    uT = sb2("uT", [P, 4, 2, SEQ + 2 * CONV_PAD])
                    head_gains = sb2("head_gains", [P, 2 * HD])
                    axial = sb2("axial", [P, 2, TT, HD // 2])
                    with scope("ab") as sb3:
                        hidden = [sb3(n, [P, KC, 2 * SEQ], F32R) for n in ("h_hi", "h_lo")]
                        normalize_transpose(hidden, (0, 1, 2, 3), sc[0], sh[0])
                        project_and_convolve("ab_in", hidden, proj, uT, conv_w, conv_b, head_gains, axial)
                    with scope("ab_heads") as sb3:
                        prepare_axial_heads(proj, head_gains, axial, sb3("four", [P, 4 * 640]))
                    hT = sb2("heads_T", [P, 4, 2 * SEQ])
                    k_padded = sb2("k_padded", [P, B_KV, 2 * SEQ])
                    groups = [([proj[:, t, AB_Q0 + i * P:AB_Q0 + (i + 1) * P] for t in range(4)],
                               [lambda engine, bank, i=i: copy_out(engine, hT[:, i, :], bank)]) for i in range(4)]
                    groups.append(([proj[:, t, AB_K0:AB_K0 + P] for t in range(4)],
                                   [lambda engine, bank, kv=kv: copy_out(engine, k_padded[kv * HD:(kv + 1) * HD, kv, :],
                                                                         bank[kv * HD:(kv + 1) * HD, :])
                                    for kv in range(B_KV)]))
                    transpose_groups(groups, k_padded)
                    units = []
                    for h in range(B_HEADS):
                        kv, i = h // 4, h % 4
                        vs = [proj[:, t, AB_V0 + kv * HD:AB_V0 + (kv + 1) * HD] for t in range(4)]
                        for t in range(TT):
                            units.append({"rows": [(hT[:, i, t * P:(t + 1) * P], k_padded[:, kv, :], 0, BANK, vs)],
                                          "width": BANK, "mask": None, "weigh": plain_weigh(BANK + h * HD, (t,))})
                        units.append({"rows": [(hT[:, i, t * P:(t + 1) * P], k_padded[:, kv, SEQ:2 * SEQ],
                                                (t - 2) * SEQ, SEQ, vs[2:4]) for t in (2, 3)],
                                      "width": BANK, "mask": None, "weigh": plain_weigh(BANK + h * HD, (2, 3))})
                    ln_rows = sb2("ln_rows", [P, 2 * BANK])
                    with scope("ab_attend") as sb3:
                        attend(units, (sb3("probs", [P, 3, BANK]), sb3("probsT", [P, 2, BANK])) + sums2,
                               lambda done: convolution_taps(uT, conv_w, conv_b, TAPS_WITH_SLABS, None, done, None),
                               lambda step: pool_taps(step, uT, conv_w, conv_b, POOL_TAPS_WITH_SLABS, CONV_W))
                    with scope("ab_finish") as sb3:
                        finish_conv_and_gate(proj, ln_rows, sb3("tanh_y", [P, 4, BANK]), sb3("tanh_z", [P, 4, D]))
                with scope("ab_out") as sb2:
                    turned_y = [sb2(n, [P, KC, 2 * SEQ], F32R) for n in ("y_hi", "y_lo")]
                    turn_mixed(turned_y, 4)
                    out_project("ab_out", turned_y, (0, 1, 2, 3), [gate_rows[:, v, :] for v in range(2)])

                both, own = (0, 1, 2, 3), (0, 1)
                with scope("cd") as sb2:
                    proj = sb2("proj", [P, 4, CD_N])
                    with scope("cd") as sb3:
                        hidden = [sb3(n, [P, KC, 2 * SEQ], F32R) for n in ("h_hi", "h_lo")]
                        normalize_transpose(hidden, both, sc[1], sh[1])
                        project("cd_in", hidden, [BANK] * 6, [own, own, both, both, own, own], proj)
                    kT = sb2("kT", [P, 4, 2 * SEQ])
                    q_padded = sb2("q_padded", [P, D_HEADS // 2, 2, SEQ])
                    wf = sb2("wf", [P, C_GROUPS, P])
                    dft_c = sb2("dft_c", [P, 2 * P])
                    dft_t = sb2("dft_t", [P, 2, TT, SEQ])
                    with scope("cd_fourier") as sb3:
                        fgT = sb3("fgT", [P, C_GROUPS, SEQ])
                        groups = []
                        for i in (0, 2):
                            groups.append(([proj[:, t, CD_Q0 + k * P:CD_Q0 + (k + 1) * P] for k in (i, i + 1) for t in own],
                                           [lambda engine, bank, i=i, g=g: copy_out(
                                               engine, q_padded[g * HD:(g + 1) * HD, i:i + 2, g, :],
                                               bank[g * HD:(g + 1) * HD, :].rearrange("p (k s) -> p k s", k=2),
                                               HD ** -0.5) for g in range(2)]))
                            groups.append(([proj[:, t, CD_F0 + k * P:CD_F0 + (k + 1) * P] for k in (i, i + 1) for t in own],
                                           [lambda engine, bank, i=i: copy_out(
                                               engine, fgT[:, i:i + 2, :],
                                               bank.rearrange("p (k s) -> p k s", k=2))]))
                        for i in range(4):
                            groups.append(([proj[:, t, CD_K0 + i * P:CD_K0 + (i + 1) * P] for t in both],
                                           [lambda engine, bank, i=i: copy_out(engine, kT[:, i, :], bank)]))
                        transpose_groups(groups, q_padded)
                        fourier(fgT, wf, dft_c, dft_t, sb3)

                    def bias_of(t, h, n=1):
                        i = t * D_HEADS + h
                        c0 = (CD_F0, CD_Z0)[i // 8] + (i % 4) * SEQ
                        return proj[:, 2 + i // 4 % 2, c0:c0 + n * SEQ]

                    relative_bias(bias_of, onehot, rpb, col_mask)
                    units = []
                    for h in range(D_HEADS):
                        vs = [proj[:, t, CD_V0 + h * HD:CD_V0 + (h + 1) * HD] for t in both]
                        for t in own:
                            units.append({"rows": [(q_padded[:, h // 2, h % 2, t * P:(t + 1) * P], kT[:, h // 2, :],
                                                    0, BANK, vs)],
                                          "width": BANK, "scale": 1.0, "mask": bias_of(t, h),
                                          "weigh": plain_weigh(BANK + h * HD, (t,))})
                    with scope("cd_attend") as sb3:
                        attend(units, (sb3("probs", [P, 3, BANK]), sb3("probsT", [P, 2, BANK])) + sums2)
                    gate_by_z(proj, 2, CD_Z0)
                with scope("cd_out") as sb2:
                    turned_y = [sb2(n, [P, KC, SEQ], F32R) for n in ("y_hi", "y_lo")]
                    turn_mixed(turned_y, 2)
                    out_project("cd_out", turned_y, own, [gate_rows[:, 0, :]])

        def turn_conditions(pe, turned):
            for kind in range(2):
                rows = slice(HD * kind, HD * kind + 2)
                for f in range(24):
                    mm = nc.tensor.transpose(banks[:, kind, 2 * f:2 * f + 2], ada_rows[rows, f * P:(f + 1) * P],
                                             ident[rows, rows])
                mm.then_inc(turned, 1)

        def add_biases(dve, turned, ada_ready):
            for kind, (b0, g0) in enumerate(((0, 24), (36, 60))):
                dve.wait_ge(turned, kind + 1)
                nc.vector.tensor_tensor(ada[:, kind, :, :], banks[:, kind, 0:48].rearrange("p (f v) -> p f v", v=2),
                                        feats2[:, b0:b0 + 24].unsqueeze(2).broadcast_to([P, 24, 2]),
                                        ALU.add).then_inc(ada_ready, 1)
                dve.wait_ge(ada_ready, kind + 1)
                for v in range(2):
                    nc.vector.scalar_tensor_tensor(out=scales[:, kind, v, :], in0=ada[:, kind, 8:16, v],
                                                   scalar=1.0, in1=feats2[:, g0:g0 + KC], op0=ALU.add, op1=ALU.mult)

        def spread_gates(pe, kind, n_gates, rows_ready):
            for v in range(n_gates):
                for c in range(KC):
                    mm = nc.tensor.matmul(banks[:, 2 * v + c // 4, (c % 4) * P:(c % 4 + 1) * P],
                                          ada[:, kind, 16 + c, v:v + 1].broadcast_to([P, P]), ident[:],
                                          start=True, stop=True)
                mm.then_inc(rows_ready, 1)

        def copy_gates(act, n_gates, rows_ready):
            for v in range(n_gates):
                act.wait_ge(rows_ready, v + 1)
                nc.scalar.copy(gate_rows[:, v, :].rearrange("p (b n) -> p b n", b=2), banks[:, 2 * v:2 * v + 2, :])

        def convolution_taps(uT, conv_w, conv_b, first_tap, last_tap, done, uT_ready):
            dve = nc.vector
            order = [(j, c) for j in range(CONV_W) for c in range(3)]
            for n, (j, c) in list(enumerate(order))[first_tap:last_tap]:
                if j == 0:
                    dve.wait_ge(uT_ready, c + 1)
                elif n - 3 >= first_tap:
                    dve.wait_ge(done, n - 3 - first_tap + 1)
                tap = uT[:, c, :, j:j + SEQ]
                if j == 0:
                    ins = dve.tensor_scalar(convolved(c), tap, conv_w[:, c, 0:1], conv_b[:, c:c + 1], ALU.mult, ALU.add)
                else:
                    ins = dve.scalar_tensor_tensor(out=convolved(c), in0=tap, scalar=conv_w[:, c, j:j + 1],
                                                   in1=convolved(c), op0=ALU.mult, op1=ALU.add)
                ins.then_inc(done, 1)
                yield

        def convolved(c):
            return mixed[:, c, 0:BANK].rearrange("p (s n) -> p s n", s=2)

        def pool_taps(step, uT, conv_w, conv_b, j0, j1):
            product = ada_rows[:, 2 * D:2 * D + BANK].rearrange("p (s n) -> p s n", s=2)
            for j in range(j0, j1):
                tap, w = uT[:, 3, :, j:j + SEQ], conv_w[:, 3, j:j + 1]
                if j == 0:
                    step(nc.gpsimd.tensor_scalar(convolved(3), tap, w, conv_b[:, 3:4], ALU.mult, ALU.add))
                else:
                    step(nc.gpsimd.tensor_scalar(product, tap, w, None, ALU.mult))
                    step(nc.gpsimd.tensor_tensor(convolved(3), convolved(3), product, ALU.add))

        def project_and_convolve(key, hidden, proj, uT, conv_w, conv_b, head_gains, axial):
            n_slabs = -(-AB_N // BANK)
            widths = [min(BANK, AB_N - s * BANK) for s in range(n_slabs)]
            tiles = range(4)
            TURN_AT = 3
            H = B_HEADS + B_KV
            HEADS_A_PART = 8
            with stage("evacuated", "tanh_ready", "glu_ready", "glu_turned", "uT_ready", "zeroed", "tap_done",
                       "weights_here", "tables_here", "sums_ready", "pool_step") as (
                    evacuated, tanh_ready, glu_ready, glu_turned, uT_ready, zeroed, tap_done,
                    weights_here, tables_here, sums_ready, pool_step), \
                    nc.sbuf_tensor("head_squares", [P, HD], F32) as squares, nc.Block() as block:
                @block.sync
                def _(sp):
                    sp.dma_start(conv_w[:], dram["conv_w"]).then_inc(weights_here, 16)
                    sp.dma_start(head_gains[:], dram["rows"][:, 2 * BANK:2 * BANK + 2 * HD].broadcast_to([P, 2 * HD])
                                 ).then_inc(tables_here, 16)
                    sp.dma_start(axial[:], dram["axial"]).then_inc(tables_here, 16)
                    load_behind(sp, key, n_slabs)
                    sp.wait_ge(tables_here, 32)

                @block.gpsimd
                def _(pool):
                    nc.gpsimd.memset(uT[:], 0.0).then_inc(zeroed, 1)
                    pool.wait_ge(weights_here, 16)
                    pool.wait_ge(uT_ready, 4)
                    step = InOrder(pool, pool_step)
                    pool_taps(step, uT, conv_w, conv_b, 0, POOL_TAPS_WITH_SLABS)
                    pool.wait_ge(sums_ready, 4 * H)
                    step(nc.gpsimd.tensor_scalar(rstd[:, 0:4 * H], sums[:, 0:4 * H], 1.0 / HD, EPS, ALU.mult, ALU.add))
                    step(nc.gpsimd.tensor_tensor(rstd[:, 0:4 * H], rstd[:, 0:4 * H], minus_half[:, 0:4 * H], ALU.pow))
                    q = rstd[:, 0:4 * H].rearrange("p (t h) -> p t h", t=4)[:, :, 0:B_HEADS]
                    nc.gpsimd.tensor_scalar(q, q, HD ** -0.5, None, ALU.mult)

                @block.tensor
                def _(pe):
                    for s in range(n_slabs):
                        if s >= 2:
                            pe.wait_ge(evacuated, 4 * (s - 1))
                        if s == TURN_AT:
                            pe.wait_ge(glu_ready, 4)
                            for c in range(4):
                                for t in tiles:
                                    mm = nc.tensor.transpose(banks[:, 4 * (s % 2) + c, t * P:(t + 1) * P],
                                                             mixed[:, t, BANK + c * P:BANK + (c + 1) * P], ident[:])
                                mm.then_inc(glu_turned, 1)
                            pe.wait_ge(uT_ready, 4)
                        multiply_slab(pe, key, s, hidden, widths[s], tiles)

                @block.scalar
                def _(act):
                    def copy_products(s):
                        products_done(act, key, s)
                        for t in tiles:
                            nc.scalar.copy(proj[:, t, s * BANK:s * BANK + widths[s]],
                                           banks[:, 4 * (s % 2) + t, 0:widths[s]]).then_inc(evacuated, 1)
                            if s == 1:
                                act.wait_ge(evacuated, 4 + t + 1)
                                nc.scalar.activation(mixed[:, t, 0:BANK], proj[:, t, AB_GATE0:AB_GATE0 + BANK],
                                                     ACT.Tanh, scale=0.5).then_inc(tanh_ready, 1)

                    for q in range(4 * n_slabs):
                        split_hi(act, key, q)
                        if q >= 5 and q % 4 == 1:
                            copy_products(q // 4 - 1)
                        if q == 4 * TURN_AT + 2:
                            act.wait_ge(zeroed, 1)
                            for c in range(4):
                                act.wait_ge(glu_turned, c + 1)
                                nc.scalar.activation(uT[:, c, :, CONV_PAD:CONV_PAD + SEQ],
                                                     banks[:, 4 * (TURN_AT % 2) + c, :].rearrange(
                                                         "p (s n) -> p s n", s=2),
                                                     ACT.Copy, scale=0.5).then_inc(uT_ready, 1)
                        n0 = (q - 4 * TURN_AT - 6) * HEADS_A_PART
                        for n in range(max(n0, 0), min(n0 + HEADS_A_PART, 4 * H)):
                            c0 = AB_Q0 + n % H * HD
                            nc.scalar.activation(squares[:], proj[:, n // H, c0:c0 + HD], ACT.Square,
                                                 accum_out=sums[:, n:n + 1]).then_inc(sums_ready, 1)
                            act.wait_ge(sums_ready, n + 1)
                    copy_products(n_slabs - 1)

                @block.vector
                def _(dve):
                    more = convolution_taps(uT, conv_w, conv_b, 0, TAPS_WITH_SLABS, tap_done, uT_ready)
                    for q in range(4 * n_slabs):
                        split_lo(dve, key, q)
                        if q == 10:
                            for t in tiles:
                                dve.wait_ge(tanh_ready, t + 1)
                                nc.vector.scalar_tensor_tensor(
                                    out=mixed[:, t, BANK:D], in0=mixed[:, t, 0:BANK], scalar=1.0,
                                    in1=proj[:, t, 0:BANK], op0=ALU.add, op1=ALU.mult).then_inc(glu_ready, 1)
                        if q == 4 * TURN_AT + 2:
                            dve.wait_ge(weights_here, 16)
                        if q >= 4 * TURN_AT + 2:
                            advance(more, 7 if q < 4 * (n_slabs - 1) else 3)
                    advance(more)

        def prepare_axial_heads(proj, gains, axial, flat):
            H = B_HEADS + B_KV
            qk = proj[:, :, AB_Q0:AB_Q0 + H * HD].rearrange("p t (h d) -> p t h d", h=H)
            temps = [flat[:, i * 640:(i + 1) * 640] for i in range(4)]
            with stage("dve_step", "pool_step", "rows_ready") as (dve_step, pool_step, rows_ready), \
                    nc.Block() as block:
                @block.tensor
                def _(pe):
                    spread_gates(pe, 0, 2, rows_ready)

                def scale_heads(engine, step, tiles):
                    here = qk[:, tiles, :, :]
                    T = tiles.stop - tiles.start
                    per_head = rstd[:, tiles.start * H:tiles.stop * H].rearrange("p (t h) -> p t h", t=T).unsqueeze(
                        3).broadcast_to([P, T, H, HD])
                    step(engine.tensor_tensor(here, here, per_head, ALU.mult))
                    for h0, h1, gain in ((0, B_HEADS, gains[:, 0:HD]), (B_HEADS, H, gains[:, HD:2 * HD])):
                        last = engine.tensor_tensor(
                            here[:, :, h0:h1, :], here[:, :, h0:h1, :],
                            gain.unsqueeze(1).unsqueeze(1).broadcast_to([P, T, h1 - h0, HD]), ALU.mult)
                    step(last)

                @block.scalar
                def _(act):
                    copy_gates(act, 2, rows_ready)

                @block.vector
                def _(dve):
                    step = InOrder(dve, dve_step)
                    scale_heads(nc.vector, step, slice(0, 2))
                    rope(dve, step, qk[:, 0:TT, :, :], axial[:, 0, :, :], axial[:, 1, :, :], HD // 2, temps)

                @block.gpsimd
                def _(pool):
                    scale_heads(nc.gpsimd, InOrder(pool, pool_step), slice(2, 4))

        def finish_conv_and_gate(proj, ln_rows, tanh_y, tanh_z):
            y = mixed[:, :, 0:BANK]
            stats, mv = sums[:, 48:72], sums[:, 72:80]
            with stage("rows_here", "turned_back", "stats_ready", "pool_step", "rstd_ready", "tanh_z_ready",
                       "normed", "tanh_y_ready", "dve_step") as (
                    rows_here, turned_back, stats_ready, pool_step, rstd_ready, tanh_z_ready, normed, tanh_y_ready,
                    dve_step), nc.Block() as block:
                @block.sync
                def _(sp):
                    sp.dma_start(ln_rows[:], dram["rows"][:, 0:2 * BANK].broadcast_to([P, 2 * BANK])
                                 ).then_inc(rows_here, 16)

                @block.tensor
                def _(pe):
                    for t in range(4):
                        for c in range(4):
                            mm = nc.tensor.transpose(banks[:, t, c * P:(c + 1) * P],
                                                     mixed[:, c, t * P:(t + 1) * P], ident[:])
                        mm.then_inc(turned_back, 1)

                @block.scalar
                def _(act):
                    for t in range(4):
                        nc.scalar.activation(tanh_z[:, t, :], proj[:, t, AB_Z0:AB_Z0 + D], ACT.Tanh,
                                             scale=0.5).then_inc(tanh_z_ready, 1)
                    for t in range(4):
                        act.wait_ge(normed, t + 1)
                        nc.scalar.activation(tanh_y[:, t, :], y[:, t, :], ACT.Tanh, scale=0.5).then_inc(tanh_y_ready, 1)

                @block.gpsimd
                def _(pool):
                    step = InOrder(pool, pool_step)
                    pool.wait_ge(stats_ready, 1)
                    step(nc.gpsimd.tensor_scalar(rstd[:, 48:52], mv.rearrange("p (t v) -> p t v", v=2)[:, :, 1],
                                                 EPS, None, ALU.add))
                    nc.gpsimd.tensor_tensor(rstd[:, 48:52], rstd[:, 48:52], minus_half[:, 0:4],
                                            ALU.pow).then_inc(rstd_ready, 1)

                @block.vector
                def _(dve):
                    step = InOrder(dve, dve_step)
                    for t in range(4):
                        dve.wait_ge(turned_back, t + 1)
                        last = nc.vector.bn_stats(stats[:, 6 * t:6 * t + 6], banks[:, t, :])
                    step(last)
                    for t in range(4):
                        last = nc.vector.bn_aggr(mv[:, 2 * t:2 * t + 2], stats[:, 6 * t:6 * t + 6])
                    last.then_inc(stats_ready, 1)
                    dve.wait_ge(stats_ready, 1)
                    dve.wait_ge(rows_here, 16)
                    for t in range(4):
                        last = nc.vector.scalar_tensor_tensor(out=y[:, t, :], in0=banks[:, t, :],
                                                              scalar=mv[:, 2 * t:2 * t + 1], in1=ln_rows[:, 0:BANK],
                                                              op0=ALU.subtract, op1=ALU.mult)
                    step(last)
                    dve.wait_ge(rstd_ready, 1)
                    for t in range(4):
                        nc.vector.scalar_tensor_tensor(out=y[:, t, :], in0=y[:, t, :], scalar=rstd[:, 48 + t:49 + t],
                                                       in1=ln_rows[:, BANK:2 * BANK], op0=ALU.mult,
                                                       op1=ALU.add).then_inc(normed, 1)
                    for t in range(4):
                        z = proj[:, t, AB_Z0:AB_Z0 + D]
                        dve.wait_ge(tanh_z_ready, t + 1)
                        last = nc.vector.scalar_tensor_tensor(out=z, in0=tanh_z[:, t, :], scalar=1.0, in1=z,
                                                              op0=ALU.add, op1=ALU.mult)
                    step(last)
                    for t in range(4):
                        dve.wait_ge(tanh_y_ready, t + 1)
                        last = nc.vector.scalar_tensor_tensor(out=y[:, t, :], in0=tanh_y[:, t, :], scalar=1.0,
                                                              in1=y[:, t, :], op0=ALU.add, op1=ALU.mult)
                    step(last)
                    for half, scale in ((0, 0.25), (1, 0.5)):
                        here = mixed[:, :, half * BANK:(half + 1) * BANK]
                        z = proj[:, :, AB_Z0 + half * BANK:AB_Z0 + (half + 1) * BANK]
                        nc.vector.scalar_tensor_tensor(out=here, in0=z, scalar=scale, in1=here, op0=ALU.mult,
                                                       op1=ALU.mult)

        def gate_by_z(proj, T, z0):
            with stage("tanh_ready", "dve_step", "rows_ready") as (tanh_ready, dve_step, rows_ready), \
                    nc.sbuf_tensor(f"tanh_z_{z0}", [P, T, D], F32) as tanh_z, nc.Block() as block:
                @block.scalar
                def _(act):
                    for t in range(T):
                        nc.scalar.activation(tanh_z[:, t, :], proj[:, t, z0:z0 + D], ACT.Tanh,
                                             scale=0.5).then_inc(tanh_ready, 1)
                    copy_gates(act, 1, rows_ready)

                @block.tensor
                def _(pe):
                    spread_gates(pe, 1, 1, rows_ready)

                @block.vector
                def _(dve):
                    step = InOrder(dve, dve_step)
                    for t in range(T):
                        z = proj[:, t, z0:z0 + D]
                        dve.wait_ge(tanh_ready, t + 1)
                        step(nc.vector.scalar_tensor_tensor(out=z, in0=tanh_z[:, t, :], scalar=1.0, in1=z,
                                                            op0=ALU.add, op1=ALU.mult))
                        nc.vector.scalar_tensor_tensor(out=mixed[:, t, :], in0=z, scalar=0.5, in1=mixed[:, t, :],
                                                       op0=ALU.mult, op1=ALU.mult)

        def fourier(fgT, wf, dft_c, dft_t, sb3):
            channels = sb3("channels", [P, C_GROUPS, TT, 2 * P])
            frT = sb3("frT", [P, C_GROUPS, SEQ])
            with stage("tables_here", "channels_ready", "channels_copied", "tokens_ready", "tokens_copied",
                       "product_ready") as (
                    tables_here, channels_ready, channels_copied, tokens_ready, tokens_copied,
                    product_ready), nc.Block() as block:
                @block.sync
                def _(sp):
                    for dst, name in ((wf, "w_fourier"), (dft_c, "dft_c"), (dft_t, "dft_t")):
                        sp.dma_start(dst[:], dram[name]).then_inc(tables_here, 16)

                @block.tensor
                def _(pe):
                    pe.wait_ge(tables_here, 48)
                    for g in range(C_GROUPS):
                        for t in range(TT):
                            mm = nc.tensor.matmul(banks[:, g, t * SEQ:(t + 1) * SEQ], fgT[:, g, t * P:(t + 1) * P],
                                                  dft_c[:], start=True, stop=True)
                        mm.then_inc(channels_ready, 1)
                    for g in range(C_GROUPS):
                        pe.wait_ge(channels_copied, g + 1)
                        a = channels[:, g, :, :]
                        accumulate(banks[:, 4 + g // 2, (g % 2) * SEQ:(g % 2 + 1) * SEQ],
                                   [(a[:, t, v * P:(v + 1) * P], dft_t[:, v, t, :]) for t in range(TT)
                                    for v in range(2)]).then_inc(tokens_ready, 1)
                    for g in range(C_GROUPS):
                        pe.wait_ge(tokens_copied, g // 2 + 1)
                        for t in range(TT):
                            mm = nc.tensor.matmul(banks[:, 6 + t, g * P:(g + 1) * P], frT[:, g, t * P:(t + 1) * P],
                                                  wf[:, g, :], start=True, stop=True)
                    mm.then_inc(product_ready, 1)

                @block.vector
                def _(dve):
                    for g in range(C_GROUPS):
                        dve.wait_ge(channels_ready, g + 1)
                        nc.vector.tensor_copy(channels[:, g, :, :], banks[:, g, :].rearrange(
                            "p (t n) -> p t n", t=TT)).then_inc(channels_copied, 1)
                    dve.wait_ge(product_ready, 1)
                    for t in range(TT):
                        nc.vector.tensor_copy(mixed[:, t, 0:BANK], banks[:, 6 + t, :])

                @block.scalar
                def _(act):
                    for b in range(C_GROUPS // 2):
                        act.wait_ge(tokens_ready, 2 * b + 2)
                        nc.scalar.copy(frT[:, 2 * b:2 * b + 2, :],
                                       banks[:, 4 + b, :].rearrange("p (g s) -> p g s", g=2)).then_inc(tokens_copied, 1)

        def relative_bias(bias_of, onehot, rpb, col_mask):
            with stage("spread",) as (spread,), nc.Block() as block:
                @block.tensor
                def _(pe):
                    for ck in range(GRID_W):
                        shift = GRID_W - 1 - ck
                        for parity in range(2):
                            mm = nc.tensor.matmul(
                                banks[parity * HD:(parity + 1) * HD, ck // 8, (ck % 8) * 56:(ck % 8 + 1) * 56],
                                onehot[:, shift:shift + GRID_W], rpb[:, parity, :], start=True, stop=True)
                    mm.then_inc(spread, 1)

                @block.vector
                def _(dve):
                    dve.wait_ge(spread, 1)
                    table = banks[:, :, 0:8 * 56].rearrange("p b (j h r) -> p r h b j", j=8, h=D_HEADS)
                    mask = col_mask[:].rearrange("p (b j) -> p b j", j=8).unsqueeze(1).broadcast_to([P, 4, 8, 8])
                    for t in range(TT):
                        for h0 in (0, 4):
                            four = bias_of(t, h0, 4).rearrange("p (h r b j) -> p h r b j", h=4, r=ROWS, b=8)
                            for rk in range(ROWS):
                                nc.vector.tensor_tensor(four[:, :, rk, :, :], table[:, rk - 2 * t + 3, h0:h0 + 4, :, :],
                                                        mask, ALU.add)

        first_block()
        final_norm(dram["final_gain"], False)
        second_block()
        final_norm(dram["final_norm_g"], True)


def _slabs(w):
    w = np.asarray(w)
    short = -w.shape[-1] % BANK
    w = np.concatenate([w, np.zeros(w.shape[:-1] + (short,), w.dtype)], axis=-1)
    lead = w.shape[:-2]
    w = w.reshape(-1, KC, P, w.shape[-1] // BANK, BANK).transpose(0, 3, 2, 1, 4)
    return np.ascontiguousarray(w.reshape(-1, P, KC * BANK))


def _features(v):
    v = np.asarray(v)
    v = v.reshape(v.shape[:-1] + (-1, P))
    return np.moveaxis(v, -1, 0)


def _w_in_order():
    starts = dict(q=0, kc=384, vc=512, ks=640, vs=768, kw=896, vw=1024)
    cols = [c for pair in NSA_PAIRS for h in pair for c in range(h * HD, (h + 1) * HD)]
    for name in ("kc", "ks", "kw", "vc", "vs", "vw"):
        cols += list(range(starts[name], starts[name] + NSA_G * HD))
    return np.array(cols + list(range(GATE0, N_IN)))


def _ukv_order():
    per = MLA_NOPE + HD
    return np.array([h * per + part * MLA_NOPE + d for part in range(2) for h in range(MLA_H) for d in range(HD)])


def _tables():
    i = np.arange(P)
    q = np.arange(SEQ)
    t = {}
    t["ident"] = np.eye(P)
    inv = [1.0 / theta ** (np.arange(0, dim, 2, dtype=np.float32) / np.float32(dim))
           for theta, dim in ((np.float32(500000.0), 16), (np.float32(500000.0), 32), (np.float32(10000.0), 64))]
    t["freqs"] = np.tile(np.concatenate(inv), (P, 1))
    tri = np.where(i[:, None] >= i[None, :], 0.0, NEG)
    t["causal"] = np.concatenate([tri, np.zeros((P, P)), tri], axis=1)
    gamma = 1.0 - 2.0 ** (-5.0 - np.arange(RET_H))
    gap = (q[None, :] - i[:, None]).astype(np.float64)
    fade = np.where(gap >= 0, gamma[:, None, None] ** np.maximum(gap, 0)[None], 0.0) * HD ** -0.5
    t["decay"] = np.concatenate([fade, fade[:, :, 0:P]], axis=2).transpose(1, 0, 2)
    keep = np.zeros((P, TT, 16))
    for tile in range(TT):
        keep[:, tile, 0:N_CMP] = (np.arange(N_CMP)[None, :] * 16 + 31) <= (tile * P + i)[:, None]
    t["cmp_keep"] = keep.reshape(P, TT * 16)
    t["cmp_add"] = np.where(keep > 0, 0.0, NEG).reshape(P, TT * 16)
    freq = np.float32(10000.0) ** (-np.arange(HD // 4, dtype=np.float32) / np.float32(HD // 4))
    ang = np.concatenate([(q // GRID_W)[:, None] * freq, (q % GRID_W)[:, None] * freq], axis=1)
    t["axial"] = np.stack([np.cos(ang), np.sin(ang)]).reshape(2, TT, P, HD // 2).transpose(2, 0, 1, 3)
    w = 2 * np.pi * np.outer(i, i) / P
    t["dft_c"] = np.concatenate([np.cos(w), np.sin(w)], axis=1)
    w = 2 * np.pi * (np.outer(q, q) % SEQ) / SEQ
    t["dft_t"] = (np.stack([np.cos(w), -np.sin(w)]) / np.sqrt(SEQ * P)).reshape(2, TT, P, SEQ).transpose(2, 0, 1, 3)
    t["onehot"] = (np.arange(2 * GRID_W - 1)[None, :] == (GRID_W - 1 + 15 - np.arange(N_DC))[:, None])
    col = np.arange(GRID_W)
    start = np.clip(col - 8, 0, GRID_W - 16)
    ok = (col[None, :] >= start[:, None]) & (col[None, :] < start[:, None] + 16)
    t["col_mask"] = np.tile(np.where(ok, 0.0, NEG), (2, 1))
    return {k: np.ascontiguousarray(v, dtype=np.float32) for k, v in t.items()}


def _ab_order():
    split = np.concatenate([np.arange(0, HD, 2), np.arange(1, HD, 2)])
    cols = list(range(AB_Q0))
    for i in range(B_HEADS // 2):
        for h in (i, i + B_HEADS // 2):
            cols += list(AB_Q0 + h * HD + split)
    for kv in range(B_KV):
        cols += list(AB_K0 + kv * HD + split)
    return np.array(cols + list(range(AB_V0, AB_N))), split


def _layout(a):
    cat = np.concatenate
    d = _tables()
    L = DEPTH
    tiles = lambda v: np.ascontiguousarray(np.asarray(v).reshape(-1, P, D).transpose(1, 0, 2))
    d["x"] = tiles(a["x"])
    d["ctx"] = tiles(a["ctx_2"])
    d["positions"] = np.ascontiguousarray(np.asarray(a["positions"]).reshape(TT, P).T)
    d["w_in"] = _slabs(np.asarray(a["w_in"])[:, :, _w_in_order()])
    w1 = [np.asarray(a[n]).reshape(L, CMP_LP, P, P).transpose(0, 2, 1, 3).reshape(L, P, CMP_LP * P)
          for n in ("cmp_w1_k", "cmp_w1_v")]
    d["cmp_w1"] = cat(w1, axis=2)
    d["small"] = cat([np.asarray(a["mla_w_uq"]).reshape(L, 2, P, 480).transpose(0, 2, 1, 3).reshape(L, P, 960),
                      np.asarray(a["mla_w_ukv"])[:, :, _ukv_order()], np.asarray(a["cmp_w2_k"]),
                      np.asarray(a["cmp_w2_v"])], axis=2)
    d["w_out"] = _slabs(a["w_out"])
    d["w_up"] = _slabs(a["w_up"])
    d["w_down"] = np.asarray(a["w_down"]).reshape(L, 8, 4, P, D).transpose(0, 1, 3, 2, 4).reshape(L * 8, P, SLAB)
    d["feats"] = cat([_features(a["ln1_gain"]), _features(a["ln2_gain"]), _features(a["mla_q_norm"]),
                      _features(a["mla_kv_norm"]), _features(np.asarray(a["cmp_pos_k"]).reshape(L, -1)),
                      _features(np.asarray(a["cmp_pos_v"]).reshape(L, -1))], axis=2)
    d["gn_gain"] = np.asarray(a["ret_gn_gain"]).reshape(L, RET_H * HD)
    d["final_gain"] = np.asarray(a["final_gain"]).reshape(1, D)
    d["final_norm_g"] = np.asarray(a["final_norm_g_2"]).reshape(1, D)
    order, split = _ab_order()
    d["ab_in"] = _slabs(np.asarray(a["ab_w_in_2"])[:, :, order])
    for to, of in (("ab_ada", "ab_w_ada_2"), ("ab_out", "ab_w_out_2"), ("cd_ada", "cd_w_ada_2"),
                   ("cd_in", "cd_w_in_2"), ("cd_out", "cd_w_out_2")):
        d[to] = _slabs(a[of])
    d["cond"] = np.stack([_features(np.asarray(a[n]).reshape(-1)) for n in ("c_2", "c_ctx_2")], axis=2)
    d["feats2"] = cat([_features(np.asarray(a[n]).reshape(-1)) for n in (
        "ab_b_ada_2", "ab_norm_g_2", "ab_conv_b_2", "cd_b_ada_2", "cd_norm_g_2")], axis=1)
    d["conv_w"] = np.asarray(a["ab_conv_w_2"]).reshape(CONV_W, 4, P).transpose(2, 1, 0)
    d["rows"] = cat([np.asarray(a["ab_ln_g_2"]), np.asarray(a["ab_ln_b_2"]),
                     np.asarray(a["ab_q_norm_g_2"])[:, split], np.asarray(a["ab_k_norm_g_2"])[:, split]], axis=1)
    d["w_fourier"] = np.asarray(a["cd_w_fourier_2"]).reshape(C_GROUPS, P, P).transpose(1, 0, 2)
    rpb = np.asarray(a["cd_rpb_2"])[0, :, 4:4 + N_DR, :].transpose(2, 0, 1)
    later = cat([np.zeros_like(rpb[:, :, :1]), rpb[:, :, :-1]], axis=2)
    d["rpb"] = np.stack([rpb, later], axis=1).reshape(N_DC, 2, D_HEADS * N_DR)
    return {k: np.ascontiguousarray(v) for k, v in d.items()}


def kernel(**inputs):
    import concourse.bacc as bacc
    from concourse.bass_utils import run_bass_kernel_spmd

    nc = bacc.Bacc("TRN2", target_bir_lowering=False, num_devices=1)
    arrays, dram = {}, {}
    for name, a in _layout(inputs).items():
        arrays[f"in_{name}"] = a
        dram[name] = nc.dram_tensor(f"in_{name}", a.shape, mybir.dt.from_np(a.dtype), kind="ExternalInput").ap()
    out = nc.dram_tensor("out_0", (1, SEQ, D), F32, kind="ExternalOutput").ap()
    build_program(nc, dram, out)
    r = run_bass_kernel_spmd(nc, [arrays], core_ids=[0])
    return r.results[0]["out_0"]
```

```python
from contextlib import ExitStack, contextmanager

import numpy as np

import concourse.bass as bass
from concourse import mybir

F32 = mybir.dt.float32
F32R = mybir.dt.float32r
I32 = mybir.dt.int32
ALU = mybir.AluOpType
ACT = mybir.ActivationFunctionType
AX = mybir.AxisListType

P = 128
D = 1024
KC = D // P
SEQ = 256
TT = SEQ // P
DEPTH = 2
DFF = 4 * D
HD = 64
EPS = 1e-6
NEG = -1e30
SLAB = 4096
HALF = SLAB // 2
SLOTS = 5
PART = SLAB // 4
PARTS = 3
AHEAD = 2
BANK = 512

NSA_H, NSA_G, NSA_R = 6, 2, 3
MLA_H, MLA_NOPE, MLA_PE, MLA_QK = 5, 64, 32, 96
RET_H = 5
Q0, KCMP0, KSLC0, KWIN0 = 0, 384, 512, 640
VCMP0, VSLC0, VWIN0 = 768, 896, 1024
GATE0, CQ0, CKV0, KPE0 = 1152, 1170, 1426, 1554
RQ0, RK0, RV0, RG0 = 1586, 1906, 2226, 2546
N_IN = 2866
W_IN_SLABS = -(-N_IN // BANK)
NSA_PAIRS = ((0, 3), (1, 4), (2, 5))
N_CMP = (SEQ - 32) // 16 + 1
CMP_LP = 16
ROPE_P, ROPE_M, ROPE_R = (0, 8), (8, 24), (24, 56)
ROPE_N = 56

AB_VAL0, AB_GATE0, AB_Q0, AB_K0, AB_V0, AB_Z0, AB_N = 0, 512, 1024, 1536, 1664, 1792, 2816
B_HEADS, B_KV = 8, 2
CONV_W, CONV_PAD = 31, 15
TAPS_WITH_SLABS, POOL_TAPS_WITH_SLABS = 54, 16
CD_F0, CD_Q0, CD_K0, CD_V0, CD_Z0, CD_N = 0, 512, 1024, 1536, 2048, 3072
D_HEADS, C_GROUPS = 8, 4
GRID_W, ROWS, N_DR, N_DC = 64, 4, 7, 31

LAYER_SLABS = [("w_in", W_IN_SLABS), ("adapt0", 1), ("adapt1", 1), ("cmp_k", 1), ("adapt2", 1), ("cmp_v", 1),
               ("small", 1), ("adapt3", 2), ("adapt5", 1), ("w_out", 2), ("ffn", 16)]
ADA_NAMES = ("ab_ada", "cd_ada")
ADA_SLABS = 3 * D // BANK
ADA_HALVES = {"adapt0": (0, 2), "adapt1": (2, 4), "adapt2": (4, 6), "adapt3": (6, 10), "adapt5": (10, 12)}
WHOLE = ("cmp_k", "cmp_v", "small")
FFN_GROUPS = DFF // BANK
FFN_ORDER = [("w_up", 0)] + [u for g in range(1, FFN_GROUPS) for u in (("w_up", g), ("w_down", g - 1))]
FFN_ORDER.append(("w_down", FFN_GROUPS - 1))
SECOND_SLABS = [("ab_in", 6), ("ab_out", 2), ("cd_in", 6), ("cd_out", 2)]
SMALL_W = 2 * 480 + 640 + 2 * HD
UQ0, UKV0, W2K0, W2V0 = 0, 960, 1600, 1664


class InOrder:

    def __init__(self, engine, done):
        self.engine, self.done, self.n = engine, done, 0

    def __call__(self, instruction):
        self.n += 1
        instruction.then_inc(self.done, 1)
        self.engine.wait_ge(self.done, self.n)


def slab_plan():
    halves, first, first_part, n_parts = [], {}, {}, 0
    uses = [((name, layer), name, layer * n, n) for layer in range(DEPTH) for name, n in LAYER_SLABS]
    uses += [(name, name, 0, n) for name, n in SECOND_SLABS]
    for key, name, at, n in uses:
        first[key], first_part[key] = len(halves), n_parts
        if name in ADA_HALVES:
            halves += [(ADA_NAMES[key[1]], h // 2, h % 2 * HALF, HALF) for h in range(*ADA_HALVES[name])]
            continue
        n_parts += 0 if name in WHOLE else 4 * n
        if name in WHOLE:
            halves.append({"cmp_k": ("cmp_w1", key[1], 0, HALF), "cmp_v": ("cmp_w1", key[1], HALF, HALF),
                           "small": ("small", key[1], 0, SMALL_W)}[name])
            continue
        for i in range(n):
            for c0 in (0, HALF):
                if name == "ffn":
                    name_of, g = FFN_ORDER[i]
                    halves.append((name_of, at // 2 + g, c0, HALF))
                else:
                    halves.append((name, at + i, c0, HALF))
    return halves, first, first_part


def build_program(nc, dram, out):
    plan, first, first_part = slab_plan()
    with ExitStack() as ctx:
        def sbuf(name, shape, dt=F32):
            return ctx.enter_context(nc.sbuf_tensor(name, shape, dt))

        ring = sbuf("ring", [P, SLOTS, HALF])
        w_hi, w_lo = sbuf("w_hi", [P, PARTS, PART], F32R), sbuf("w_lo", [P, PARTS, PART], F32R)
        x = sbuf("x", [P, 4, D])
        mixed = sbuf("mixed", [P, 4, D])
        ident = sbuf("ident", [P, P])
        sums = sbuf("sums", [P, 96])
        rstd = sbuf("rstd", [P, 64])
        minus_half = sbuf("minus_half", [P, 40])
        cond, cond_t = sbuf("cond", [P, KC, 2]), sbuf("cond_t", [P, KC, 2])
        ada_rows = sbuf("ada_rows", [P, 3 * D])
        gate_rows = ada_rows[:, 0:2 * D].rearrange("p (v n) -> p v n", v=2)
        ada = sbuf("ada", [P, 2, 24, 2])
        scales = sbuf("scales", [P, 2, 2, KC])
        feats2 = sbuf("feats2", [P, 24 + 8 + 4 + 24 + 8])
        col_mask = sbuf("col_mask", [P, GRID_W])
        onehot = sbuf("onehot", [N_DC, 2 * GRID_W - 1])
        rpb = sbuf("rpb", [N_DC, 2, D_HEADS * N_DR])
        banks = ctx.enter_context(nc.psum_tensor("banks", [P, 8, BANK], F32))

        half_landed = [ctx.enter_context(nc.semaphore(f"half_landed{i}")) for i in range(SLOTS)]
        half_used = ctx.enter_context(nc.semaphore("half_used"))
        hi_ready = ctx.enter_context(nc.semaphore("hi_ready"))
        part_ready = ctx.enter_context(nc.semaphore("part_ready"))
        part_used = ctx.enter_context(nc.semaphore("part_used"))
        x_here, tables_here, loaded = (ctx.enter_context(nc.semaphore(n)) for n in ("x_here", "tables_here", "loaded"))
        stored = ctx.enter_context(nc.semaphore("stored"))
        n_loaded, n_stages = [0], [0]

        def load_half(sp, i):
            if i >= len(plan):
                return
            if i >= SLOTS:
                sp.wait_ge(half_used, i - SLOTS + 1)
            name, at, c0, width = plan[i]
            sp.dma_start(ring[:, i % SLOTS, 0:width], dram[name][at, :, c0:c0 + width]).then_inc(
                half_landed[i % SLOTS], 16)

        def load_behind(sp, key, n_slabs, halves=2):
            for i in range(first[key], first[key] + halves * n_slabs):
                load_half(sp, i + SLOTS)

        def half_here(engine, i):
            engine.wait_ge(half_landed[i % SLOTS], 16 * (i // SLOTS + 1))

        def part_source(key, q):
            return ring[:, (first[key] + q // 2) % SLOTS, (q % 2) * PART:(q % 2 + 1) * PART]

        def split_hi(act, key, q):
            n = first_part[key] + q
            if q % 2 == 0:
                half_here(act, first[key] + q // 2)
            if n >= PARTS:
                act.wait_ge(part_used, n - PARTS + 1)
            nc.scalar.copy(w_hi[:, n % PARTS, :], part_source(key, q)).then_inc(hi_ready, 1)

        def split_lo(dve, key, q):
            n = first_part[key] + q
            dve.wait_ge(hi_ready, n + 1)
            nc.vector.tensor_tensor(w_lo[:, n % PARTS, :], part_source(key, q), w_hi[:, n % PARTS, :].bitcast(F32),
                                    ALU.subtract).then_inc(part_ready, 1)
            if q % 2 == 1:
                dve.wait_ge(part_ready, n + 1)
                dve.sem_inc(half_used, 1)

        next_key = {"ab_in": "ab_out", "ab_out": "cd_in", "cd_in": "cd_out", ("ffn", DEPTH - 1): "ab_in"}
        for layer in range(DEPTH):
            next_key["w_out", layer] = ("ffn", layer)
            if layer:
                next_key["ffn", layer - 1] = ("w_in", layer)

        def split_own(split, engine, key, q):
            if key not in next_key.values() or q >= AHEAD:
                split(engine, key, q)

        def split_ahead(split, engine, key):
            if key in next_key:
                for q in range(AHEAD):
                    split(engine, next_key[key], q)

        def part(key, q):
            n = (first_part[key] + q) % PARTS
            return [w[:, n, :].rearrange("p (k n) -> p k n", k=2) for w in (w_hi, w_lo)]

        def multiply(dst, left, right, first_one, last_one, shares_bank=False):
            pairs = ((left[0], right[0]), (left[0], right[1]), (left[1], right[0]))
            for i, (a, b) in enumerate(pairs):
                mm = nc.tensor.matmul(dst, a, b, start=first_one and i == 0, stop=last_one and i == 2,
                                      skip_group_check=shares_bank)
            return mm

        def adapt_products(pe, layer, h0, h1, bank, copied):
            place = next(p for p, (a, b) in ADA_HALVES.items() if a <= h0 and h1 <= b)
            for h in range(h0, h1):
                i = first[place, layer] + h - ADA_HALVES[place][0]
                w = ring[:, i % SLOTS, :].rearrange("p (k n) -> p k n", k=KC // 2)
                half_here(pe, i)
                for kk in range(KC // 2):
                    k = h % 2 * (KC // 2) + kk
                    if k == 0 and copied is not None:
                        pe.wait_ge(copied, 1)
                    mm = nc.tensor.matmul(banks[0:2, bank, :], cond[:, k, :], w[:, kk, :], start=(k == 0),
                                          stop=(k == KC - 1))
                    if kk == KC // 2 - 1:
                        mm.then_inc(half_used, 1)
                    yield

        def copy_adapted(act, layer, s, bank):
            place, (a, _) = next((p, ab) for p, ab in ADA_HALVES.items() if ab[0] <= 2 * s + 1 < ab[1])
            act.wait_ge(half_used, first[place, layer] + 2 * s + 1 - a + 1)
            return nc.scalar.copy(ada_rows[HD * layer:HD * layer + 2, s * BANK:(s + 1) * BANK], banks[0:2, bank, :])

        def advance(work, n=1000):
            for _ in range(n):
                next(work, None)

        def load_const(sp, dst, src):
            sp.dma_start(dst, src).then_inc(loaded, 16)
            n_loaded[0] += 16

        @contextmanager
        def stage(*names):
            n_stages[0] += 1
            sems = [nc.alloc_semaphore(f"{n}_{n_stages[0]}") for n in names]
            yield sems
            nc.clear_and_free_semaphores(sems)
            nc.all_engine_barrier()

        def accumulate(dst, pairs):
            n = len(pairs)
            for i, (lhsT, rhs) in enumerate(pairs):
                mm = nc.tensor.matmul(dst, lhsT, rhs, start=(i == 0), stop=(i == n - 1))
            return mm


        NORM_SIGNALS = ("squares_summed", "norm_step", "norm_rstd", "scaled", "scaled_too", "x_turned", "norm_high",
                        "norm_whole", "norm_low", "norm_low_too")

        def norm_programs(signals, hidden, tiles, scales, shifts=None, spare=None, load_rest=None):
            (squares_summed, norm_step, norm_rstd, scaled, scaled_too, x_turned, norm_high, norm_whole, norm_low,
             norm_low_too) = signals
            T, per = len(tiles), len(scales)
            width = T * P
            span = width // per
            hi, lo = hidden
            mine = [n for n in range(T) if n % 2 == 0]
            others = [n for n in range(T) if n % 2 == 1]
            shared = BANK // width

            def turned(c):
                return banks[:, 4 + c // shared % 4, c % shared * width:(c % shared + 1) * width]

            def loads(sp):
                if load_rest is not None:
                    load_rest(sp)

            def on_vector(dve):
                if load_rest is not None:
                    dve.wait_ge(x_here, 16 * T)
                for n in mine:
                    t = tiles[n]
                    nc.vector.tensor_tensor_reduce(mixed[:, t, :], x[:, t, :], x[:, t, :], 1.0, 0.0, ALU.mult,
                                                   ALU.add, sums[:, n:n + 1]).then_inc(squares_summed, 1)
                dve.wait_ge(norm_rstd, 1)
                for n in others:
                    t = tiles[n]
                    nc.vector.tensor_scalar(mixed[:, t, :], x[:, t, :], rstd[:, n:n + 1], None,
                                            ALU.mult).then_inc(scaled_too, 1)
                if shifts is None:
                    for c in range(KC):
                        dve.wait_ge(norm_high, (c // shared + 1) * shared)
                        nc.vector.scalar_tensor_tensor(out=lo[:, c, 0:width], in0=turned(c), scalar=scales[0][:, c:c + 1],
                                                       in1=hi[:, c, 0:width].bitcast(F32), op0=ALU.mult,
                                                       op1=ALU.subtract).then_inc(norm_low, 1)
                    return
                for c in range(KC + 1):
                    if c < KC:
                        dve.wait_ge(norm_high, per * (c + 1))
                        if c >= 2:
                            dve.wait_ge((norm_low, norm_low_too)[c % 2], c // 2)
                        for v in range(per):
                            cols = slice(v * span, (v + 1) * span)
                            nc.vector.tensor_scalar(spare[:, c % 2, cols], turned(c)[:, cols], scales[v][:, c:c + 1],
                                                    shifts[v][:, c:c + 1], ALU.mult, ALU.add).then_inc(norm_whole, 1)
                    if c % 2 == 1:
                        dve.wait_ge(norm_whole, per * c)
                        nc.vector.tensor_tensor(lo[:, c - 1, 0:width], spare[:, 0, :], hi[:, c - 1, 0:width].bitcast(F32),
                                                ALU.subtract).then_inc(norm_low, 1)

            def on_gpsimd(pool):
                step = InOrder(pool, norm_step)
                pool.wait_ge(squares_summed, T)
                step(nc.gpsimd.tensor_scalar(rstd[:, 0:T], sums[:, 0:T], 1.0 / D, EPS, ALU.mult, ALU.add))
                nc.gpsimd.tensor_tensor(rstd[:, 0:T], rstd[:, 0:T], minus_half[:, 0:T], ALU.pow).then_inc(norm_rstd, 1)
                if shifts is not None:
                    for c in range(1, KC, 2):
                        pool.wait_ge(norm_whole, per * (c + 1))
                        nc.gpsimd.tensor_tensor(lo[:, c, 0:width], spare[:, 1, :], hi[:, c, 0:width].bitcast(F32),
                                                ALU.subtract).then_inc(norm_low_too, 1)

            def on_scalar(act):
                if load_rest is not None:
                    act.wait_ge(x_here, 16 * T)
                for n in others:
                    t = tiles[n]
                    nc.scalar.activation(mixed[:, t, :], x[:, t, :], ACT.Square,
                                         accum_out=sums[:, n:n + 1]).then_inc(squares_summed, 1)
                act.wait_ge(norm_rstd, 1)
                for n in mine:
                    t = tiles[n]
                    nc.scalar.activation(mixed[:, t, :], x[:, t, :], ACT.Copy,
                                         scale=rstd[:, n:n + 1]).then_inc(scaled, 1)
                for c in range(KC):
                    act.wait_ge(x_turned, c // shared + 1)
                    for v in range(per):
                        cols = slice(v * span, (v + 1) * span)
                        shift = {} if shifts is None else {"bias": shifts[v][:, c:c + 1]}
                        nc.scalar.activation(hi[:, c, cols], turned(c)[:, cols],
                                             ACT.Copy if shifts is None else ACT.Identity,
                                             scale=scales[v][:, c:c + 1], **shift).then_inc(norm_high, 1)

            def turn(bank_of):
                for c in range(bank_of * shared, (bank_of + 1) * shared):
                    for n, t in enumerate(tiles):
                        mm = nc.tensor.transpose(turned(c)[:, n * P:(n + 1) * P], mixed[:, t, c * P:(c + 1) * P], ident[:])
                mm.then_inc(x_turned, 1)

            def low_here(pe, n_chunks):
                if shifts is None:
                    pe.wait_ge(norm_low, n_chunks)
                else:
                    pe.wait_ge(norm_low, n_chunks // 2)
                    pe.wait_ge(norm_low_too, n_chunks // 2)

            def on_tensor(pe):
                if load_rest is not None:
                    pe.wait_ge(tables_here, 32)
                pe.wait_ge(scaled, len(mine))
                pe.wait_ge(scaled_too, len(others))
                for b in range(4):
                    turn(b)

            def before_pair(pe, q):
                low_here(pe, 2 * q + 2)
                if shared == 1 and q < 2:
                    turn(4 + 2 * q)
                    turn(5 + 2 * q)

            return {"sync": loads, "vector": on_vector, "gpsimd": on_gpsimd, "scalar": on_scalar,
                    "tensor": on_tensor, "before_pair": before_pair}

        def project(key, hidden, widths, tiles_of, dst, norm_of):
            n_slabs = len(widths)
            with stage("evacuated", *NORM_SIGNALS) as (evacuated, *signals), \
                    nc.sbuf_tensor("cd_whole", [P, 2, 2 * SEQ], F32) as spare, nc.Block() as block:
                norm = norm_programs(signals, hidden, *norm_of, spare=spare)

                @block.sync
                def _(sp):
                    load_behind(sp, key, n_slabs)

                @block.gpsimd
                def _(pool):
                    norm["gpsimd"](pool)

                @block.tensor
                def _(pe):
                    norm["tensor"](pe)
                    for s in range(n_slabs):
                        if s >= 2:
                            pe.wait_ge(evacuated, s - 1)
                        multiply_slab(pe, key, s, hidden, widths[s], tiles_of[s], norm)

                @block.scalar
                def _(act):
                    norm["scalar"](act)

                    def copy_products(s):
                        products_done(act, key, s)
                        for t in tiles_of[s]:
                            last = nc.scalar.copy(dst[:, t, s * BANK:s * BANK + widths[s]],
                                                  banks[:, 4 * (s % 2) + t, 0:widths[s]])
                        last.then_inc(evacuated, 1)

                    for q in range(4 * n_slabs):
                        split_own(split_hi, act, key, q)
                        if q >= 5 and q % 4 == 1:
                            copy_products(q // 4 - 1)
                    split_ahead(split_hi, act, key)
                    copy_products(n_slabs - 1)

                @block.vector
                def _(dve):
                    norm["vector"](dve)
                    for q in range(4 * n_slabs):
                        split_own(split_lo, dve, key, q)
                    split_ahead(split_lo, dve, key)

        def multiply_slab(pe, key, s, hidden, width, tiles, norm=None):
            hi, lo = hidden
            for q in range(4):
                if norm is not None and s == 0:
                    norm["before_pair"](pe, q)
                n = first_part[key] + 4 * s + q
                pe.wait_ge(part_ready, n + 1)
                wh, wl = part(key, 4 * s + q)
                for kk in range(2):
                    k = 2 * q + kk
                    for t in tiles:
                        cols = slice(t * P, (t + 1) * P)
                        mm = multiply(banks[:, 4 * (s % 2) + t, 0:width], (hi[:, k, cols], lo[:, k, cols]),
                                      (wh[:, kk, 0:width], wl[:, kk, 0:width]), k == 0, k == KC - 1)
                mm.then_inc(part_used, 1)

        def products_done(engine, key, s):
            engine.wait_ge(part_used, first_part[key] + 4 * (s + 1))

        def transpose_groups(groups, padded=None):
            with stage("turned", "copied0", "copied1", "cleared") as (turned, copied0, copied1, cleared), \
                    nc.Block() as block:
                @block.gpsimd
                def _(pool):
                    if padded is not None:
                        nc.gpsimd.memset(padded[:], 0.0).then_inc(cleared, 1)

                @block.tensor
                def _(pe):
                    for g, (blocks, _) in enumerate(groups):
                        if g >= 8:
                            pe.wait_ge((copied0, copied1)[g % 2], (g - 8) // 2 + 1)
                        for j, src in enumerate(blocks):
                            w = src.shape[-1]
                            mm = nc.tensor.transpose(banks[0:w, g % 8, j * P:(j + 1) * P], src, ident[:])
                        mm.then_inc(turned, 1)

                @block.vector
                def _(dve):
                    if padded is not None:
                        dve.wait_ge(cleared, 1)
                    for g, (_, copies) in enumerate(groups):
                        if g % 2 == 0:
                            dve.wait_ge(turned, g + 1)
                            for copy in copies:
                                last = copy(nc.vector, banks[:, g % 8, :])
                            last.then_inc(copied0, 1)

                @block.scalar
                def _(act):
                    if padded is not None:
                        act.wait_ge(cleared, 1)
                    for g, (_, copies) in enumerate(groups):
                        if g % 2 == 1:
                            act.wait_ge(turned, g + 1)
                            for copy in copies:
                                last = copy(nc.scalar, banks[:, g % 8, :])
                            last.then_inc(copied1, 1)

        def copy_out(engine, dst, src, scale=None, bias=None):
            if engine is nc.scalar:
                if scale is None:
                    return nc.scalar.copy(dst, src)
                return nc.scalar.activation(dst, src, ACT.Copy, scale=scale)
            if scale is None:
                return nc.vector.tensor_copy(dst, src)
            return nc.vector.tensor_scalar(dst, src, scale, None, ALU.mult)

        def out_project(key, turned_y, tiles, gates=None):
            with stage("gated") as (gated,), nc.Block() as block:
                @block.sync
                def _(sp):
                    load_behind(sp, key, 2)

                @block.tensor
                def _(pe):
                    for s in range(2):
                        multiply_slab(pe, key, s, turned_y, BANK, tiles)

                @block.scalar
                def _(act):
                    for q in range(8):
                        split_own(split_hi, act, key, q)
                    split_ahead(split_hi, act, key)

                @block.vector
                def _(dve):
                    def add_products(s):
                        cols = slice(s * BANK, (s + 1) * BANK)
                        products_done(dve, key, s)
                        if gates is not None:
                            for t in tiles:
                                nc.vector.tensor_tensor(mixed[:, t, cols], banks[:, 4 * s + t, :],
                                                        gates[t // 2][:, cols], ALU.mult).then_inc(gated, 1)
                        for i, t in enumerate(tiles):
                            src = banks[:, 4 * s + t, :]
                            if gates is not None:
                                dve.wait_ge(gated, s * len(tiles) + i + 1)
                                src = mixed[:, t, cols]
                            nc.vector.tensor_tensor(x[:, t, cols], src, x[:, t, cols], ALU.add)

                    for q in range(8):
                        split_own(split_lo, dve, key, q)
                        if q == 6:
                            add_products(0)
                    split_ahead(split_lo, dve, key)
                    add_products(1)

        def attend(units, buffers, aside=None, pool_aside=None):
            probs, probsT, nmax, total, inverse = buffers
            n_units = len(units)
            S, T, O = 0, 3, 5
            TURN, VALUES, WEIGH = 2, 4, 5
            SUMS = 6
            with stage("scores_ready", "max_ready", "probs_ready", "probs_turned",
                       "turned_copied", "values_ready", "weighed", "dve_step", "aside_step", "pool_step") as (
                    scores_ready, max_ready, probs_ready, probs_turned,
                    turned_copied, values_ready, weighed, dve_step, aside_step,
                    pool_step), nc.Block() as block:
                @block.gpsimd
                def _(pool):
                    if pool_aside is not None:
                        pool_aside(InOrder(pool, pool_step))

                @block.tensor
                def _(pe):
                    def scores(i):
                        if i >= 3:
                            pe.wait_ge(probs_ready, i - 2)
                        causal = units[i].get("causal")
                        if causal is not None:
                            nc.tensor.matmul(banks[:, S + i % 3, 0:3 * P], causal[0], causal[1], start=True, stop=False,
                                             skip_group_check=True)
                        for qT, kT, c0, n, _ in units[i]["rows"]:
                            mm = nc.tensor.matmul(banks[:, S + i % 3, c0:c0 + n], qT, kT, start=causal is None,
                                                  stop=True, skip_group_check=causal is not None)
                        mm.then_inc(scores_ready, 1)

                    def turn(i):
                        pe.wait_ge(probs_ready, i + 1)
                        if i >= 2:
                            pe.wait_ge(turned_copied, i - 1)
                        for c in range(units[i]["width"] // P):
                            mm = nc.tensor.transpose(banks[:, T + i % 2, c * P:(c + 1) * P],
                                                     probs[:, i % 3, c * P:(c + 1) * P], ident[:])
                        mm.then_inc(probs_turned, 1)

                    def values(i):
                        pe.wait_ge(turned_copied, i + 1)
                        if i >= 3:
                            pe.wait_ge(weighed, i - 2)
                        for r, (_, _, c0, n, vs) in enumerate(units[i]["rows"]):
                            mm = accumulate(banks[:, O + i % 3, r * HD:(r + 1) * HD],
                                            [(probsT[:, i % 2, c0 + c * P:c0 + (c + 1) * P], v)
                                             for c, v in enumerate(vs)])
                        mm.then_inc(values_ready, 1)

                    for i in range(n_units + VALUES):
                        if i < n_units:
                            scores(i)
                        if TURN <= i < n_units + TURN:
                            turn(i - TURN)
                        if i >= VALUES:
                            values(i - VALUES)

                @block.vector
                def _(dve):
                    noted = [0]

                    def note(instruction):
                        noted[0] += 1
                        instruction.then_inc(dve_step, 1)
                        return noted[0]

                    def step_both(i, w):
                        unit = units[i] if i < n_units else None
                        done = units[w] if w >= 0 else None
                        src = banks[:, S + i % 3, :]
                        masked = None
                        if unit is not None:
                            dve.wait_ge(scores_ready, i + 1)
                            if unit["mask"] is not None:
                                m = src[:, 0:unit["mask"].free_size()]
                                masked = note(nc.vector.scalar_tensor_tensor(
                                    out=m, in0=m, scalar=unit["scale"], in1=unit["mask"], op0=ALU.mult, op1=ALU.add))
                        if done is not None:
                            R = len(done["rows"])
                            dve.wait_ge(probs_ready, w + 1)
                            inverted = note(nc.vector.reciprocal(inverse[:, w % 3, 0:R], total[:, w % SUMS, 0:R]))
                        if unit is not None:
                            if masked:
                                dve.wait_ge(dve_step, masked)
                            if done is not None and done.get("gates") is not None:
                                row_max(i, unit, src, 0)
                                dve.wait_ge(dve_step, inverted)
                                for r in range(R):
                                    here = inverse[:, w % 3, r:r + 1]
                                    inverted = note(nc.vector.tensor_tensor(here, here, done["gates"][r], ALU.mult))
                                last = row_max(i, unit, src, 1)
                            else:
                                for r in range(len(unit["rows"])):
                                    last = row_max(i, unit, src, r)
                            last.then_inc(max_ready, 1)
                        elif done is not None and done.get("gates") is not None:
                            dve.wait_ge(dve_step, inverted)
                            for r in range(R):
                                here = inverse[:, w % 3, r:r + 1]
                                inverted = note(nc.vector.tensor_tensor(here, here, done["gates"][r], ALU.mult))
                        if done is not None:
                            dve.wait_ge(dve_step, inverted)
                            dve.wait_ge(values_ready, w + 1)
                            for r in range(R):
                                last = done["weigh"](r, banks[:, O + w % 3, r * HD:(r + 1) * HD],
                                                     inverse[:, w % 3, r:r + 1])
                            last.then_inc(weighed, 1)

                    def row_max(i, unit, src, r):
                        _, _, c0, n, _ = unit["rows"][r]
                        return nc.vector.tensor_reduce(nmax[:, i % 3, r:r + 1], src[:, c0:c0 + n], AX.X, ALU.max,
                                                       negate=True)

                    more = iter(()) if aside is None else aside(aside_step)
                    for i in range(n_units + WEIGH):
                        step_both(i, i - WEIGH)
                        advance(more, 2)
                    advance(more)

                @block.scalar
                def _(act):
                    def exponential(i):
                        act.wait_ge(max_ready, i + 1)
                        if i >= 3:
                            act.wait_ge(probs_turned, i - 2)
                        if i >= SUMS:
                            act.wait_ge(weighed, i - SUMS + 1)
                        src = banks[:, S + i % 3, :]
                        for r, (_, _, c0, n, _) in enumerate(units[i]["rows"]):
                            last = nc.scalar.activation(probs[:, i % 3, c0:c0 + n], src[:, c0:c0 + n], ACT.Exp,
                                                        bias=nmax[:, i % 3, r:r + 1],
                                                        accum_out=total[:, i % SUMS, r:r + 1])
                        last.then_inc(probs_ready, 1)

                    def copy_turned(i):
                        act.wait_ge(probs_turned, i + 1)
                        if i >= 2:
                            act.wait_ge(values_ready, i - 1)
                        w = units[i]["width"]
                        nc.scalar.copy(probsT[:, i % 2, 0:w], banks[:, T + i % 2, 0:w]).then_inc(turned_copied, 1)

                    for i in range(n_units + TURN):
                        if i < n_units:
                            exponential(i)
                        if i >= TURN:
                            copy_turned(i - TURN)

        def rope(dve, step, v, cos, sin, half, temps):
            advance(rope_steps(dve, step, v, cos, sin, half, temps))

        def rope_steps(dve, step, v, cos, sin, half, temps):
            T, H = v.shape[1], v.shape[2]
            shape = [P, T, H, half]
            c = cos.unsqueeze(2).broadcast_to(shape)
            s = sin.unsqueeze(2).broadcast_to(shape)
            x1, x2 = v[:, :, :, 0:half], v[:, :, :, half:2 * half]
            a, b, e, f = [t[:, 0:T * H * half].rearrange("p (t h d) -> p t h d", t=T, h=H) for t in temps]
            for dst, src, table in ((a, x1, c), (b, x2, s), (e, x2, c)):
                nc.vector.tensor_tensor(dst, src, table, ALU.mult)
                yield
            step(nc.vector.tensor_tensor(f, x1, s, ALU.mult))
            yield
            nc.vector.tensor_tensor(x1, a, b, ALU.subtract)
            yield
            step(nc.vector.tensor_tensor(x2, e, f, ALU.add))
            yield

        def first_block():
            with ExitStack() as local:
                def sb(name, shape, dt=F32):
                    return local.enter_context(nc.sbuf_tensor(name, shape, dt))

                causal = (sb("causal_ident", [P, P], F32R)[:], sb("causal_mask", [P, 3 * P], F32R)[:])
                cmp_add = sb("cmp_add", [P, TT * 16])
                cmp_keep = sb("cmp_keep", [P, TT * 16])
                feats = sb("feats", [P, DEPTH, 51])
                gn_gain = sb("gn_gain", [P, RET_H * HD])
                cosT, sinT = sb("cosT", [P, TT, ROPE_N]), sb("sinT", [P, TT, ROPE_N])
                nmax, total, inverse = (sb(n, [P, 6, 2]) for n in ("nmax", "total", "inverse"))
                k2 = sb("k2", [P, 2, NSA_G, P])
                flat = sb("flat", [P, 2, CMP_LP, NSA_G, N_CMP])
                gelu = sb("gelu", [P, 4, 4 * N_CMP])
                kcT, vc = sb("kcT", [P, N_CMP]), sb("vc", [N_CMP, NSA_G, HD])
                branch = sb("branch", [P, 2, TT * 18])

                decay = sb("decay", [P, RET_H, 3 * P])
                scratch = mixed[:, 2:4, :].rearrange("p a b -> p (a b)")

                def mixers(layer, sb2, proj, qn, kvn, pos_of):
                    fT = sb2("fT", [P, 9, SEQ])
                    k_padded = sb2("k_padded", [P, 2, NSA_G, SEQ])
                    mqT, mkT = (sb2(n, [MLA_QK, MLA_H, SEQ]) for n in ("mqT", "mkT"))
                    mla_q, mla_k = (sb2(n, [P, TT, MLA_H * MLA_QK]) for n in ("mla_q", "mla_k"))
                    mla_v = sb2("mla_v", [P, TT, MLA_H * HD])
                    latents = sb2("latents", [P, 3, SEQ])
                    probs, probsT = sb2("probs", [P, 3, 3 * P]), sb2("probsT", [P, 2, 3 * P])
                    four = sb2("four", [P, 4, 640])
                    temps = [four[:, i, :] for i in range(4)]
                    transpose_heads(proj, fT, k_padded, k2, latents, qn, kvn)
                    small_products(layer, proj, latents, k2, flat, pos_of, gelu, kcT, vc, mla_q, mla_k, mla_v,
                                   cosT, sinT, temps)
                    groups = []
                    for src, dst, scale in ((mla_q, mqT, MLA_QK ** -0.5), (mla_k, mkT, None)):
                        for h0 in range(0, MLA_H, 2):
                            hs = range(h0, min(h0 + 2, MLA_H))
                            blocks = [src[:, t, h * MLA_QK:(h + 1) * MLA_QK] for h in hs for t in range(TT)]
                            n = len(blocks) * P

                            def copy(engine, bank, dst=dst, h0=h0, hs=hs, n=n, scale=scale):
                                return copy_out(engine, dst[:, h0:h0 + len(hs), :],
                                                bank[0:MLA_QK, 0:n].rearrange("p (h s) -> p h s", h=len(hs)),
                                                scale)
                            groups.append((blocks, [copy]))
                    transpose_groups(groups)
                    compressed_attention(layer, fT, kcT, vc, cmp_add, cmp_keep, branch, four)

                    units = []
                    for b, v0 in enumerate((VSLC0, VWIN0)):
                        for pair in range(3):
                            for g in range(NSA_G):
                                units.append(causal_unit(
                                    fT[:, pair, :], k_padded[:, b, g, :],
                                    [proj[:, t, v0 + g * HD:v0 + (g + 1) * HD] for t in range(TT)],
                                    causal, add_weigh(NSA_PAIRS[pair][g] * HD),
                                    [branch[:, 0, t * 18 + NSA_PAIRS[pair][g] * 3 + b + 1:
                                            t * 18 + NSA_PAIRS[pair][g] * 3 + b + 2] for t in range(TT)]))
                    for h in range(MLA_H):
                        units.append(causal_unit(
                            mqT[:, h, :], mkT[:, h, :], [mla_v[:, t, h * HD:(h + 1) * HD] for t in range(TT)],
                            causal, plain_weigh(NSA_H * HD + h * HD, (0, 1))))
                    attend(units, (probs, probsT, nmax, total, inverse))
                    retain(layer, proj, fT, decay, gn_gain, four)

                pos_i = local.enter_context(nc.sbuf_tensor("pos_i", [P, TT], I32))
                pos = sb("pos", [P, TT])
                freqs = sb("freqs", [P, ROPE_N])
                ang, turns, quarter = (scratch[:, c:c + TT * ROPE_N].rearrange("p (t n) -> p t n", t=TT)
                                       for c in (0, 256, 512))
                mask_here = scratch[:, 1024:1024 + 3 * P]
                with nc.Block() as block:
                    @block.sync
                    def _(sp):
                        for t in range(TT):
                            sp.dma_start(x[:, t, :], dram["x"][:, t, :]).then_inc(x_here, 16)
                        sp.dma_start(ident[:], dram["ident"]).then_inc(tables_here, 16)
                        sp.dma_start(feats[:], dram["feats"]).then_inc(tables_here, 16)

                    @block.gpsimd
                    def _(pool):
                        nc.gpsimd.memset(minus_half[:], -0.5)

                def load_rest(sp):
                    for i in range(SLOTS):
                        load_half(sp, i)
                    for dst, name in ((pos_i[:], "positions"), (freqs[:], "freqs"), (mask_here, "causal"),
                                      (decay[:], "decay"), (cmp_add[:], "cmp_add"), (cmp_keep[:], "cmp_keep"),
                                      (cond[:], "cond"), (feats2[:], "feats2"), (col_mask[:], "col_mask"),
                                      (onehot[:], "onehot"), (rpb[:], "rpb"), (x[:, TT:2 * TT, :], "ctx")):
                        load_const(sp, dst, dram[name])

                def find_angles(dve, step, angles_ready):
                    dve.wait_ge(loaded, n_loaded[0])
                    step(nc.vector.tensor_copy(pos[:], pos_i[:]))
                    yield
                    for t in range(TT):
                        last = nc.vector.tensor_scalar(ang[:, t, :], freqs[:], pos[:, t:t + 1], None, ALU.mult)
                    step(last)
                    yield
                    step(nc.vector.tensor_scalar(turns, ang, 1.0 / (2 * np.pi), 1.5 * 2.0 ** 23, ALU.mult, ALU.add))
                    yield
                    step(nc.vector.tensor_scalar(turns, turns, -1.5 * 2.0 ** 23, None, ALU.add))
                    yield
                    hi = 6.28125
                    for part in (hi, 2 * np.pi - hi):
                        step(nc.vector.scalar_tensor_tensor(out=ang, in0=turns, scalar=-part, in1=ang,
                                                            op0=ALU.mult, op1=ALU.add))
                        yield
                    edge = 3.1415925
                    step(nc.vector.tensor_scalar(ang, ang, edge, -edge, ALU.min, ALU.max))
                    yield
                    step(nc.vector.scalar_tensor_tensor(out=quarter, in0=ang, scalar=-1.0, in1=ang,
                                                        op0=ALU.mult, op1=ALU.min))
                    yield
                    nc.vector.tensor_scalar(quarter, quarter, np.pi / 2, None, ALU.add).then_inc(angles_ready, 1)
                    yield
                    nc.vector.tensor_copy(causal[0], ident[:])
                    yield
                    nc.vector.tensor_copy(causal[1], mask_here)
                    yield

                for layer in range(DEPTH):
                    f = feats[:, layer, :]
                    ln1, ln2, qn, kvn = f[:, 0:8], f[:, 8:16], f[:, 16:18], f[:, 18:19]
                    pos_of = (f[:, 19:35], f[:, 35:51])
                    with scope(layer) as sb2:
                        proj = sb2("proj", [P, TT, N_IN])
                        with scope(layer) as sb3:
                            hidden = [sb3(n, [P, KC, SEQ], F32R) for n in ("h_hi", "h_lo")]
                            widths = [min(BANK, N_IN - i * BANK) for i in range(W_IN_SLABS)]
                            project_and_prepare(layer, hidden, widths, proj, sb3("turning", [P, 4, 640]), cosT, sinT,
                                                gn_gain, branch, find_angles, (ang, quarter), ((0, 1), [ln1]),
                                                None if layer else load_rest)
                        mixers(layer, sb2, proj, qn, kvn, pos_of)
                    with scope(layer) as sb2:
                        turned_y = [sb2(n, [P, KC, SEQ], F32R) for n in ("y_hi", "y_lo")]
                        turn_mixed(turned_y, TT)
                        out_project(("w_out", layer), turned_y, (0, 1))
                    with scope(layer) as sb2:
                        hidden = [sb2(n, [P, KC, SEQ], F32R) for n in ("f_hi", "f_lo")]
                        feed_forward(layer, sb2, hidden, ((0, 1), [ln2]))

        @contextmanager
        def scope(layer):
            with ExitStack() as local:
                yield lambda name, shape, dt=F32: local.enter_context(nc.sbuf_tensor(f"{name}_{layer}", shape, dt))

        def causal_unit(qT, kT, vs, causal, weigh, gates=None):
            return {"rows": [(qT[:, 0:P], kT[:, 0:P], 0, P, vs[0:1]),
                             (qT[:, P:2 * P], kT[:, 0:2 * P], P, 2 * P, vs)],
                    "width": 3 * P, "mask": None, "causal": causal, "weigh": weigh, "gates": gates}

        def add_weigh(column):
            def weigh(t, product, inverse):
                here = mixed[:, t, column:column + HD]
                return nc.vector.scalar_tensor_tensor(out=here, in0=product, scalar=inverse, in1=here,
                                                      op0=ALU.mult, op1=ALU.add)
            return weigh

        def plain_weigh(column, tiles):
            def weigh(r, product, inverse):
                return nc.vector.tensor_scalar(mixed[:, tiles[r], column:column + HD], product, inverse, None, ALU.mult)
            return weigh

        def project_and_prepare(layer, hidden, widths, proj, four, cosT, sinT, gn_gain, branch, find_angles,
                                angles, norm_of, load_rest):
            key, n_slabs = ("w_in", layer), len(widths)
            temps = [four[:, i, :] for i in range(4)]
            with stage("evacuated", "dve_step", "pool_step", "sums_ready", "rstd_ready", "tanh_ready", "gain_here",
                       "cond_tanh", "cond_ready", "angles_ready", "angles_turned", *NORM_SIGNALS) as (
                    evacuated, dve_step, pool_step, sums_ready, rstd_ready, tanh_ready, gain_here, cond_tanh,
                    cond_ready, angles_ready, angles_turned, *signals), nc.Block() as block:
                norm = norm_programs(signals, hidden, *norm_of, load_rest=load_rest)

                @block.sync
                def _(sp):
                    norm["sync"](sp)
                    sp.dma_start(gn_gain[:], dram["gn_gain"][layer:layer + 1, :].broadcast_to([P, RET_H * HD])
                                 ).then_inc(gain_here, 16)
                    load_behind(sp, key, n_slabs)
                    load_behind(sp, ("adapt0", layer), 1)
                    sp.wait_ge(gain_here, 16)
                    sp.wait_ge(loaded, n_loaded[0])

                @block.tensor
                def _(pe):
                    norm["tensor"](pe)
                    for s in range(n_slabs):
                        if s >= 2:
                            pe.wait_ge(evacuated, s - 1)
                        multiply_slab(pe, key, s, hidden, widths[s], (0, 1), norm)
                    if layer == 0:
                        pe.wait_ge(cond_ready, 1)
                    pe.wait_ge(half_used, first["adapt0", layer])
                    advance(adapt_products(pe, layer, 0, 2, 2, None))

                @block.scalar
                def _(act):
                    norm["scalar"](act)

                    def copy_products(s):
                        products_done(act, key, s)
                        for t in range(TT):
                            last = nc.scalar.copy(proj[:, t, s * BANK:s * BANK + widths[s]],
                                                  banks[:, 4 * (s % 2) + t, 0:widths[s]])
                        last.then_inc(evacuated, 1)

                    for q in range(4 * n_slabs):
                        split_own(split_hi, act, key, q)
                        if layer == 0 and q == 10:
                            act.wait_ge(angles_ready, 1)
                            nc.scalar.activation(sinT[:], angles[0], ACT.Sin)
                            nc.scalar.activation(cosT[:], angles[1], ACT.Sin).then_inc(angles_turned, 1)
                            nc.scalar.activation(cond_t[:], cond[:], ACT.Tanh, scale=0.5).then_inc(cond_tanh, 1)
                        if q >= 5 and q % 4 == 1:
                            copy_products(q // 4 - 1)
                        if q == 14:
                            act.wait_ge(evacuated, GATE0 // BANK + 1)
                            nc.scalar.activation(branch[:, 1, :].rearrange("p (t n) -> p t n", t=TT),
                                                 proj[:, :, GATE0:GATE0 + 18], ACT.Tanh, scale=0.5).then_inc(tanh_ready, 1)
                    split_ahead(split_hi, act, key)
                    copy_products(n_slabs - 1)
                    copy_adapted(act, layer, 0, 2)

                @block.gpsimd
                def _(pool):
                    norm["gpsimd"](pool)
                    step = InOrder(pool, pool_step)
                    pool.wait_ge(sums_ready, 1)
                    step(nc.gpsimd.tensor_scalar(rstd[:, 0:4], sums[:, 0:4], EPS, None, ALU.add))
                    nc.gpsimd.tensor_tensor(rstd[:, 0:4], rstd[:, 0:4], minus_half[:, 0:4], ALU.pow).then_inc(rstd_ready, 1)

                @block.vector
                def _(dve):
                    norm["vector"](dve)
                    step = InOrder(dve, dve_step)
                    sq = four[:, 0, :]

                    def rotate(c0, n, d, table):
                        a, b = table
                        view = proj[:, :, c0:c0 + n * d].rearrange("p t (h d) -> p t h d", h=n)
                        dve.wait_ge(evacuated, (c0 + n * d - 1) // BANK + 1)
                        return rope_steps(dve, step, view, cosT[:, :, a:b], sinT[:, :, a:b], b - a, temps)

                    def preparation():
                        if layer == 0:
                            dve.wait_ge(angles_turned, 1)
                            dve.wait_ge(cond_tanh, 1)
                            step(nc.vector.tensor_scalar(cond_t[:], cond_t[:], 0.5, 0.5, ALU.mult, ALU.add))
                            nc.vector.tensor_tensor(cond[:], cond[:], cond_t[:], ALU.mult).then_inc(cond_ready, 1)
                        yield from rotate(Q0, 12, HD, ROPE_P)
                        yield from rotate(KPE0, 1, MLA_PE, ROPE_M)
                        for t in range(TT):
                            for c0, n, k in ((CQ0, 256, t), (CKV0, P, TT + t)):
                                step(nc.vector.tensor_tensor_reduce(sq[:, 0:n], proj[:, t, c0:c0 + n],
                                                                    proj[:, t, c0:c0 + n], 1.0 / n, 0.0, ALU.mult,
                                                                    ALU.add, sums[:, k:k + 1]))
                                yield
                        dve.sem_inc(sums_ready, 1)
                        yield from rotate(RQ0, RET_H, HD, ROPE_R)
                        dve.wait_ge(tanh_ready, 1)
                        nc.vector.tensor_scalar(branch[:, 0, :], branch[:, 1, :], 0.5, 0.5, ALU.mult, ALU.add)
                        yield
                        dve.wait_ge(rstd_ready, 1)
                        for t in range(TT):
                            for c0, n, k in ((CQ0, 256, t), (CKV0, P, TT + t)):
                                nc.vector.tensor_scalar(proj[:, t, c0:c0 + n], proj[:, t, c0:c0 + n], rstd[:, k:k + 1],
                                                        None, ALU.mult)
                                yield
                        yield from rotate(RK0, RET_H, HD, ROPE_R)

                    more = preparation()
                    angle_steps = find_angles(dve, step, angles_ready) if layer == 0 else iter(())
                    for q in range(4 * n_slabs):
                        split_own(split_lo, dve, key, q)
                        advance(angle_steps, 0 if q < 4 else 2)
                        advance(more, 0 if q < 11 else 1 if q < 17 else 0 if q < 18 else 3)
                    advance(more)

        def scratch_ret():
            return mixed[:, 0:TT, 704:704 + RET_H * HD]

        def transpose_heads(proj, fT, k_padded, k2, latents, qn, kvn):
            def cols(c0, w):
                return [proj[:, t, c0:c0 + w] for t in range(TT)]

            def pad_keys(branch, parity):
                lanes = slice(parity * HD, (parity + 1) * HD)
                return lambda engine, bank: copy_out(engine, k_padded[lanes, branch, parity, :],
                                                     bank[lanes, branch * SEQ:(branch + 1) * SEQ])

            def to_fT(b, scales=(None, None)):
                if scales[0] == scales[1]:
                    return [lambda engine, bank: copy_out(engine, fT[:, b:b + 2, :],
                                                          bank.rearrange("p (b s) -> p b s", b=2), scales[0])]
                return [lambda engine, bank, i=i: copy_out(engine, fT[:, b + i, :], bank[:, i * SEQ:(i + 1) * SEQ],
                                                           scales[i]) for i in range(2)]

            q_scale = HD ** -0.5

            order = [Q0, Q0 + P, Q0 + 2 * P, KSLC0, KWIN0, RQ0, RQ0 + P, RK0, RK0 + P]
            order[3:5] = []
            groups = [(cols(order[b], P) + cols(order[b + 1], P), to_fT(b, scales))
                      for b, scales in ((0, (q_scale, q_scale)), (2, (q_scale, None)), (4, (None, None)))]
            groups.append((cols(KSLC0, P) + cols(KWIN0, P), [pad_keys(b, g) for b in range(2) for g in range(2)]))
            groups.append((cols(order[6], P), [lambda engine, bank: copy_out(engine, fT[:, 6, :], bank[:, 0:SEQ])]))
            groups.append((cols(RQ0 + 2 * P, HD) + cols(RK0 + 2 * P, HD), [
                lambda engine, bank: copy_out(engine, fT[0:HD, 7:9, :],
                                              bank[0:HD, :].rearrange("p (b s) -> p b s", b=2))]))

            def pair_up(kv, g, parity):
                def copy(engine, bank):
                    src = bank[g * HD:(g + 1) * HD, kv * SEQ:(kv + 1) * SEQ].rearrange("p (m e) -> p m e", e=2)
                    return copy_out(engine, k2[parity * HD:(parity + 1) * HD, kv, g, :], src[:, :, parity])
                return copy

            groups.append((cols(KCMP0, P) + cols(VCMP0, P),
                           [pair_up(kv, g, e) for kv in range(2) for g in range(NSA_G) for e in range(2)]))

            def latent(dst, c0, scale):
                return lambda engine, bank: copy_out(engine, dst, bank[:, c0:c0 + SEQ], scale)

            groups.append((cols(CQ0, P) + cols(CQ0 + P, P),
                           [latent(latents[:, 0, :], 0, qn[:, 0:1]), latent(latents[:, 1, :], SEQ, qn[:, 1:2])]))
            groups.append((cols(CKV0, P), [latent(latents[:, 2, :], 0, kvn)]))
            transpose_groups(groups, k_padded)

        def small_products(layer, proj, latents, k2, flat, pos_of, gelu, kcT, vc, mla_q, mla_k, mla_v, cosT, sinT, temps):
            h_w1, h_small = [first[name, layer] for name in ("cmp_k", "cmp_v")], first["small", layer]
            w1 = [ring[:, h % SLOTS, :].rearrange("p (l h) -> p l h", l=CMP_LP) for h in h_w1]
            small = ring[:, h_small % SLOTS, :]
            NC2 = NSA_G * N_CMP
            with stage("dve_step", "flat_ready", "hidden_ready", "inner_ready", "tanh_ready", "gelu_ready", "mla_ready",
                       "cmp_ready", "act_copied", "row_copied", "ret_tanh_ready") as (
                    dve_step, flat_ready, hidden_ready, inner_ready, tanh_ready, gelu_ready, mla_ready, cmp_ready,
                    act_copied, row_copied, ret_tanh_ready), nc.Block() as block:
                @block.sync
                def _(sp):
                    for i in range(first["adapt1", layer], first["adapt3", layer]):
                        load_half(sp, i + SLOTS)

                @block.tensor
                def _(pe):
                    for kv, (h0, copied) in enumerate(((2, None), (4, row_copied))):
                        between = adapt_products(pe, layer, h0, h0 + 2, 7, copied)
                        advance(between, 1)
                        if kv == 0:
                            pe.wait_ge(flat_ready, 1)
                        half_here(pe, h_w1[kv])
                        for lp in range(CMP_LP):
                            mm = nc.tensor.matmul(banks[:, 0, kv * NC2:(kv + 1) * NC2], w1[kv][:, lp, :],
                                                  flat[:, kv, lp, :, :].rearrange("p g n -> p (g n)"),
                                                  start=lp == 0, stop=lp == CMP_LP - 1)
                            if lp % 2 == 0:
                                advance(between, 1)
                        if kv == 0:
                            mm.then_inc(half_used, 1)
                    mm.then_inc(hidden_ready, 1)
                    pe.wait_ge(hidden_ready, 1)
                    pe.sem_inc(half_used, 1)
                    half_here(pe, h_small)
                    for t in range(TT):
                        accumulate(banks[:, 1 + t, 0:480],
                                   [(latents[:, c, t * P:(t + 1) * P],
                                     small[:, UQ0 + c * 480:UQ0 + (c + 1) * 480]) for c in range(2)])
                        for part in range(2):
                            mm = nc.tensor.matmul(banks[:, 3 + 2 * part + t, 0:320], latents[:, 2, t * P:(t + 1) * P],
                                                  small[:, UKV0 + part * 320:UKV0 + (part + 1) * 320],
                                                  start=True, stop=True)
                    mm.then_inc(mla_ready, 1)
                    pe.wait_ge(gelu_ready, 1)
                    for g in range(NSA_G):
                        nc.tensor.matmul(banks[g * HD:(g + 1) * HD, 0, BANK // 2:BANK // 2 + N_CMP], small[:, W2K0:W2K0 + HD],
                                         gelu[:, 3, g * N_CMP:(g + 1) * N_CMP], start=True, stop=True)
                    for g in range(NSA_G):
                        mm = nc.tensor.matmul(banks[0:N_CMP, 0, 128 + g * HD:128 + (g + 1) * HD],
                                              gelu[:, 3, NC2 + g * N_CMP:NC2 + (g + 1) * N_CMP],
                                              small[:, W2V0:W2V0 + HD], start=True, stop=True)
                    mm.then_inc(cmp_ready, 1)
                    pe.wait_ge(cmp_ready, 1)
                    pe.sem_inc(half_used, 1)

                @block.vector
                def _(dve):
                    step = InOrder(dve, dve_step)
                    for kv in range(2):
                        tok = k2[:, kv, :, :].rearrange("p g (m e) -> p e g m", e=8)
                        for half in range(2):
                            last = nc.vector.tensor_tensor(
                                flat[:, kv, half * 8:half * 8 + 8, :, :], tok[:, :, :, half:half + N_CMP],
                                pos_of[kv][:, half * 8:half * 8 + 8].unsqueeze(2).unsqueeze(3).broadcast_to(
                                    [P, 8, NSA_G, N_CMP]), ALU.add)
                    last.then_inc(flat_ready, 1)
                    dve.wait_ge(ret_tanh_ready, 1)
                    ret_tanh, ret_gate = scratch_ret(), proj[:, 0:TT, RG0:RG0 + RET_H * HD]
                    step(nc.vector.tensor_scalar(ret_tanh, ret_tanh, 0.5, 0.5, ALU.mult, ALU.add))
                    nc.vector.tensor_tensor(ret_gate, ret_gate, ret_tanh, ALU.mult)
                    dve.wait_ge(hidden_ready, 1)
                    step(nc.vector.tensor_copy(gelu[:, 0, :], banks[:, 0, 0:2 * NC2]))
                    step(nc.vector.tensor_tensor(gelu[:, 1, :], gelu[:, 0, :], gelu[:, 0, :], ALU.mult))
                    step(nc.vector.tensor_scalar(gelu[:, 1, :], gelu[:, 1, :], 0.044715, 1.0, ALU.mult, ALU.add))
                    nc.vector.tensor_tensor(gelu[:, 1, :], gelu[:, 1, :], gelu[:, 0, :], ALU.mult).then_inc(inner_ready, 1)
                    dve.wait_ge(tanh_ready, 1)
                    step(nc.vector.scalar_tensor_tensor(out=gelu[:, 3, :], in0=gelu[:, 2, :], scalar=1.0,
                                                        in1=gelu[:, 0, :], op0=ALU.add, op1=ALU.mult))
                    nc.vector.tensor_scalar(gelu[:, 3, :], gelu[:, 3, :], 0.5, None, ALU.mult).then_inc(gelu_ready, 1)
                    dve.wait_ge(act_copied, 1)
                    q4 = mla_q.rearrange("p t (h d) -> p t h d", h=MLA_H)
                    a, b = ROPE_M
                    rope(dve, step, q4[:, :, :, MLA_NOPE:MLA_QK], cosT[:, :, a:b], sinT[:, :, a:b], b - a, temps)
                    k4 = mla_k.rearrange("p t (h d) -> p t h d", h=MLA_H)
                    for t in range(TT):
                        nc.vector.tensor_copy(k4[:, t, :, MLA_NOPE:MLA_QK],
                                              proj[:, t, KPE0:KPE0 + MLA_PE].unsqueeze(1).broadcast_to(
                                                  [P, MLA_H, MLA_PE]))
                    dve.wait_ge(cmp_ready, 1)
                    nc.vector.tensor_copy(kcT[:], banks[:, 0, BANK // 2:BANK // 2 + N_CMP])
                    nc.vector.tensor_copy(vc[:, :, :].rearrange("p g d -> p (g d)"), banks[0:N_CMP, 0, 128:256])

                @block.scalar
                def _(act):
                    nc.scalar.activation(scratch_ret(), proj[:, 0:TT, RG0:RG0 + RET_H * HD], ACT.Tanh,
                                         scale=0.5).then_inc(ret_tanh_ready, 1)
                    copy_adapted(act, layer, 1, 7).then_inc(row_copied, 1)
                    copy_adapted(act, layer, 2, 7)
                    act.wait_ge(inner_ready, 1)
                    nc.scalar.activation(gelu[:, 2, :], gelu[:, 1, :], ACT.Tanh,
                                         scale=float(np.sqrt(2 / np.pi))).then_inc(tanh_ready, 1)
                    act.wait_ge(mla_ready, 1)
                    for t in range(TT):
                        last = nc.scalar.copy(mla_q[:, t, :], banks[:, 1 + t, 0:480])
                    last.then_inc(act_copied, 1)
                    for t in range(TT):
                        nc.scalar.copy(mla_k[:, t, :].rearrange("p (h d) -> p h d", h=MLA_H)[:, :, 0:MLA_NOPE],
                                       banks[:, 3 + t, 0:320].rearrange("p (h d) -> p h d", h=MLA_H))
                        nc.scalar.copy(mla_v[:, t, :], banks[:, 5 + t, 0:320])

        def compressed_attention(layer, fT, kcT, vc, cmp_add, cmp_keep, branch, four):
            N = NSA_H * TT
            jobs = [(pair, g, t) for g in range(NSA_G) for pair in range(3) for t in range(TT)]
            NG = N // NSA_G
            s, p = (four[:, i, 0:N * N_CMP].rearrange("p (j n) -> p j n", j=N) for i in range(2))
            pT = mixed[0:N_CMP, 2:4, :].rearrange("p a b -> p (a b)")
            s4 = s.rearrange("p (a t) n -> p a t n", t=TT)
            p4 = p.rearrange("p (a t) n -> p a t n", t=TT)

            def table(m):
                return m[:, :].rearrange("p (t n) -> p t n", t=TT)[:, :, 0:N_CMP].unsqueeze(1).broadcast_to(
                    [P, NSA_H, TT, N_CMP])

            def turned(j):
                return pT[:, j * P:(j + 1) * P]

            with stage("scores_ready", "dve_step", "shifted", "exp_ready", "probs_ready", "probs_turned", "copied",
                       "values_ready", "row_copied") as (
                    scores_ready, dve_step, shifted, exp_ready, probs_ready, probs_turned, copied,
                    values_ready, row_copied), nc.Block() as block:
                @block.sync
                def _(sp):
                    load_behind(sp, ("adapt3", layer), 2)

                @block.tensor
                def _(pe):
                    for j, (pair, g, t) in enumerate(jobs):
                        mm = nc.tensor.matmul(banks[:, 7 * g, (j - g * NG) * N_CMP:(j - g * NG + 1) * N_CMP],
                                              fT[g * HD:(g + 1) * HD, pair, t * P:(t + 1) * P],
                                              kcT[g * HD:(g + 1) * HD, :], start=True, stop=True)
                    mm.then_inc(scores_ready, 1)
                    first_slab = adapt_products(pe, layer, 6, 8, 6, None)
                    advance(first_slab, 3)
                    second_slab = adapt_products(pe, layer, 8, 10, 6, row_copied)
                    pe.wait_ge(probs_ready, 1)
                    for j in range(N):
                        mm = nc.tensor.transpose(banks[0:N_CMP, 1 + j // 4, (j % 4) * P:(j % 4 + 1) * P],
                                                 p[:, j, :], ident[:])
                    mm.then_inc(probs_turned, 1)
                    advance(first_slab)
                    pe.wait_ge(copied, 1)
                    for j, (pair, g, t) in enumerate(jobs):
                        mm = nc.tensor.matmul(banks[:, 4 + j // 8, (j % 8) * HD:(j % 8 + 1) * HD],
                                              turned(j), vc[:, g, :], start=True, stop=True)
                    mm.then_inc(values_ready, 1)
                    advance(second_slab)

                @block.vector
                def _(dve):
                    step = InOrder(dve, dve_step)
                    dve.wait_ge(scores_ready, 1)
                    for g in range(NSA_G):
                        pairs = slice(g * NSA_H // NSA_G, (g + 1) * NSA_H // NSA_G)
                        last = nc.vector.tensor_tensor(
                            s4[:, pairs, :, :],
                            banks[:, 7 * g, 0:NG * N_CMP].rearrange("p (a t n) -> p a t n", t=TT, n=N_CMP),
                            table(cmp_add)[:, pairs, :, :], ALU.add)
                    step(last)
                    step(nc.vector.tensor_reduce(sums[:, 0:N], s, AX.X, ALU.max))
                    nc.vector.tensor_tensor(s, s, sums[:, 0:N].unsqueeze(2).broadcast_to([P, N, N_CMP]),
                                            ALU.subtract).then_inc(shifted, 1)
                    dve.wait_ge(exp_ready, 1)
                    step(nc.vector.tensor_tensor(p4, p4, table(cmp_keep), ALU.mult))
                    step(nc.vector.tensor_reduce(sums[:, 0:N], p, AX.X, ALU.add))
                    step(nc.vector.tensor_scalar(sums[:, 0:N], sums[:, 0:N], 1e-30, None, ALU.max))
                    step(nc.vector.reciprocal(sums[:, 16:16 + N], sums[:, 0:N]))
                    nc.vector.tensor_tensor(p, p, sums[:, 16:16 + N].unsqueeze(2).broadcast_to([P, N, N_CMP]),
                                            ALU.mult).then_inc(probs_ready, 1)
                    dve.wait_ge(probs_turned, 1)
                    nc.vector.tensor_copy(pT[:, 0:3 * BANK].rearrange("p (b n) -> p b n", b=3),
                                          banks[0:N_CMP, 1:4, :]).then_inc(copied, 1)
                    dve.wait_ge(values_ready, 1)
                    for j, (pair, g, t) in enumerate(jobs):
                        head = NSA_PAIRS[pair][g]
                        nc.vector.tensor_scalar(mixed[:, t, head * HD:(head + 1) * HD],
                                                banks[:, 4 + j // 8, (j % 8) * HD:(j % 8 + 1) * HD],
                                                branch[:, 0, t * 18 + head * 3:t * 18 + head * 3 + 1], None, ALU.mult)

                @block.scalar
                def _(act):
                    act.wait_ge(shifted, 1)
                    nc.scalar.activation(p, s, ACT.Exp).then_inc(exp_ready, 1)
                    copy_adapted(act, layer, 3, 6).then_inc(row_copied, 1)
                    copy_adapted(act, layer, 4, 6)

        def retain(layer, proj, fT, decay, gn_gain, four):
            heads = [(fT[0:HD, 3, :], fT[0:HD, 5, :]), (fT[HD:P, 3, :], fT[HD:P, 5, :]),
                     (fT[0:HD, 4, :], fT[0:HD, 6, :]), (fT[HD:P, 4, :], fT[HD:P, 6, :]),
                     (fT[0:HD, 7, :], fT[0:HD, 8, :])]
            N = TT * RET_H

            def faded_of(h):
                return four[:, h, 0:3 * P] if h < 4 else mixed[:, 2, 0:3 * P]

            with stage("scores_ready", "faded_ready", "values_ready", "dve_step", "sums_ready", "rstd_ready",
                       "pool_step") as (
                    scores_ready, faded_ready, values_ready, dve_step, sums_ready, rstd_ready, pool_step), \
                    nc.Block() as block:
                @block.sync
                def _(sp):
                    load_behind(sp, ("adapt5", layer), 1)

                @block.scalar
                def _(act):
                    copy_adapted(act, layer, 5, 7)

                @block.tensor
                def _(pe):
                    for h, (qT, kT) in enumerate(heads):
                        nc.tensor.matmul(banks[:, h, 0:SEQ], kT[:, 0:P], qT[:, 0:SEQ], start=True, stop=True)
                        nc.tensor.matmul(banks[:, h, SEQ:SEQ + P], kT[:, P:SEQ], qT[:, P:SEQ],
                                         start=True, stop=True).then_inc(scores_ready, 1)
                    for h in range(RET_H):
                        pe.wait_ge(faded_ready, h + 1)
                        v = [proj[:, t, RV0 + h * HD:RV0 + (h + 1) * HD] for t in range(TT)]
                        f = faded_of(h)
                        nc.tensor.matmul(banks[:, 5, h * HD:(h + 1) * HD], f[:, 0:P], v[0], start=True, stop=True)
                        accumulate(banks[:, 6, h * HD:(h + 1) * HD],
                                   [(f[:, P:2 * P], v[0]), (f[:, 2 * P:3 * P], v[1])]).then_inc(values_ready, 1)
                    advance(adapt_products(pe, layer, 10, 12, 7, None))

                @block.vector
                def _(dve):
                    step = InOrder(dve, dve_step)
                    for h in range(RET_H):
                        dve.wait_ge(scores_ready, h + 1)
                        nc.vector.tensor_tensor(faded_of(h), banks[:, h, 0:3 * P], decay[:, h, :],
                                                ALU.mult).then_inc(faded_ready, 1)
                    dve.wait_ge(values_ready, RET_H)
                    o3 = mixed[:, 0:TT, 704:1024]
                    for t in range(TT):
                        last = nc.vector.tensor_copy(o3[:, t, :], banks[:, 5 + t, 0:320])
                    step(last)
                    o = o3.rearrange("p t (h d) -> p t h d", h=RET_H)
                    sq = mixed[:, 3, 0:TT * 320].rearrange("p (t h d) -> p t h d", t=TT, h=RET_H)

                    def per_head(a):
                        return a.rearrange("p (t h) -> p t h", t=TT).unsqueeze(3).broadcast_to([P, TT, RET_H, HD])

                    m3 = sums[:, 0:N].rearrange("p (t h) -> p t h", t=TT)
                    step(nc.vector.tensor_reduce(m3, o, AX.X, ALU.add))
                    step(nc.vector.tensor_scalar(sums[:, 0:N], sums[:, 0:N], 1.0 / HD, None, ALU.mult))
                    step(nc.vector.tensor_tensor(o, o, per_head(sums[:, 0:N]), ALU.subtract))
                    step(nc.vector.tensor_tensor(sq, o, o, ALU.mult))
                    nc.vector.tensor_reduce(sums[:, 16:16 + N].rearrange("p (t h) -> p t h", t=TT), sq, AX.X,
                                            ALU.add).then_inc(sums_ready, 1)
                    dve.wait_ge(rstd_ready, 1)
                    step(nc.vector.tensor_tensor(o, o, per_head(rstd[:, 0:N]), ALU.mult))
                    step(nc.vector.tensor_tensor(o3, o3, gn_gain[:].unsqueeze(1).broadcast_to([P, TT, 320]), ALU.mult))
                    nc.vector.tensor_tensor(o3, o3, proj[:, 0:TT, RG0:RG0 + 320], ALU.mult)

                @block.gpsimd
                def _(pool):
                    step = InOrder(pool, pool_step)
                    pool.wait_ge(sums_ready, 1)
                    step(nc.gpsimd.tensor_scalar(rstd[:, 0:N], sums[:, 16:16 + N], 1.0 / HD, EPS, ALU.mult, ALU.add))
                    nc.gpsimd.tensor_tensor(rstd[:, 0:N], rstd[:, 0:N], minus_half[:, 0:N], ALU.pow).then_inc(rstd_ready, 1)

        def turn_mixed(turned_y, T):
            hi, lo = turned_y
            per = 4 // T
            n_groups = KC // per
            with stage("turned", "high_ready") as (turned, high_ready), nc.Block() as block:
                @block.tensor
                def _(pe):
                    for g in range(n_groups):
                        for j in range(4):
                            k, t = g * per + j // T, j % T
                            mm = nc.tensor.transpose(banks[:, g, j * P:(j + 1) * P], mixed[:, t, k * P:(k + 1) * P],
                                                     ident[:])
                        mm.then_inc(turned, 1)

                @block.scalar
                def _(act):
                    for g in range(n_groups):
                        act.wait_ge(turned, g + 1)
                        nc.scalar.copy(hi[:, g * per:(g + 1) * per, 0:T * P],
                                       banks[:, g, :].rearrange("p (k s) -> p k s", k=per)).then_inc(high_ready, 1)

                @block.vector
                def _(dve):
                    for g in range(n_groups):
                        dve.wait_ge(high_ready, g + 1)
                        k = slice(g * per, (g + 1) * per)
                        nc.vector.tensor_tensor(lo[:, k, 0:T * P], banks[:, g, :].rearrange("p (k s) -> p k s", k=per),
                                                hi[:, k, 0:T * P].bitcast(F32), ALU.subtract)

        def feed_forward(layer, sb2, hidden, norm_of):
            hi, lo = hidden
            key = ("ffn", layer)
            relu, square = sb2("relu", [P, 4, SEQ]), sb2("square", [P, 4, SEQ])
            u_hi, u_lo = (sb2(n, [P, 2, 4, SEQ], F32R) for n in ("u_hi", "u_lo"))

            def hidden_banks(g):
                return banks[:, 2 * (g % 2):2 * (g % 2) + 2, :].rearrange("p b (f s) -> p (b f) s", f=2)

            with stage("relu_ready", "square_ready", "high_ready", "u_ready", *NORM_SIGNALS) as (
                    relu_ready, square_ready, high_ready, u_ready, *signals), nc.Block() as block:
                norm = norm_programs(signals, hidden, *norm_of)

                @block.sync
                def _(sp):
                    load_behind(sp, key, 2 * FFN_GROUPS)

                @block.gpsimd
                def _(pool):
                    norm["gpsimd"](pool)

                @block.tensor
                def _(pe):
                    def up(i, g):
                        if g >= 2:
                            pe.wait_ge(relu_ready, g - 1)
                        for q in range(4):
                            if i == 0:
                                norm["before_pair"](pe, q)
                            pe.wait_ge(part_ready, first_part[key] + 4 * i + q + 1)
                            wh, wl = part(key, 4 * i + q)
                            for kk in range(2):
                                k = 2 * q + kk
                                for f in range(4):
                                    cols = slice(f * P, (f + 1) * P)
                                    mm = multiply(banks[:, 2 * (g % 2) + f // 2, (f % 2) * SEQ:(f % 2 + 1) * SEQ],
                                                  (wh[:, kk, cols], wl[:, kk, cols]), (hi[:, k, :], lo[:, k, :]),
                                                  k == 0 and f % 2 == 0, k == KC - 1, shares_bank=True)
                            mm.then_inc(part_used, 1)

                    def down(i, g):
                        pe.wait_ge(u_ready, g + 1)
                        for q in range(4):
                            pe.wait_ge(part_ready, first_part[key] + 4 * i + q + 1)
                            wh, wl = [w.rearrange("p k n -> p (k n)") for w in part(key, 4 * i + q)]
                            for t in range(TT):
                                tok = slice(t * P, (t + 1) * P)
                                for n in range(2):
                                    cols = slice(n * BANK, (n + 1) * BANK)
                                    mm = multiply(banks[:, 4 + 2 * t + n, :],
                                                  (u_hi[:, g % 2, q, tok], u_lo[:, g % 2, q, tok]),
                                                  (wh[:, cols], wl[:, cols]), g == 0 and q == 0,
                                                  g == FFN_GROUPS - 1 and q == 3)
                            mm.then_inc(part_used, 1)

                    norm["tensor"](pe)
                    for i, (name, g) in enumerate(FFN_ORDER):
                        (up if name == "w_up" else down)(i, g)

                @block.scalar
                def _(act):
                    norm["scalar"](act)

                    def activate(i, g):
                        products_done(act, key, i)
                        if g >= 1:
                            act.wait_ge(square_ready, g)
                        nc.scalar.activation(relu[:], hidden_banks(g), ACT.Relu).then_inc(relu_ready, 1)
                        act.wait_ge(square_ready, g + 1)
                        nc.scalar.copy(u_hi[:, g % 2, :, :], square[:]).then_inc(high_ready, 1)

                    for i in range(2 * FFN_GROUPS):
                        for q in range(PARTS):
                            split_own(split_hi, act, key, 4 * i + q)
                        if i >= 1 and FFN_ORDER[i - 1][0] == "w_up":
                            activate(i - 1, FFN_ORDER[i - 1][1])
                        split_own(split_hi, act, key, 4 * i + PARTS)
                    split_ahead(split_hi, act, key)

                @block.vector
                def _(dve):
                    norm["vector"](dve)

                    def activate(g):
                        dve.wait_ge(relu_ready, g + 1)
                        nc.vector.tensor_tensor(square[:], relu[:], relu[:], ALU.mult).then_inc(square_ready, 1)
                        dve.wait_ge(high_ready, g + 1)
                        nc.vector.tensor_tensor(u_lo[:, g % 2, :, :], square[:], u_hi[:, g % 2, :, :].bitcast(F32),
                                                ALU.subtract).then_inc(u_ready, 1)

                    for i in range(2 * FFN_GROUPS):
                        for q in range(PARTS):
                            split_own(split_lo, dve, key, 4 * i + q)
                        if i >= 1 and FFN_ORDER[i - 1][0] == "w_up":
                            activate(FFN_ORDER[i - 1][1])
                        split_own(split_lo, dve, key, 4 * i + PARTS)
                    split_ahead(split_lo, dve, key)
                    products_done(dve, key, 2 * FFN_GROUPS - 1)
                    for t in range(TT):
                        for n in range(2):
                            here = x[:, t, n * BANK:(n + 1) * BANK]
                            nc.vector.tensor_tensor(here, banks[:, 4 + 2 * t + n, :], here, ALU.add)

        def final_norm(gain_dram, store):
            with stage("gain_here", "squares_summed", "pool_step", "rstd_ready", "normed", "turned",
                       "ada_ready") as (
                    gain_here, squares_summed, pool_step, rstd_ready, normed, turned, ada_ready), nc.Block() as block:
                gain = mixed[:, 2, :]

                @block.tensor
                def _(pe):
                    if not store:
                        turn_conditions(pe, turned)

                @block.sync
                def _(sp):
                    sp.dma_start(gain, gain_dram.broadcast_to([P, D])).then_inc(gain_here, 16)
                    if store:
                        for t in range(TT):
                            sp.wait_ge(normed, t + 1)
                            sp.dma_start(out[0, t * P:(t + 1) * P, :], x[:, t, :]).then_inc(stored, 16)
                        sp.wait_ge(stored, 16 * TT)

                @block.scalar
                def _(act):
                    nc.scalar.activation(mixed[:, 1, :], x[:, 1, :], ACT.Square,
                                         accum_out=sums[:, 1:2]).then_inc(squares_summed, 1)

                @block.vector
                def _(dve):
                    nc.vector.tensor_tensor_reduce(mixed[:, 0, :], x[:, 0, :], x[:, 0, :], 1.0, 0.0, ALU.mult,
                                                   ALU.add, sums[:, 0:1]).then_inc(squares_summed, 1)
                    dve.wait_ge(rstd_ready, 1)
                    dve.wait_ge(gain_here, 16)
                    for t in range(TT):
                        nc.vector.scalar_tensor_tensor(out=x[:, t, :], in0=x[:, t, :], scalar=rstd[:, t:t + 1],
                                                       in1=gain, op0=ALU.mult, op1=ALU.mult).then_inc(normed, 1)
                    if not store:
                        add_biases(dve, turned, ada_ready)

                @block.gpsimd
                def _(pool):
                    step = InOrder(pool, pool_step)
                    pool.wait_ge(squares_summed, TT)
                    step(nc.gpsimd.tensor_scalar(rstd[:, 0:TT], sums[:, 0:TT], 1.0 / D, EPS, ALU.mult, ALU.add))
                    nc.gpsimd.tensor_tensor(rstd[:, 0:TT], rstd[:, 0:TT], minus_half[:, 0:TT],
                                            ALU.pow).then_inc(rstd_ready, 1)

        def second_block():
            with ExitStack() as local:
                def sb(name, shape, dt=F32):
                    return local.enter_context(nc.sbuf_tensor(name, shape, dt))

                nmax2, total2, inverse2 = (sb(n, [P, 6, 2]) for n in ("nmax2", "total2", "inverse2"))
                sums2 = (nmax2, total2, inverse2)
                conv_b = feats2[:, 32:36]
                sc = [[scales[:, kind, v, :] for v in range(2)] for kind in range(2)]
                sh = [[ada[:, kind, 0:8, v] for v in range(2)] for kind in range(2)]

                with scope("ab") as sb2:
                    proj = sb2("proj", [P, 4, AB_N])
                    conv_w = sb2("conv_w", [P, 4, CONV_W])
                    uT = sb2("uT", [P, 4, 2, SEQ + 2 * CONV_PAD])
                    head_gains = sb2("head_gains", [P, 2 * HD])
                    axial = sb2("axial", [P, 2, TT, HD // 2])
                    with scope("ab") as sb3:
                        hidden = [sb3(n, [P, KC, 2 * SEQ], F32R) for n in ("h_hi", "h_lo")]
                        project_and_convolve("ab_in", hidden, proj, uT, conv_w, conv_b, head_gains, axial,
                                             ((0, 1, 2, 3), sc[0], sh[0]))
                    with scope("ab_heads") as sb3:
                        prepare_axial_heads(proj, head_gains, axial, sb3("four", [P, 4 * 640]))
                    hT = sb2("heads_T", [P, 4, 2 * SEQ])
                    k_padded = sb2("k_padded", [P, B_KV, 2 * SEQ])
                    groups = [([proj[:, t, AB_Q0 + i * P:AB_Q0 + (i + 1) * P] for t in range(4)],
                               [lambda engine, bank, i=i: copy_out(engine, hT[:, i, :], bank)]) for i in range(4)]
                    groups.append(([proj[:, t, AB_K0:AB_K0 + P] for t in range(4)],
                                   [lambda engine, bank, kv=kv: copy_out(engine, k_padded[kv * HD:(kv + 1) * HD, kv, :],
                                                                         bank[kv * HD:(kv + 1) * HD, :])
                                    for kv in range(B_KV)]))
                    transpose_groups(groups, k_padded)
                    units = []
                    for h in range(B_HEADS):
                        kv, i = h // 4, h % 4
                        vs = [proj[:, t, AB_V0 + kv * HD:AB_V0 + (kv + 1) * HD] for t in range(4)]
                        for t in range(TT):
                            units.append({"rows": [(hT[:, i, t * P:(t + 1) * P], k_padded[:, kv, :], 0, BANK, vs)],
                                          "width": BANK, "mask": None, "weigh": plain_weigh(BANK + h * HD, (t,))})
                        units.append({"rows": [(hT[:, i, t * P:(t + 1) * P], k_padded[:, kv, SEQ:2 * SEQ],
                                                (t - 2) * SEQ, SEQ, vs[2:4]) for t in (2, 3)],
                                      "width": BANK, "mask": None, "weigh": plain_weigh(BANK + h * HD, (2, 3))})
                    ln_rows = sb2("ln_rows", [P, 2 * BANK])
                    with scope("ab_attend") as sb3:
                        attend(units, (sb3("probs", [P, 3, BANK]), sb3("probsT", [P, 2, BANK])) + sums2,
                               lambda done: convolution_taps(uT, conv_w, conv_b, TAPS_WITH_SLABS, None, done, None),
                               lambda step: pool_taps(step, uT, conv_w, conv_b, POOL_TAPS_WITH_SLABS, CONV_W))
                    with scope("ab_finish") as sb3:
                        finish_conv_and_gate(proj, ln_rows, sb3("tanh_y", [P, 4, BANK]), sb3("tanh_z", [P, 4, D]))
                with scope("ab_out") as sb2:
                    turned_y = [sb2(n, [P, KC, 2 * SEQ], F32R) for n in ("y_hi", "y_lo")]
                    turn_mixed(turned_y, 4)
                    out_project("ab_out", turned_y, (0, 1, 2, 3), [gate_rows[:, v, :] for v in range(2)])

                both, own = (0, 1, 2, 3), (0, 1)
                with scope("cd") as sb2:
                    proj = sb2("proj", [P, 4, CD_N])
                    with scope("cd") as sb3:
                        hidden = [sb3(n, [P, KC, 2 * SEQ], F32R) for n in ("h_hi", "h_lo")]
                        project("cd_in", hidden, [BANK] * 6, [own, own, both, both, own, own], proj,
                                (both, sc[1], sh[1]))
                    kT = sb2("kT", [P, 4, 2 * SEQ])
                    q_padded = sb2("q_padded", [P, D_HEADS // 2, 2, SEQ])
                    wf = sb2("wf", [P, C_GROUPS, P])
                    dft_c = sb2("dft_c", [P, 2 * P])
                    dft_t = sb2("dft_t", [P, 2, TT, SEQ])
                    def bias_of(t, h, n=1):
                        i = t * D_HEADS + h
                        c0 = (CD_F0, CD_Z0)[i // 8] + (i % 4) * SEQ
                        return proj[:, 2 + i // 4 % 2, c0:c0 + n * SEQ]

                    with scope("cd_fourier") as sb3:
                        fgT = sb3("fgT", [P, C_GROUPS, SEQ])
                        groups = []
                        for i in (0, 2):
                            groups.append(([proj[:, t, CD_Q0 + k * P:CD_Q0 + (k + 1) * P] for k in (i, i + 1) for t in own],
                                           [lambda engine, bank, i=i, g=g: copy_out(
                                               engine, q_padded[g * HD:(g + 1) * HD, i:i + 2, g, :],
                                               bank[g * HD:(g + 1) * HD, :].rearrange("p (k s) -> p k s", k=2),
                                               HD ** -0.5) for g in range(2)]))
                            groups.append(([proj[:, t, CD_F0 + k * P:CD_F0 + (k + 1) * P] for k in (i, i + 1) for t in own],
                                           [lambda engine, bank, i=i: copy_out(
                                               engine, fgT[:, i:i + 2, :],
                                               bank.rearrange("p (k s) -> p k s", k=2))]))
                        for i in range(4):
                            groups.append(([proj[:, t, CD_K0 + i * P:CD_K0 + (i + 1) * P] for t in both],
                                           [lambda engine, bank, i=i: copy_out(engine, kT[:, i, :], bank)]))
                        transpose_groups(groups, q_padded)
                        fourier_and_bias(fgT, wf, dft_c, dft_t, sb3, bias_of)

                    units = []
                    for h in range(D_HEADS):
                        vs = [proj[:, t, CD_V0 + h * HD:CD_V0 + (h + 1) * HD] for t in both]
                        for t in own:
                            units.append({"rows": [(q_padded[:, h // 2, h % 2, t * P:(t + 1) * P], kT[:, h // 2, :],
                                                    0, BANK, vs)],
                                          "width": BANK, "scale": 1.0, "mask": bias_of(t, h),
                                          "weigh": plain_weigh(BANK + h * HD, (t,))})
                    with scope("cd_attend") as sb3:
                        attend(units, (sb3("probs", [P, 3, BANK]), sb3("probsT", [P, 2, BANK])) + sums2)
                    gate_by_z(proj, 2, CD_Z0)
                with scope("cd_out") as sb2:
                    turned_y = [sb2(n, [P, KC, SEQ], F32R) for n in ("y_hi", "y_lo")]
                    turn_mixed(turned_y, 2)
                    out_project("cd_out", turned_y, own, [gate_rows[:, 0, :]])

        def turn_conditions(pe, turned):
            for kind in range(2):
                rows = slice(HD * kind, HD * kind + 2)
                for f in range(24):
                    mm = nc.tensor.transpose(banks[:, kind, 2 * f:2 * f + 2], ada_rows[rows, f * P:(f + 1) * P],
                                             ident[rows, rows])
                mm.then_inc(turned, 1)

        def add_biases(dve, turned, ada_ready):
            for kind, (b0, g0) in enumerate(((0, 24), (36, 60))):
                dve.wait_ge(turned, kind + 1)
                nc.vector.tensor_tensor(ada[:, kind, :, :], banks[:, kind, 0:48].rearrange("p (f v) -> p f v", v=2),
                                        feats2[:, b0:b0 + 24].unsqueeze(2).broadcast_to([P, 24, 2]),
                                        ALU.add).then_inc(ada_ready, 1)
                dve.wait_ge(ada_ready, kind + 1)
                for v in range(2):
                    nc.vector.scalar_tensor_tensor(out=scales[:, kind, v, :], in0=ada[:, kind, 8:16, v],
                                                   scalar=1.0, in1=feats2[:, g0:g0 + KC], op0=ALU.add, op1=ALU.mult)

        def spread_gates(pe, kind, n_gates, rows_ready):
            for v in range(n_gates):
                for c in range(KC):
                    mm = nc.tensor.matmul(banks[:, 2 * v + c // 4, (c % 4) * P:(c % 4 + 1) * P],
                                          ada[:, kind, 16 + c, v:v + 1].broadcast_to([P, P]), ident[:],
                                          start=True, stop=True)
                mm.then_inc(rows_ready, 1)

        def copy_gates(act, n_gates, rows_ready):
            for v in range(n_gates):
                act.wait_ge(rows_ready, v + 1)
                nc.scalar.copy(gate_rows[:, v, :].rearrange("p (b n) -> p b n", b=2), banks[:, 2 * v:2 * v + 2, :])

        def convolution_taps(uT, conv_w, conv_b, first_tap, last_tap, done, uT_ready):
            dve = nc.vector
            order = [(j, c) for j in range(CONV_W) for c in range(3)]
            for n, (j, c) in list(enumerate(order))[first_tap:last_tap]:
                if j == 0:
                    dve.wait_ge(uT_ready, c + 1)
                elif n - 3 >= first_tap:
                    dve.wait_ge(done, n - 3 - first_tap + 1)
                tap = uT[:, c, :, j:j + SEQ]
                if j == 0:
                    ins = dve.tensor_scalar(convolved(c), tap, conv_w[:, c, 0:1], conv_b[:, c:c + 1], ALU.mult, ALU.add)
                else:
                    ins = dve.scalar_tensor_tensor(out=convolved(c), in0=tap, scalar=conv_w[:, c, j:j + 1],
                                                   in1=convolved(c), op0=ALU.mult, op1=ALU.add)
                ins.then_inc(done, 1)
                yield

        def convolved(c):
            return mixed[:, c, 0:BANK].rearrange("p (s n) -> p s n", s=2)

        def pool_taps(step, uT, conv_w, conv_b, j0, j1):
            product = ada_rows[:, 2 * D:2 * D + BANK].rearrange("p (s n) -> p s n", s=2)
            for j in range(j0, j1):
                tap, w = uT[:, 3, :, j:j + SEQ], conv_w[:, 3, j:j + 1]
                if j == 0:
                    step(nc.gpsimd.tensor_scalar(convolved(3), tap, w, conv_b[:, 3:4], ALU.mult, ALU.add))
                else:
                    step(nc.gpsimd.tensor_scalar(product, tap, w, None, ALU.mult))
                    step(nc.gpsimd.tensor_tensor(convolved(3), convolved(3), product, ALU.add))

        def project_and_convolve(key, hidden, proj, uT, conv_w, conv_b, head_gains, axial,
                                 norm_of):
            n_slabs = -(-AB_N // BANK)
            widths = [min(BANK, AB_N - s * BANK) for s in range(n_slabs)]
            tiles = range(4)
            TURN_AT = 3
            H = B_HEADS + B_KV
            HEADS_A_PART = 8
            with stage("evacuated", "tanh_ready", "glu_ready", "glu_turned", "uT_ready", "zeroed", "tap_done",
                       "weights_here", "tables_here", "sums_ready", "pool_step",
                       *NORM_SIGNALS) as (
                    evacuated, tanh_ready, glu_ready, glu_turned, uT_ready, zeroed, tap_done,
                    weights_here, tables_here, sums_ready, pool_step, *signals), \
                    nc.sbuf_tensor("ab_whole", [P, 2, 2 * SEQ], F32) as spare, nc.Block() as block:
                norm = norm_programs(signals, hidden, *norm_of, spare=spare)
                squares = spare[:, 0, 0:HD]

                @block.sync
                def _(sp):
                    sp.dma_start(conv_w[:], dram["conv_w"]).then_inc(weights_here, 16)
                    sp.dma_start(head_gains[:], dram["rows"][:, 2 * BANK:2 * BANK + 2 * HD].broadcast_to([P, 2 * HD])
                                 ).then_inc(tables_here, 16)
                    sp.dma_start(axial[:], dram["axial"]).then_inc(tables_here, 16)
                    load_behind(sp, key, n_slabs)
                    sp.wait_ge(tables_here, 32)

                @block.gpsimd
                def _(pool):
                    norm["gpsimd"](pool)
                    nc.gpsimd.memset(uT[:], 0.0).then_inc(zeroed, 1)
                    pool.wait_ge(weights_here, 16)
                    pool.wait_ge(uT_ready, 4)
                    step = InOrder(pool, pool_step)
                    pool_taps(step, uT, conv_w, conv_b, 0, POOL_TAPS_WITH_SLABS)
                    pool.wait_ge(sums_ready, 4 * H)
                    step(nc.gpsimd.tensor_scalar(rstd[:, 0:4 * H], sums[:, 0:4 * H], 1.0 / HD, EPS, ALU.mult, ALU.add))
                    step(nc.gpsimd.tensor_tensor(rstd[:, 0:4 * H], rstd[:, 0:4 * H], minus_half[:, 0:4 * H], ALU.pow))
                    q = rstd[:, 0:4 * H].rearrange("p (t h) -> p t h", t=4)[:, :, 0:B_HEADS]
                    nc.gpsimd.tensor_scalar(q, q, HD ** -0.5, None, ALU.mult)

                @block.tensor
                def _(pe):
                    norm["tensor"](pe)
                    for s in range(n_slabs):
                        if s >= 2:
                            pe.wait_ge(evacuated, 4 * (s - 1))
                        if s == TURN_AT:
                            pe.wait_ge(glu_ready, 4)
                            for c in range(4):
                                for t in tiles:
                                    mm = nc.tensor.transpose(banks[:, 4 * (s % 2) + c, t * P:(t + 1) * P],
                                                             mixed[:, t, BANK + c * P:BANK + (c + 1) * P], ident[:])
                                mm.then_inc(glu_turned, 1)
                            pe.wait_ge(uT_ready, 4)
                        multiply_slab(pe, key, s, hidden, widths[s], tiles, norm)

                @block.scalar
                def _(act):
                    norm["scalar"](act)

                    def copy_products(s):
                        products_done(act, key, s)
                        for t in tiles:
                            nc.scalar.copy(proj[:, t, s * BANK:s * BANK + widths[s]],
                                           banks[:, 4 * (s % 2) + t, 0:widths[s]]).then_inc(evacuated, 1)
                            if s == 1:
                                act.wait_ge(evacuated, 4 + t + 1)
                                nc.scalar.activation(mixed[:, t, 0:BANK], proj[:, t, AB_GATE0:AB_GATE0 + BANK],
                                                     ACT.Tanh, scale=0.5).then_inc(tanh_ready, 1)

                    for q in range(4 * n_slabs):
                        split_own(split_hi, act, key, q)
                        if q >= 5 and q % 4 == 1:
                            copy_products(q // 4 - 1)
                        if q == 4 * TURN_AT + 2:
                            act.wait_ge(zeroed, 1)
                            for c in range(4):
                                act.wait_ge(glu_turned, c + 1)
                                nc.scalar.activation(uT[:, c, :, CONV_PAD:CONV_PAD + SEQ],
                                                     banks[:, 4 * (TURN_AT % 2) + c, :].rearrange(
                                                         "p (s n) -> p s n", s=2),
                                                     ACT.Copy, scale=0.5).then_inc(uT_ready, 1)
                        n0 = (q - 4 * TURN_AT - 6) * HEADS_A_PART
                        for n in range(max(n0, 0), min(n0 + HEADS_A_PART, 4 * H)):
                            c0 = AB_Q0 + n % H * HD
                            nc.scalar.activation(squares, proj[:, n // H, c0:c0 + HD], ACT.Square,
                                                 accum_out=sums[:, n:n + 1]).then_inc(sums_ready, 1)
                            act.wait_ge(sums_ready, n + 1)
                    split_ahead(split_hi, act, key)
                    copy_products(n_slabs - 1)

                @block.vector
                def _(dve):
                    norm["vector"](dve)
                    more = convolution_taps(uT, conv_w, conv_b, 0, TAPS_WITH_SLABS, tap_done, uT_ready)
                    for q in range(4 * n_slabs):
                        split_own(split_lo, dve, key, q)
                        if q == 10:
                            for t in tiles:
                                dve.wait_ge(tanh_ready, t + 1)
                                nc.vector.scalar_tensor_tensor(
                                    out=mixed[:, t, BANK:D], in0=mixed[:, t, 0:BANK], scalar=1.0,
                                    in1=proj[:, t, 0:BANK], op0=ALU.add, op1=ALU.mult).then_inc(glu_ready, 1)
                        if q == 4 * TURN_AT + 2:
                            dve.wait_ge(weights_here, 16)
                        if q >= 4 * TURN_AT + 2:
                            advance(more, 7 if q < 4 * (n_slabs - 1) else 3)
                    split_ahead(split_lo, dve, key)
                    advance(more)

        def prepare_axial_heads(proj, gains, axial, flat):
            H = B_HEADS + B_KV
            qk = proj[:, :, AB_Q0:AB_Q0 + H * HD].rearrange("p t (h d) -> p t h d", h=H)
            temps = [flat[:, i * 640:(i + 1) * 640] for i in range(4)]
            with stage("dve_step", "pool_step", "rows_ready") as (dve_step, pool_step, rows_ready), \
                    nc.Block() as block:
                @block.tensor
                def _(pe):
                    spread_gates(pe, 0, 2, rows_ready)

                def scale_heads(engine, step, tiles):
                    here = qk[:, tiles, :, :]
                    T = tiles.stop - tiles.start
                    per_head = rstd[:, tiles.start * H:tiles.stop * H].rearrange("p (t h) -> p t h", t=T).unsqueeze(
                        3).broadcast_to([P, T, H, HD])
                    step(engine.tensor_tensor(here, here, per_head, ALU.mult))
                    for h0, h1, gain in ((0, B_HEADS, gains[:, 0:HD]), (B_HEADS, H, gains[:, HD:2 * HD])):
                        last = engine.tensor_tensor(
                            here[:, :, h0:h1, :], here[:, :, h0:h1, :],
                            gain.unsqueeze(1).unsqueeze(1).broadcast_to([P, T, h1 - h0, HD]), ALU.mult)
                    step(last)

                @block.scalar
                def _(act):
                    copy_gates(act, 2, rows_ready)

                @block.vector
                def _(dve):
                    step = InOrder(dve, dve_step)
                    scale_heads(nc.vector, step, slice(0, 2))
                    rope(dve, step, qk[:, 0:TT, :, :], axial[:, 0, :, :], axial[:, 1, :, :], HD // 2, temps)

                @block.gpsimd
                def _(pool):
                    scale_heads(nc.gpsimd, InOrder(pool, pool_step), slice(2, 4))

        def finish_conv_and_gate(proj, ln_rows, tanh_y, tanh_z):
            y = mixed[:, :, 0:BANK]
            stats, mv = sums[:, 48:72], sums[:, 72:80]
            with stage("rows_here", "turned_back", "stats_ready", "pool_step", "rstd_ready", "tanh_z_ready",
                       "normed", "tanh_y_ready", "dve_step") as (
                    rows_here, turned_back, stats_ready, pool_step, rstd_ready, tanh_z_ready, normed, tanh_y_ready,
                    dve_step), nc.Block() as block:
                @block.sync
                def _(sp):
                    sp.dma_start(ln_rows[:], dram["rows"][:, 0:2 * BANK].broadcast_to([P, 2 * BANK])
                                 ).then_inc(rows_here, 16)

                @block.tensor
                def _(pe):
                    for t in range(4):
                        for c in range(4):
                            mm = nc.tensor.transpose(banks[:, t, c * P:(c + 1) * P],
                                                     mixed[:, c, t * P:(t + 1) * P], ident[:])
                        mm.then_inc(turned_back, 1)

                @block.scalar
                def _(act):
                    for t in range(4):
                        nc.scalar.activation(tanh_z[:, t, :], proj[:, t, AB_Z0:AB_Z0 + D], ACT.Tanh,
                                             scale=0.5).then_inc(tanh_z_ready, 1)
                    for t in range(4):
                        act.wait_ge(normed, t + 1)
                        nc.scalar.activation(tanh_y[:, t, :], y[:, t, :], ACT.Tanh, scale=0.5).then_inc(tanh_y_ready, 1)

                @block.gpsimd
                def _(pool):
                    step = InOrder(pool, pool_step)
                    pool.wait_ge(stats_ready, 1)
                    step(nc.gpsimd.tensor_scalar(rstd[:, 48:52], mv.rearrange("p (t v) -> p t v", v=2)[:, :, 1],
                                                 EPS, None, ALU.add))
                    nc.gpsimd.tensor_tensor(rstd[:, 48:52], rstd[:, 48:52], minus_half[:, 0:4],
                                            ALU.pow).then_inc(rstd_ready, 1)

                @block.vector
                def _(dve):
                    step = InOrder(dve, dve_step)
                    for t in range(4):
                        dve.wait_ge(turned_back, t + 1)
                        last = nc.vector.bn_stats(stats[:, 6 * t:6 * t + 6], banks[:, t, :])
                    step(last)
                    for t in range(4):
                        last = nc.vector.bn_aggr(mv[:, 2 * t:2 * t + 2], stats[:, 6 * t:6 * t + 6])
                    last.then_inc(stats_ready, 1)
                    dve.wait_ge(stats_ready, 1)
                    dve.wait_ge(rows_here, 16)
                    for t in range(4):
                        last = nc.vector.scalar_tensor_tensor(out=y[:, t, :], in0=banks[:, t, :],
                                                              scalar=mv[:, 2 * t:2 * t + 1], in1=ln_rows[:, 0:BANK],
                                                              op0=ALU.subtract, op1=ALU.mult)
                    step(last)
                    dve.wait_ge(rstd_ready, 1)
                    for t in range(4):
                        nc.vector.scalar_tensor_tensor(out=y[:, t, :], in0=y[:, t, :], scalar=rstd[:, 48 + t:49 + t],
                                                       in1=ln_rows[:, BANK:2 * BANK], op0=ALU.mult,
                                                       op1=ALU.add).then_inc(normed, 1)
                    for t in range(4):
                        z = proj[:, t, AB_Z0:AB_Z0 + D]
                        dve.wait_ge(tanh_z_ready, t + 1)
                        last = nc.vector.scalar_tensor_tensor(out=z, in0=tanh_z[:, t, :], scalar=1.0, in1=z,
                                                              op0=ALU.add, op1=ALU.mult)
                    step(last)
                    for t in range(4):
                        dve.wait_ge(tanh_y_ready, t + 1)
                        last = nc.vector.scalar_tensor_tensor(out=y[:, t, :], in0=tanh_y[:, t, :], scalar=1.0,
                                                              in1=y[:, t, :], op0=ALU.add, op1=ALU.mult)
                    step(last)
                    for half, scale in ((0, 0.25), (1, 0.5)):
                        here = mixed[:, :, half * BANK:(half + 1) * BANK]
                        z = proj[:, :, AB_Z0 + half * BANK:AB_Z0 + (half + 1) * BANK]
                        nc.vector.scalar_tensor_tensor(out=here, in0=z, scalar=scale, in1=here, op0=ALU.mult,
                                                       op1=ALU.mult)

        def gate_by_z(proj, T, z0):
            with stage("tanh_ready", "dve_step", "rows_ready") as (tanh_ready, dve_step, rows_ready), \
                    nc.sbuf_tensor(f"tanh_z_{z0}", [P, T, D], F32) as tanh_z, nc.Block() as block:
                @block.scalar
                def _(act):
                    for t in range(T):
                        nc.scalar.activation(tanh_z[:, t, :], proj[:, t, z0:z0 + D], ACT.Tanh,
                                             scale=0.5).then_inc(tanh_ready, 1)
                    copy_gates(act, 1, rows_ready)

                @block.tensor
                def _(pe):
                    spread_gates(pe, 1, 1, rows_ready)

                @block.vector
                def _(dve):
                    step = InOrder(dve, dve_step)
                    for t in range(T):
                        z = proj[:, t, z0:z0 + D]
                        dve.wait_ge(tanh_ready, t + 1)
                        step(nc.vector.scalar_tensor_tensor(out=z, in0=tanh_z[:, t, :], scalar=1.0, in1=z,
                                                            op0=ALU.add, op1=ALU.mult))
                        nc.vector.scalar_tensor_tensor(out=mixed[:, t, :], in0=z, scalar=0.5, in1=mixed[:, t, :],
                                                       op0=ALU.mult, op1=ALU.mult)

        def fourier_and_bias(fgT, wf, dft_c, dft_t, sb3, bias_of):
            channels = sb3("channels", [P, C_GROUPS, TT, 2 * P])
            frT = sb3("frT", [P, C_GROUPS, SEQ])
            with stage("tables_here", "channels_ready", "channels_copied", "tokens_ready", "tokens_copied",
                       "product_ready", "spread", "window_added") as (
                    tables_here, channels_ready, channels_copied, tokens_ready, tokens_copied,
                    product_ready, spread, window_added), nc.Block() as block:
                @block.sync
                def _(sp):
                    for dst, name in ((wf, "w_fourier"), (dft_c, "dft_c"), (dft_t, "dft_t")):
                        sp.dma_start(dst[:], dram[name]).then_inc(tables_here, 16)

                @block.tensor
                def _(pe):
                    spread_bias(pe, 0, 4).then_inc(spread, 1)
                    pe.wait_ge(tables_here, 48)
                    for g in range(C_GROUPS):
                        for t in range(TT):
                            mm = nc.tensor.matmul(banks[:, g, t * SEQ:(t + 1) * SEQ], fgT[:, g, t * P:(t + 1) * P],
                                                  dft_c[:], start=True, stop=True)
                        mm.then_inc(channels_ready, 1)
                    pe.wait_ge(window_added, 1)
                    for g in range(C_GROUPS):
                        pe.wait_ge(channels_copied, g + 1)
                        a = channels[:, g, :, :]
                        accumulate(banks[:, 4 + g // 2, (g % 2) * SEQ:(g % 2 + 1) * SEQ],
                                   [(a[:, t, v * P:(v + 1) * P], dft_t[:, v, t, :]) for t in range(TT)
                                    for v in range(2)]).then_inc(tokens_ready, 1)
                    for g in range(C_GROUPS):
                        pe.wait_ge(tokens_copied, g // 2 + 1)
                        for t in range(TT):
                            mm = nc.tensor.matmul(banks[:, 6 + t, g * P:(g + 1) * P], frT[:, g, t * P:(t + 1) * P],
                                                  wf[:, g, :], start=True, stop=True)
                    mm.then_inc(product_ready, 1)
                    spread_bias(pe, 1, 0).then_inc(spread, 1)

                @block.vector
                def _(dve):
                    dve.wait_ge(spread, 1)
                    add_window(dve, bias_of, 0, 4).then_inc(window_added, 1)
                    for g in range(C_GROUPS):
                        dve.wait_ge(channels_ready, g + 1)
                        nc.vector.tensor_copy(channels[:, g, :, :], banks[:, g, :].rearrange(
                            "p (t n) -> p t n", t=TT)).then_inc(channels_copied, 1)
                    dve.wait_ge(product_ready, 1)
                    for t in range(TT):
                        nc.vector.tensor_copy(mixed[:, t, 0:BANK], banks[:, 6 + t, :])
                    dve.wait_ge(spread, 2)
                    add_window(dve, bias_of, 1, 0)

                @block.scalar
                def _(act):
                    for b in range(C_GROUPS // 2):
                        act.wait_ge(tokens_ready, 2 * b + 2)
                        nc.scalar.copy(frT[:, 2 * b:2 * b + 2, :],
                                       banks[:, 4 + b, :].rearrange("p (g s) -> p g s", g=2)).then_inc(tokens_copied, 1)

        def spread_bias(pe, half, bank0):
            for ck in range(half * GRID_W // 2, (half + 1) * GRID_W // 2):
                shift = GRID_W - 1 - ck
                for parity in range(2):
                    mm = nc.tensor.matmul(
                        banks[parity * HD:(parity + 1) * HD, bank0 + ck // 8 % 4, (ck % 8) * 56:(ck % 8 + 1) * 56],
                        onehot[:, shift:shift + GRID_W], rpb[:, parity, :], start=True, stop=True)
            return mm

        def add_window(dve, bias_of, half, bank0):
            table = banks[:, bank0:bank0 + 4, 0:8 * 56].rearrange("p b (j h r) -> p r h b j", j=8, h=D_HEADS)
            b = slice(4 * half, 4 * half + 4)
            mask = col_mask[:].rearrange("p (b j) -> p b j", j=8)[:, b, :].unsqueeze(1).broadcast_to([P, 4, 4, 8])
            for t in range(TT):
                for h0 in (0, 4):
                    four = bias_of(t, h0, 4).rearrange("p (h r b j) -> p h r b j", h=4, r=ROWS, b=8)
                    for rk in range(ROWS):
                        last = nc.vector.tensor_tensor(four[:, :, rk, b, :], table[:, rk - 2 * t + 3, h0:h0 + 4, :, :],
                                                       mask, ALU.add)
            return last

        first_block()
        final_norm(dram["final_gain"], False)
        second_block()
        final_norm(dram["final_norm_g"], True)


def _slabs(w):
    w = np.asarray(w)
    short = -w.shape[-1] % BANK
    w = np.concatenate([w, np.zeros(w.shape[:-1] + (short,), w.dtype)], axis=-1)
    lead = w.shape[:-2]
    w = w.reshape(-1, KC, P, w.shape[-1] // BANK, BANK).transpose(0, 3, 2, 1, 4)
    return np.ascontiguousarray(w.reshape(-1, P, KC * BANK))


def _features(v):
    v = np.asarray(v)
    v = v.reshape(v.shape[:-1] + (-1, P))
    return np.moveaxis(v, -1, 0)


def _w_in_order():
    starts = dict(q=0, kc=384, vc=512, ks=640, vs=768, kw=896, vw=1024)
    cols = [c for pair in NSA_PAIRS for h in pair for c in range(h * HD, (h + 1) * HD)]
    for name in ("kc", "ks", "kw", "vc", "vs", "vw"):
        cols += list(range(starts[name], starts[name] + NSA_G * HD))
    return np.array(cols + list(range(GATE0, N_IN)))


def _ukv_order():
    per = MLA_NOPE + HD
    return np.array([h * per + part * MLA_NOPE + d for part in range(2) for h in range(MLA_H) for d in range(HD)])


def _tables():
    i = np.arange(P)
    q = np.arange(SEQ)
    t = {}
    t["ident"] = np.eye(P)
    inv = [1.0 / theta ** (np.arange(0, dim, 2, dtype=np.float32) / np.float32(dim))
           for theta, dim in ((np.float32(500000.0), 16), (np.float32(500000.0), 32), (np.float32(10000.0), 64))]
    t["freqs"] = np.tile(np.concatenate(inv), (P, 1))
    tri = np.where(i[:, None] >= i[None, :], 0.0, NEG)
    t["causal"] = np.concatenate([tri, np.zeros((P, P)), tri], axis=1)
    gamma = 1.0 - 2.0 ** (-5.0 - np.arange(RET_H))
    gap = (q[None, :] - i[:, None]).astype(np.float64)
    fade = np.where(gap >= 0, gamma[:, None, None] ** np.maximum(gap, 0)[None], 0.0) * HD ** -0.5
    t["decay"] = np.concatenate([fade, fade[:, :, 0:P]], axis=2).transpose(1, 0, 2)
    keep = np.zeros((P, TT, 16))
    for tile in range(TT):
        keep[:, tile, 0:N_CMP] = (np.arange(N_CMP)[None, :] * 16 + 31) <= (tile * P + i)[:, None]
    t["cmp_keep"] = keep.reshape(P, TT * 16)
    t["cmp_add"] = np.where(keep > 0, 0.0, NEG).reshape(P, TT * 16)
    freq = np.float32(10000.0) ** (-np.arange(HD // 4, dtype=np.float32) / np.float32(HD // 4))
    ang = np.concatenate([(q // GRID_W)[:, None] * freq, (q % GRID_W)[:, None] * freq], axis=1)
    t["axial"] = np.stack([np.cos(ang), np.sin(ang)]).reshape(2, TT, P, HD // 2).transpose(2, 0, 1, 3)
    w = 2 * np.pi * np.outer(i, i) / P
    t["dft_c"] = np.concatenate([np.cos(w), np.sin(w)], axis=1)
    w = 2 * np.pi * (np.outer(q, q) % SEQ) / SEQ
    t["dft_t"] = (np.stack([np.cos(w), -np.sin(w)]) / np.sqrt(SEQ * P)).reshape(2, TT, P, SEQ).transpose(2, 0, 1, 3)
    t["onehot"] = (np.arange(2 * GRID_W - 1)[None, :] == (GRID_W - 1 + 15 - np.arange(N_DC))[:, None])
    col = np.arange(GRID_W)
    start = np.clip(col - 8, 0, GRID_W - 16)
    ok = (col[None, :] >= start[:, None]) & (col[None, :] < start[:, None] + 16)
    t["col_mask"] = np.tile(np.where(ok, 0.0, NEG), (2, 1))
    return {k: np.ascontiguousarray(v, dtype=np.float32) for k, v in t.items()}


def _ab_order():
    split = np.concatenate([np.arange(0, HD, 2), np.arange(1, HD, 2)])
    cols = list(range(AB_Q0))
    for i in range(B_HEADS // 2):
        for h in (i, i + B_HEADS // 2):
            cols += list(AB_Q0 + h * HD + split)
    for kv in range(B_KV):
        cols += list(AB_K0 + kv * HD + split)
    return np.array(cols + list(range(AB_V0, AB_N))), split


def _layout(a):
    cat = np.concatenate
    d = _tables()
    L = DEPTH
    tiles = lambda v: np.ascontiguousarray(np.asarray(v).reshape(-1, P, D).transpose(1, 0, 2))
    d["x"] = tiles(a["x"])
    d["ctx"] = tiles(a["ctx_2"])
    d["positions"] = np.ascontiguousarray(np.asarray(a["positions"]).reshape(TT, P).T)
    d["w_in"] = _slabs(np.asarray(a["w_in"])[:, :, _w_in_order()])
    w1 = [np.asarray(a[n]).reshape(L, CMP_LP, P, P).transpose(0, 2, 1, 3).reshape(L, P, CMP_LP * P)
          for n in ("cmp_w1_k", "cmp_w1_v")]
    d["cmp_w1"] = cat(w1, axis=2)
    d["small"] = cat([np.asarray(a["mla_w_uq"]).reshape(L, 2, P, 480).transpose(0, 2, 1, 3).reshape(L, P, 960),
                      np.asarray(a["mla_w_ukv"])[:, :, _ukv_order()], np.asarray(a["cmp_w2_k"]),
                      np.asarray(a["cmp_w2_v"])], axis=2)
    d["w_out"] = _slabs(a["w_out"])
    d["w_up"] = _slabs(a["w_up"])
    d["w_down"] = np.asarray(a["w_down"]).reshape(L, 8, 4, P, D).transpose(0, 1, 3, 2, 4).reshape(L * 8, P, SLAB)
    d["feats"] = cat([_features(a["ln1_gain"]), _features(a["ln2_gain"]), _features(a["mla_q_norm"]),
                      _features(a["mla_kv_norm"]), _features(np.asarray(a["cmp_pos_k"]).reshape(L, -1)),
                      _features(np.asarray(a["cmp_pos_v"]).reshape(L, -1))], axis=2)
    d["gn_gain"] = np.asarray(a["ret_gn_gain"]).reshape(L, RET_H * HD)
    d["final_gain"] = np.asarray(a["final_gain"]).reshape(1, D)
    d["final_norm_g"] = np.asarray(a["final_norm_g_2"]).reshape(1, D)
    order, split = _ab_order()
    d["ab_in"] = _slabs(np.asarray(a["ab_w_in_2"])[:, :, order])
    for to, of in (("ab_ada", "ab_w_ada_2"), ("ab_out", "ab_w_out_2"), ("cd_ada", "cd_w_ada_2"),
                   ("cd_in", "cd_w_in_2"), ("cd_out", "cd_w_out_2")):
        d[to] = _slabs(a[of])
    d["cond"] = np.stack([_features(np.asarray(a[n]).reshape(-1)) for n in ("c_2", "c_ctx_2")], axis=2)
    d["feats2"] = cat([_features(np.asarray(a[n]).reshape(-1)) for n in (
        "ab_b_ada_2", "ab_norm_g_2", "ab_conv_b_2", "cd_b_ada_2", "cd_norm_g_2")], axis=1)
    d["conv_w"] = np.asarray(a["ab_conv_w_2"]).reshape(CONV_W, 4, P).transpose(2, 1, 0)
    d["rows"] = cat([np.asarray(a["ab_ln_g_2"]), np.asarray(a["ab_ln_b_2"]),
                     np.asarray(a["ab_q_norm_g_2"])[:, split], np.asarray(a["ab_k_norm_g_2"])[:, split]], axis=1)
    d["w_fourier"] = np.asarray(a["cd_w_fourier_2"]).reshape(C_GROUPS, P, P).transpose(1, 0, 2)
    rpb = np.asarray(a["cd_rpb_2"])[0, :, 4:4 + N_DR, :].transpose(2, 0, 1)
    later = cat([np.zeros_like(rpb[:, :, :1]), rpb[:, :, :-1]], axis=2)
    d["rpb"] = np.stack([rpb, later], axis=1).reshape(N_DC, 2, D_HEADS * N_DR)
    return {k: np.ascontiguousarray(v) for k, v in d.items()}


def kernel(**inputs):
    import concourse.bacc as bacc
    from concourse.bass_utils import run_bass_kernel_spmd

    nc = bacc.Bacc("TRN2", target_bir_lowering=False, num_devices=1)
    arrays, dram = {}, {}
    for name, a in _layout(inputs).items():
        arrays[f"in_{name}"] = a
        dram[name] = nc.dram_tensor(f"in_{name}", a.shape, mybir.dt.from_np(a.dtype), kind="ExternalInput").ap()
    out = nc.dram_tensor("out_0", (1, SEQ, D), F32, kind="ExternalOutput").ap()
    build_program(nc, dram, out)
    r = run_bass_kernel_spmd(nc, [arrays], core_ids=[0])
    return r.results[0]["out_0"]
```
